# Optimizing a Trainium2 kernel written in Bass

```python
import math
import jax, jax.numpy as jnp
from jax import lax
import numpy as np

D_MODEL = 1024
BATCH = 1
SEQ = 128
DEPTH = 1
DEC_BATCH = 1
DEC_SEQ = 512
PAST_LEN = 128

GRID_W = 64
HEAD_DIM = 64
N_HEADS = 8
N_KV_HEADS = 2
ATTN_W = N_HEADS * HEAD_DIM
KV_W = N_KV_HEADS * HEAD_DIM
D_CONV = D_MODEL // 2
MIX_W = ATTN_W + D_CONV
IN_W = ATTN_W + 2 * KV_W + 2 * D_CONV
CONV_WIDTH = 31
CONV_PAD = CONV_WIDTH // 2
Q_BLOCK = 128
ROPE_THETA = 10000.0
ROPE_AXIS_DIM = HEAD_DIM // 2
N_EXPERTS = 16
CAPACITY_FACTOR = 2
D_FF_EXPERT = 1024
EPS = 1e-6

kernel_name = "hybrid_dit_gqa_conformer_ecmoe_step"

def rms_norm(x, g):
    x32 = x.astype(jnp.float32)
    y = x32 * lax.rsqrt(jnp.mean(x32 * x32, axis=-1, keepdims=True) + EPS)
    return (y * g.astype(jnp.float32)).astype(x.dtype)

def layer_norm(x, g, b):
    x32 = x.astype(jnp.float32)
    mu = jnp.mean(x32, axis=-1, keepdims=True)
    var = jnp.mean(jnp.square(x32 - mu), axis=-1, keepdims=True)
    y = (x32 - mu) * lax.rsqrt(var + EPS)
    return (y * g.astype(jnp.float32) + b.astype(jnp.float32)).astype(x.dtype)

def modulation(cond, w_mod, b_mod):
    m = jax.nn.silu(cond) @ w_mod + b_mod
    return jnp.split(m[:, None, :], 6, axis=-1)

def rope_axis(x, pos):
    half = ROPE_AXIS_DIM // 2
    freqs = ROPE_THETA ** (-jnp.arange(half, dtype=jnp.float32) / half)
    ang = pos.astype(jnp.float32)[:, None] * freqs[None, :]
    cos = jnp.cos(ang)[None, :, None, :]
    sin = jnp.sin(ang)[None, :, None, :]
    x32 = x.astype(jnp.float32)
    x1, x2 = x32[..., :half], x32[..., half:]
    return jnp.concatenate([x1 * cos - x2 * sin, x2 * cos + x1 * sin], axis=-1).astype(x.dtype)

def axial_rope(x):
    n = x.shape[1]
    rows = n // GRID_W
    pos_row = jnp.repeat(jnp.arange(rows, dtype=jnp.int32), GRID_W)
    pos_col = jnp.tile(jnp.arange(GRID_W, dtype=jnp.int32), rows)
    return jnp.concatenate([rope_axis(x[..., :ROPE_AXIS_DIM], pos_row),
                            rope_axis(x[..., ROPE_AXIS_DIM:], pos_col)], axis=-1)

def block_attention(q, k, v):
    b, nq, h, d = q.shape
    nkv = k.shape[2]
    g = h // nkv
    nb = nq // Q_BLOCK
    qb = q.reshape(b, nb, Q_BLOCK, nkv, g, d).transpose(1, 0, 2, 3, 4, 5)
    scale = 1.0 / math.sqrt(d)

    def one_block(qblk):
        s = jnp.einsum('bqkgd,bskd->bkgqs', qblk, k, preferred_element_type=jnp.float32) * scale
        p = jax.nn.softmax(s, axis=-1).astype(v.dtype)
        return jnp.einsum('bkgqs,bskd->bqkgd', p, v)

    out = lax.map(one_block, qb)
    return out.transpose(1, 0, 2, 3, 4, 5).reshape(b, nq, h * d)

def conformer_conv(a, gt, conv_w, conv_b, ln_g, ln_b):
    u = a * jax.nn.sigmoid(gt)
    y = lax.conv_general_dilated(u, conv_w[:, None, :], window_strides=(1,),
                                 padding=[(CONV_PAD, CONV_PAD)],
                                 dimension_numbers=('NWC', 'WIO', 'NWC'),
                                 feature_group_count=D_CONV) + conv_b
    return jax.nn.silu(layer_norm(y, ln_g, ln_b))

def mixer(h, w_in, q_norm, k_norm, conv_w, conv_b, ln_g, ln_b, w_out, latent, k_ctx, v_ctx):
    b, n, _ = h.shape
    p = h @ w_in
    q = rms_norm(p[..., :ATTN_W].reshape(b, n, N_HEADS, HEAD_DIM), q_norm)
    k = rms_norm(p[..., ATTN_W:ATTN_W + KV_W].reshape(b, n, N_KV_HEADS, HEAD_DIM), k_norm)
    v = p[..., ATTN_W + KV_W:ATTN_W + 2 * KV_W].reshape(b, n, N_KV_HEADS, HEAD_DIM)
    a = p[..., ATTN_W + 2 * KV_W:ATTN_W + 2 * KV_W + D_CONV]
    gt = p[..., ATTN_W + 2 * KV_W + D_CONV:]
    if latent:
        q = axial_rope(q)
        k_all = jnp.concatenate([axial_rope(k), k_ctx.astype(k.dtype)], axis=1)
        v_all = jnp.concatenate([v, v_ctx.astype(v.dtype)], axis=1)
    else:
        k_all, v_all = k, v
    attn = block_attention(q, k_all, v_all)
    conv = conformer_conv(a, gt, conv_w, conv_b, ln_g, ln_b)
    out = jnp.concatenate([attn, conv], axis=-1) @ w_out
    return out, k, v

def ec_moe(h, w_router, w_gate, w_up, w_down):
    b, n, d = h.shape
    cap = CAPACITY_FACTOR * n // N_EXPERTS
    logits = jnp.einsum('bnd,de->bne', h, w_router, preferred_element_type=jnp.float32)
    aff = jax.nn.softmax(logits, axis=-1)
    gates, idx = lax.top_k(jnp.swapaxes(aff, 1, 2), cap)
    xs = jax.vmap(lambda hb, ib: hb[ib])(h, idx)
    hg = jnp.einsum('becd,edf->becf', xs, w_gate)
    hu = jnp.einsum('becd,edf->becf', xs, w_up)
    y = jnp.einsum('becf,efd->becd', jax.nn.silu(hg) * hu, w_down) * gates.astype(h.dtype)[..., None]
    return jax.vmap(lambda ib, yb: jnp.zeros((n, d), h.dtype).at[ib.reshape(-1)].add(yb.reshape(-1, d)))(idx, y)

def setup_inputs(seed: int = 0) -> dict:
    key = jax.random.key(seed)
    ks = jax.random.split(key, 24)
    f32 = jnp.float32
    nrm = lambda k, s, sc: jax.random.normal(k, s, f32) * sc
    gain = lambda k, s: 1.0 + 0.05 * jax.random.normal(k, s, f32)
    return {
        "x_prompt": nrm(ks[0], (BATCH, SEQ, D_MODEL), 1.0),
        "x_sample": nrm(ks[1], (DEC_BATCH, DEC_SEQ, D_MODEL), 1.0),
        "c": nrm(ks[2], (DEC_BATCH, D_MODEL), 1.0),
        "c_ctx": nrm(ks[3], (D_MODEL,), 1.0),
        "cache_k": nrm(ks[4], (DEC_BATCH, DEPTH, PAST_LEN, N_KV_HEADS, HEAD_DIM), 1.0),
        "cache_v": nrm(ks[5], (DEC_BATCH, DEPTH, PAST_LEN, N_KV_HEADS, HEAD_DIM), 1.0),
        "w_mod": nrm(ks[6], (DEPTH, D_MODEL, 6 * D_MODEL), 0.5 * D_MODEL ** -0.5),
        "b_mod": nrm(ks[7], (DEPTH, 6 * D_MODEL), 0.01),
        "g_pre_mix": gain(ks[8], (DEPTH, D_MODEL)),
        "g_post_mix": gain(ks[9], (DEPTH, D_MODEL)),
        "g_pre_ffn": gain(ks[10], (DEPTH, D_MODEL)),
        "g_post_ffn": gain(ks[11], (DEPTH, D_MODEL)),
        "w_in": nrm(ks[12], (DEPTH, D_MODEL, IN_W), D_MODEL ** -0.5),
        "q_norm": gain(ks[13], (DEPTH, HEAD_DIM)),
        "k_norm": gain(ks[14], (DEPTH, HEAD_DIM)),
        "conv_w": nrm(ks[15], (DEPTH, CONV_WIDTH, D_CONV), CONV_WIDTH ** -0.5),
        "conv_b": nrm(ks[16], (DEPTH, D_CONV), 0.01),
        "conv_ln_g": gain(ks[17], (DEPTH, D_CONV)),
        "conv_ln_b": nrm(ks[18], (DEPTH, D_CONV), 0.01),
        "w_out": nrm(ks[19], (DEPTH, MIX_W, D_MODEL), MIX_W ** -0.5),
        "w_router": nrm(ks[20], (DEPTH, D_MODEL, N_EXPERTS), D_MODEL ** -0.5),
        "w_gate": nrm(ks[21], (DEPTH, N_EXPERTS, D_MODEL, D_FF_EXPERT), D_MODEL ** -0.5),
        "w_up": nrm(ks[22], (DEPTH, N_EXPERTS, D_MODEL, D_FF_EXPERT), D_MODEL ** -0.5),
        "w_down": nrm(ks[23], (DEPTH, N_EXPERTS, D_FF_EXPERT, D_MODEL), D_FF_EXPERT ** -0.5),
    }

def reference(x_prompt, x_sample, c, c_ctx, cache_k, cache_v, w_mod, b_mod,
              g_pre_mix, g_post_mix, g_pre_ffn, g_post_ffn, w_in, q_norm, k_norm,
              conv_w, conv_b, conv_ln_g, conv_ln_b, w_out, w_router, w_gate, w_up, w_down):
    xp, xs = x_prompt, x_sample
    new_k, new_v = [], []
    for l in range(DEPTH):
        mix_args = (w_in[l], q_norm[l], k_norm[l], conv_w[l], conv_b[l],
                    conv_ln_g[l], conv_ln_b[l], w_out[l])
        moe_args = (w_router[l], w_gate[l], w_up[l], w_down[l])

        sh1, sc1, ga1, sh2, sc2, ga2 = modulation(c_ctx[None, :], w_mod[l], b_mod[l])
        h = rms_norm(xp, g_pre_mix[l]) * (1.0 + sc1) + sh1
        out, k_ctx, v_ctx = mixer(h, *mix_args, False, None, None)
        xp = xp + ga1 * rms_norm(out, g_post_mix[l])
        h = rms_norm(xp, g_pre_ffn[l]) * (1.0 + sc2) + sh2
        xp = xp + ga2 * rms_norm(ec_moe(h, *moe_args), g_post_ffn[l])
        new_k.append(k_ctx)
        new_v.append(v_ctx)

        sh1, sc1, ga1, sh2, sc2, ga2 = modulation(c, w_mod[l], b_mod[l])
        h = rms_norm(xs, g_pre_mix[l]) * (1.0 + sc1) + sh1
        out, _, _ = mixer(h, *mix_args, True, cache_k[:, l], cache_v[:, l])
        xs = xs + ga1 * rms_norm(out, g_post_mix[l])
        h = rms_norm(xs, g_pre_ffn[l]) * (1.0 + sc2) + sh2
        xs = xs + ga2 * rms_norm(ec_moe(h, *moe_args), g_post_ffn[l])

    k_state = jnp.stack(new_k, axis=1)
    v_state = jnp.stack(new_v, axis=1)
    return (xp, xs, k_state, v_state)


_drawn_inputs = setup_inputs


def setup_inputs(seed=0):
    import zlib

    import numpy as np

    out = dict(_drawn_inputs(seed))
    spreads = {}
    factors = {'g_post_ffn': 3.901, 'q_norm': 8.0, 'conv_b': 2.798, 'conv_ln_b': 2.85}
    for name, (base, spread) in spreads.items():
        noise = np.random.default_rng([zlib.crc32(name.encode()), seed]).standard_normal(out[name].shape)
        drawn = base * np.exp(spread * noise) if base else spread * noise
        out[name] = __import__('jax').numpy.asarray(drawn.astype(out[name].dtype))
    for name, factor in factors.items():
        out[name] = (out[name] * factor).astype(out[name].dtype)
    return out
```

```python
import numpy as np
import concourse.bass as bass
import concourse.mybir as mybir

P = 128
D = 1024
KC = D // P
NLAT, NCTX = 512, 128
NTOK = NLAT + NCTX
LT = NLAT // P
NT = NTOK // P
HD, NH, NKV = 64, 8, 2
AW, KVW, DC = NH * HD, NKV * HD, 512
CC = DC // P
TAPS, PAD = 31, 15
NE, F = 16, 1024
CL, CP = 2 * NLAT // NE, 2 * NCTX // NE
CS = CL + CP
EPS = 1e-6
HALF = 512
MOD_CHUNKS = 6 * KC

RING = 8
PRE = 6
GROUP = 4
UNITS = 6

CU = PAD + NLAT + PAD + NCTX + PAD
CY = NLAT + PAD + NCTX
CTX_Y = NLAT + PAD

TILES = [4, 0, 1, 2, 3]
SCAT0 = 16 * NT


def tok(i):
    return slice(i * P, (i + 1) * P)


def ycols(i):
    return slice(CTX_Y, CTX_Y + P) if i == LT else slice(i * P, (i + 1) * P)


def build(nc, a, outs):
    F32, U32 = mybir.dt.float32, mybir.dt.uint32
    ALU, ACT, AX = mybir.AluOpType, mybir.ActivationFunctionType, mybir.AxisListType

    def sb(name, shape, dt=F32):
        return nc.alloc_sbuf_tensor(name, shape, dt)

    def sem(name):
        return nc.alloc_semaphore(name)

    ring = sb("ring", [P, RING, KC * HALF])
    scratch = ring[:, PRE:RING, :].rearrange("p s n -> p (s n)")
    xn = scratch[:, 0:NT * D].rearrange("p (t d) -> p t d", d=D)
    xjunk = scratch[:, NT * D:(NT + 1) * D]
    at = 0
    u = scratch[:, at:at + CC * CU].rearrange("p (c n) -> p c n", n=CU); at += CC * CU
    prob = scratch[:, at:at + 2 * NTOK].rearrange("p (b n) -> p b n", n=NTOK)
    pool_prod = scratch[:, at:at + 2 * CY].rearrange("p (b n) -> p b n", n=CY)
    at += 2 * NTOK
    probT = scratch[:, at:at + 2 * NTOK].rearrange("p (b n) -> p b n", n=NTOK); at += 2 * NTOK
    qk = scratch[:, at:at + 2 * NTOK].rearrange("p (b n) -> p b n", n=NTOK)
    attn = scratch[:, at:at + 2 * AW].rearrange("p (b n) -> p b n", n=AW)
    at += 2 * NTOK
    qk2 = scratch[:, at:at + NTOK]; ln_rstd = qk2; at += NTOK
    rope_a = scratch[:, at:at + NTOK]; at += NTOK
    assert at <= scratch.shape[1]
    ln_sq = scratch[:, 0:CC * NTOK].rearrange("p (c n) -> p c n", n=NTOK)
    ln_tanh = scratch[:, 0:CC * CY].rearrange("p (c n) -> p c n", n=CY)

    x = sb("x", [P, NT, D])
    big = sb("big", [P, KC, NTOK])
    y = sb("y", [P, CC, CY])
    rows = sb("rows", [P, 2, D])
    gtile = sb("gtile", [P, 2, D])
    kT = sb("kT", [P, NTOK + P])
    v = sb("v", [P, NT + 1, KVW])
    ident = sb("ident", [P, P])
    ones = sb("ones", [P, P])
    prow = sb("prow", [P, P])
    pcol = sb("pcol", [P, P])
    cw_rows = sb("cw_rows", [P, P])
    cw = sb("cw", [P, TAPS, CC])
    wr = sb("wr", [P, KC, NE])
    kcache = sb("kcache", [P, KVW])
    cond = sb("cond", [P, KC, 2])
    cond_t = sb("cond_t", [P, 2 * KC])
    cond_s = sb("cond_s", [P, 2 * KC])
    mod = sb("mod", [P, MOD_CHUNKS, 2])
    a1 = sb("a1", [P, KC, 2])
    a2 = sb("a2", [P, KC, 2])
    gcol = sb("gcol", [P, 2, KC, 2])
    lnc = sb("lnc", [P, 2, CC])
    nhalf = sb("nhalf", [P, 1])
    ss = sb("ss", [P, 4 * NT])
    ms = sb("ms", [P, 4 * NT])
    rs = sb("rs", [P, 4 * NT])
    hss = sb("hss", [P, 2, 10])
    hms = sb("hms", [P, 2, 10])
    hrs = sb("hrs", [P, 2, 10])
    nmax = sb("nmax", [P, NT * NH])
    rsum = sb("rsum", [P, NT * NH])
    rinv = sb("rinv", [P, NT, NH])
    rt_max = sb("rt_max", [P, NT])
    rt_sum = sb("rt_sum", [P, NT])
    rt_inv = sb("rt_inv", [P, NT])
    rt_exp = sb("rt_exp", [P, 2, NE])
    aff = sb("aff", [P, 2, NE])
    topv = sb("topv", [NE, CS])
    topi = sb("topi", [NE, CS], U32)
    topf = sb("topf", [NE, CS])
    gateT = sb("gateT", [CS, NE])
    idxT = sb("idxT", [CS, NE], U32)
    gate_of = sb("gate_of", [CS, GROUP, 1])
    idx_of = [sb(f"idx_of{i}", [CS, 1], U32) for i in range(GROUP)]

    affT = kT[0:NE, 0:NTOK]
    cos = rows[:, 0, 0:NT * HD].rearrange("p (t d) -> p t d", d=HD)
    sin = rows[:, 0, NT * HD:2 * NT * HD].rearrange("p (t d) -> p t d", d=HD)
    gain = rows[:, 1, 0:NTOK]
    qT = big[:, 0:4, :]
    attnT = big[:, 4:8, :]
    flat = big[:].rearrange("p c n -> p (c n)")
    xT = [flat[:, i * 640:(i + 1) * 640].rearrange("p (c n) -> p c n", n=CS) for i in range(2)]
    hid = [flat[:, (2 + i) * 640:(3 + i) * 640].rearrange("p (c n) -> p c n", n=CS) for i in range(2)]
    tanh_g = flat[:, 4 * 640:5 * 640].rearrange("p (b n) -> p b n", b=2)
    act_g = flat[:, 5 * 640:6 * 640].rearrange("p (b n) -> p b n", b=2)
    a2x = flat[:, 6 * 640:7 * 640].rearrange("p (c n) -> p c n", n=CS)
    sh2x = flat[:, 7 * 640:8 * 640].rearrange("p (c n) -> p c n", n=CS)
    xg = rows
    yflat = y[:].rearrange("p c n -> p (c n)")
    ys = yflat[0:CS, 0:2 * D].rearrange("p (b n) -> p b n", n=D)
    fin = ring[:, 0:2, :].rearrange("p s n -> p (s n)")[:, 0:NT * D].rearrange("p (t d) -> p t d", d=D)

    ps = nc.alloc_psum_tensor("ps", [P, 8, 512], F32)

    PB_MOD, PG = 0, MOD_CHUNKS
    PCB = PG + 4 * KC
    PLG, PLB, PCND = PCB + CC, PCB + 2 * CC, PCB + 3 * CC
    PROWS = PCND + 2 * KC

    table = nc.dram_tensor("norm_rows", [NTOK, D], F32).ap()
    accum = nc.dram_tensor("expert_sum", [NTOK, D], F32).ap()
    y_prompt, y_sample, new_k, new_v = outs
    x_rows = [a["x_sample"][0, tok(i), :] for i in range(LT)] + [a["x_prompt"][0]]
    y_rows = [y_sample[0, tok(i), :] for i in range(LT)] + [y_prompt[0]]
    w_mod, w_in, w_out = a["w_mod"][0], a["w_in"][0], a["w_out"][0]

    def cols(w, c0, n):
        return w[:, c0:c0 + n].rearrange("(k p) n -> p k n", p=P)

    GT0 = AW + 2 * KVW + DC
    pre_units = ([cols(w_mod, n * HALF, HALF) for n in range(4)]
                 + [cols(w_in, GT0, DC), cols(w_in, AW + 2 * KVW, DC)]
                 + [cols(w_mod, n * HALF, HALF) for n in range(4, 12)]
                 + [cols(w_in, AW, 2 * KVW), cols(w_in, 0, AW)]
                 + [cols(w_out, n * HALF, HALF) for n in range(2)])
    U_GT, U_A, U_MOD, U_KV, U_Q, U_WO = 4, 5, 6, 14, 15, 16
    NPRE = len(pre_units)
    assert NPRE % PRE == 0

    def slot(s, n=HALF):
        return ring[:, s, 0:KC * n].rearrange("p (k n) -> p k n", n=n)

    landed = [sem(f"landed{s}") for s in range(RING)]
    pre_used = sem("pre_used")
    units_used = sem("units_used")
    x_in = [sem(f"x_in{i}") for i in range(NT)]
    params_in, cw_in, cond_dma, tab_in, wr_in, kc_in, vc_in = (
        sem(n) for n in ("params_in", "cw_in", "cond_dma", "tab_in", "wr_in", "kc_in", "vc_in"))
    ident_in = sem("ident_in")
    consts = sem("consts")
    pT, pcols = sem("pT"), sem("pcols")
    cond_tanh, cond_ok = sem("cond_tanh"), sem("cond_ok")
    mod_mm, mod_ok, mod_raw = sem("mod_mm"), sem("mod_ok"), sem("mod_raw")
    ss_ok, rs_ok, xn_ok = sem("ss_ok"), sem("rs_ok"), sem("xn_ok")
    xT_mm, hT_act, hT_dve = sem("xT_mm"), sem("hT_act"), sem("hT_dve")
    glu_mm, gt_ok, glu_ok, pads = sem("glu_mm"), sem("gt_ok"), sem("glu_ok"), sem("pads")
    conv_dve, conv_pool, pool_step = sem("conv_dve"), sem("conv_pool"), sem("pool_step")
    qkv_mm, qkv_cp, qk_sq, qk_ss, qk_rs, rope_ok = (
        sem(n) for n in ("qkv_mm", "qkv_cp", "qk_sq", "qk_ss", "qk_rs", "rope_ok"))
    gain_ok = sem("gain_ok")
    qkT_mm, qkT_cp = sem("qkT_mm"), sem("qkT_cp")
    g_mm, g_ok = sem("g_mm"), sem("g_ok")
    s_mm, max_ok, exp_ok, t_mm, pt_dve, pt_act, pv_mm = (
        sem(n) for n in ("s_mm", "max_ok", "exp_ok", "t_mm", "pt_dve", "pt_act", "pv_mm"))
    o_norm, ot_mm, ot_ok = sem("o_norm"), sem("ot_mm"), sem("ot_ok")
    ln_mm, ln_cen, ln_sq_ok, ln_var, ln_rs, ln_yn, ln_th, conv_ok = (
        sem(n) for n in ("ln_mm", "ln_cen", "ln_sq_ok", "ln_var", "ln_rs", "ln_yn", "ln_th", "conv_ok"))
    out_mm, oss_ok, ors_ok, x1_ok, xss_ok, xrs_ok, xn2_ok = (
        sem(n) for n in ("out_mm", "oss_ok", "ors_ok", "x1_ok", "xss_ok", "xrs_ok", "xn2_ok"))
    table_in = [sem("table_in0"), sem("table_in1")]
    x2T_mm, h2_act, h2_dve, rt_mm, rt_mx, rt_ex, aff_ok, affT_mm, affT_ok = (
        sem(n) for n in ("x2T_mm", "h2_act", "h2_dve", "rt_mm", "rt_mx", "rt_ex", "aff_ok", "affT_mm", "affT_ok"))
    top_ok, topT_mm, slots_ok, picked = sem("top_ok"), sem("topT_mm"), sem("slots_ok"), sem("picked")
    gathered = [sem("gathered0"), sem("gathered1")]
    xgT_mm, xTe_ok, th_ok, hid_ok, ye_act, ye_dve = (
        sem(n) for n in ("xgT_mm", "xTe_ok", "th_ok", "hid_ok", "ye_act", "ye_dve"))
    mul_ok, silu_ok, conv_dve_step, rope_half, fin_mul, pool_fin, act_fin, new_k_done, pool_turn = (
        sem(n) for n in ("mul_ok", "silu_ok", "conv_dve_step", "rope_half", "fin_mul", "pool_fin", "act_fin", "new_k_done", "pool_turn"))
    scattered = sem("scattered")
    fin_in = [sem(f"fin_in{i}") for i in range(NT)]
    fss_ok, frs_ok, fin_ok, y_done, kv_done = (
        sem(n) for n in ("fss_ok", "frs_ok", "fin_ok", "y_done", "kv_done"))
    act_step, dve_step, zero_ok = sem("act_step"), sem("dve_step"), sem("zero_ok")

    def stepper(eng, s):
        count = [0]

        def step(ins):
            count[0] += 1
            ins.then_inc(s, 1)
            eng.wait_ge(s, count[0])
        return step

    heads = [(t, i, h) for t, i in enumerate(TILES) for h in range(NH)]
    NU = len(heads)
    LN_MEAN, LN_VAR = 8, 16
    stages = []
    for n in range(NU):
        if n == LN_MEAN:
            stages.append("mean")
        if n == LN_VAR:
            stages.append("var")
        stages.append(n)
    s_buf = {st: 2 * (k % 2) for k, st in enumerate(stages)}
    LATE = {"norm": 20, "silu": 24, "gate": 33}
    n_lat = lambda n: max(0, n - NH)

    block = nc.Block()
    block.__enter__()

    @block.sync
    def _(sp):
        for n, src in enumerate(pre_units):
            if n >= PRE:
                sp.wait_ge(pre_used, n - PRE + 1)
            sp.dma_start(slot(n % PRE, src.shape[2]), src).then_inc(landed[n % PRE], 16)

        def group(b):
            for q in range(GROUP):
                e = b * GROUP + q
                for n, (w, half) in enumerate((("w_gate", 0), ("w_up", 0), ("w_gate", 1), ("w_up", 1),
                                               ("w_down", 0), ("w_down", 1))):
                    j = UNITS * q + n
                    sp.wait_ge(units_used, b * (GROUP * UNITS) + (j + 1))
                    src = a[w][0, e].rearrange("(k p) n -> p k n", p=P)[:, :, half * HALF:(half + 1) * HALF]
                    sp.dma_start(slot(j % RING), src).then_inc(landed[j % RING], 16)

        with sp.Fori(0, NE // GROUP) as b:
            group(b)

        sp.wait_ge(scattered, SCAT0 + 16 * NE)
        sp.wait_ge(units_used, RING + UNITS * NE)
        for i in range(NT):
            sp.dma_start(fin[:, i, :], accum[tok(i), :]).then_inc(fin_in[i], 16)
        for i in range(NT):
            sp.wait_ge(fin_ok, i + 1)
            sp.dma_start(y_rows[i], fin[:, i, :]).then_inc(y_done, 16)
        sp.wait_ge(y_done, 16 * NT)

    @block.gpsimd
    def _(pool):
        step = stepper(pool, pool_step)
        nc.gpsimd.memset(nhalf[:], -0.5)
        nc.gpsimd.memset(ones[:], 1.0 / DC).then_inc(consts, 1)
        nc.gpsimd.memset(big[:, 0:2, 0:512], 0.0).then_inc(zero_ok, 1)
        pool.wait_ge(zero_ok, 1)
        zero = big[:, 0:2, 0:512]
        for i in range(NT):
            pool.dma_start(accum[tok(i), :].rearrange("p (a n) -> p a n", a=2), zero).then_inc(scattered, 16)

        def root(n, src, dst, scale, ready, value, done):
            pool.wait_ge(ready, value)
            tmp = ms[:, n[0]:n[1]]
            step(nc.gpsimd.tensor_scalar(tmp, src, scale, EPS, ALU.mult, ALU.add))
            nc.gpsimd.tensor_tensor(dst, tmp, nhalf[:].to_broadcast([P, n[1] - n[0]]), ALU.pow).then_inc(done, 1)

        pool.wait_ge(consts, 1)
        for i in range(NT):
            root((i, i + 1), ss[:, i:i + 1], rs[:, i:i + 1], 1.0 / D, ss_ok, i + 1, rs_ok)

        pool.wait_ge(xT_mm, KC + 1)
        nc.gpsimd.memset(u[:, :, 0:PAD], 0.0)
        nc.gpsimd.memset(u[:, :, PAD + NLAT:2 * PAD + NLAT], 0.0)
        nc.gpsimd.memset(u[:, :, CU - PAD:CU], 0.0).then_inc(pads, 1)

        c = CC - 1
        pool.wait_ge(glu_ok, 2 * CC)
        pool.wait_ge(pads, 1)
        taps = [0]

        def conv(n):
            for k in range(taps[0], min(TAPS, taps[0] + n)):
                if k == 0:
                    step(nc.gpsimd.tensor_scalar(y[:, c, :], u[:, c, 0:CY], cw[:, 0, c:c + 1],
                                                 pcol[:, PCB + c:PCB + c + 1], ALU.mult, ALU.add))
                else:
                    step(nc.gpsimd.tensor_scalar(pool_prod[:, k % 2, :], u[:, c, k:k + CY], cw[:, k, c:c + 1],
                                                 None, ALU.mult))
                    step(nc.gpsimd.tensor_tensor(y[:, c, :], y[:, c, :], pool_prod[:, k % 2, :], ALU.add))
            taps[0] = min(TAPS, taps[0] + n)

        conv(16)
        for t in range(NT):
            pool.wait_ge(qk_ss, t + 1)
            step(nc.gpsimd.tensor_scalar(hms[:, t % 2, :], hss[:, t % 2, :], 1.0 / HD, EPS, ALU.mult, ALU.add))
            nc.gpsimd.tensor_tensor(hrs[:, t % 2, :], hms[:, t % 2, :], nhalf[:].to_broadcast([P, 10]),
                                    ALU.pow).then_inc(qk_rs, 1)
            conv(3)
        conv(TAPS)
        nc.gpsimd.memset(hms[:, 0, 0:1], 0.0).then_inc(conv_pool, 1)

        pool.wait_ge(ln_var, 1)
        nc.gpsimd.tensor_tensor(ln_rstd, ln_rstd, nhalf[:].to_broadcast([P, NTOK]), ALU.pow).then_inc(ln_rs, 1)

        for t in range(NT):
            root((NT + t, NT + t + 1), ss[:, NT + t:NT + t + 1], rs[:, NT + t:NT + t + 1], 1.0 / D, oss_ok, t + 1, ors_ok)
            n = 2 * NT + t
            root((n, n + 1), ss[:, n:n + 1], rs[:, n:n + 1], 1.0 / D, xss_ok, t + 1, xrs_ok)

        def gather(q, value, gvalue, first):
            pool.wait_ge(picked, value)
            if not first:
                pool.wait_ge(xgT_mm, gvalue)
            pool.sem_inc(pool_turn, 1)
            nc.gpsimd.indirect_dma_start(
                out=xg[0:CS, q % 2, :], out_offset=None, in_=table,
                in_offset=bass.IndirectOffsetOnAxis(ap=idx_of[q][:, :1], axis=0)).then_inc(gathered[q % 2], 16)

        pool.wait_ge(table_in[0], 16 * 3)
        pool.wait_ge(table_in[1], 16 * 2)
        gather(0, 1, 0, True)
        gather(1, 2, 0, True)

        def group(b, last):
            for q in range(GROUP):
                e = b * GROUP + q
                if not (last and q >= 2):
                    gather((q + 2) % GROUP, e + 3, e + 1, False)
                pool.wait_ge(ye_act, e + 2)
                pool.wait_ge(ye_dve, e + 2)
                pool.wait_ge(scattered, e * 16 + SCAT0)
                pool.sem_inc(pool_turn, 1)
                nc.gpsimd.indirect_dma_start(
                    out=accum, out_offset=bass.IndirectOffsetOnAxis(ap=idx_of[q][:, :1], axis=0),
                    in_=ys[:, q % 2, :], in_offset=None, compute_op=ALU.add).then_inc(scattered, 16)

        with pool.Fori(0, NE // GROUP - 1) as b:
            group(b, False)
        group(NE // GROUP - 1, True)

        for i in range(NT):
            n = 3 * NT + i
            pool.wait_ge(fss_ok, i + 1)
            nc.gpsimd.tensor_scalar(ms[:, n:n + 1], ss[:, n:n + 1], 1.0 / D, EPS, ALU.mult, ALU.add).then_inc(pool_fin, 1)
            pool.wait_ge(pool_fin, i + 1)
            nc.gpsimd.tensor_tensor(rs[:, n:n + 1], ms[:, n:n + 1], nhalf[:], ALU.pow).then_inc(frs_ok, 1)

    @block.scalar
    def _(act):
        step = stepper(act, act_step)
        act.dma_start(ident[:], a["ident"]).then_inc(ident_in, 16)
        for r, name, n in ((PB_MOD, "b_mod", MOD_CHUNKS), (PG, "g_pre_mix", KC), (PG + KC, "g_post_mix", KC),
                           (PG + 2 * KC, "g_pre_ffn", KC), (PG + 3 * KC, "g_post_ffn", KC),
                           (PCB, "conv_b", CC), (PLG, "conv_ln_g", CC), (PLB, "conv_ln_b", CC)):
            act.dma_start(prow[r:r + n, :], a[name][0].rearrange("(c p) -> c p", p=P)).then_inc(params_in, 16)
        act.dma_start(prow[PCND:PCND + KC, :], a["c"][0].rearrange("(c p) -> c p", p=P)).then_inc(params_in, 16)
        act.dma_start(prow[PCND + KC:PROWS, :], a["c_ctx"].rearrange("(c p) -> c p", p=P)).then_inc(params_in, 16)
        for i in range(NT):
            act.dma_start(x[:, i, :], x_rows[i]).then_inc(x_in[i], 16)
        act.dma_start(cw_rows[0:TAPS * CC, :], a["conv_w"][0].rearrange("t (c p) -> (t c) p", p=P)).then_inc(cw_in, 16)
        act.dma_start(kcache[:], a["cache_k"][0, 0].rearrange("s h d -> s (h d)")).then_inc(kc_in, 16)
        act.dma_start(v[:, LT, :], a["cache_v"][0, 0].rearrange("s h d -> s (h d)")).then_inc(vc_in, 16)
        act.dma_start(cos, a["cos"].rearrange("(t p) d -> p t d", p=P)).then_inc(tab_in, 16)
        act.dma_start(sin, a["sin"].rearrange("(t p) d -> p t d", p=P)).then_inc(tab_in, 16)
        for h in range(NH + NKV):
            src = a["q_norm" if h < NH else "k_norm"]
            act.dma_start(gain[:, h * HD:(h + 1) * HD], src[0:1, :].to_broadcast([P, HD])).then_inc(tab_in, 16)
        act.dma_start(wr[:], a["w_router"][0].rearrange("(k p) e -> p k e", p=P)).then_inc(wr_in, 16)

        act.wait_ge(pcols, 1)
        nc.scalar.activation(cond_t[:], pcol[:, PCND:PROWS], ACT.Tanh, scale=0.5).then_inc(cond_tanh, 1)

        for i in range(NT):
            act.wait_ge(x_in[i], 16)
            step(nc.scalar.activation(xjunk, x[:, i, :], ACT.Square, accum_out=ss[:, i:i + 1]))
            act.sem_inc(ss_ok, 1)

        act.wait_ge(mod_ok, 1)
        act.wait_ge(scattered, SCAT0)
        for c in range(0, KC, 2):
            act.wait_ge(xT_mm, c + 1)
            nc.scalar.activation(big[:, c, 0:NLAT], ps[:, 4 + c % 4, :], ACT.Identity,
                                 scale=a1[:, c, 0:1], bias=mod[:, c, 0:1]).then_inc(hT_act, 1)
        act.wait_ge(xT_mm, KC + 1)
        for c in range(4):
            nc.scalar.activation(big[:, c, NLAT:NTOK], ps[:, 0, c * P:(c + 1) * P], ACT.Identity,
                                 scale=a1[:, c, 1:2], bias=mod[:, c, 1:2]).then_inc(hT_act, 1)

        for c in range(CC):
            act.wait_ge(glu_mm, c + 1)
            nc.scalar.activation(u[:, c, PAD:PAD + NLAT], ps[:, 4 + c, :], ACT.Tanh, scale=0.5).then_inc(gt_ok, 1)
            nc.scalar.activation(u[:, c, 2 * PAD + NLAT:CU - PAD], ps[:, c, 0:P], ACT.Tanh, scale=0.5).then_inc(gt_ok, 1)

        act.wait_ge(mod_mm, 2)
        nc.scalar.activation(mod[:, 16:48, :], ps[:, 3, 0:64].rearrange("p (c n) -> p c n", n=2), ACT.Copy).then_inc(mod_raw, 1)

        def copies(t):
            i = TILES[t]
            act.wait_ge(qkv_mm, t + 1)
            if t >= 2:
                act.wait_ge(rope_ok, t - 1)
                act.wait_ge(qkT_mm, 2 * (t - 1))
            if t == 2:
                act.wait_ge(new_k_done, 16)
            nc.scalar.activation(qk[:, t % 2, 0:AW].rearrange("p (j g d) -> p g j d", g=2, d=HD),
                                 ps[:, 4 + t % 2, :].rearrange("p (g j d) -> p g j d", g=2, d=HD), ACT.Copy).then_inc(qkv_cp, 1)
            nc.scalar.activation(qk[:, t % 2, AW:NTOK], ps[:, 6 + t % 2, 0:KVW], ACT.Copy).then_inc(qkv_cp, 1)
            nc.scalar.activation(v[:, i if i < LT else NT, :], ps[:, 6 + t % 2, KVW:2 * KVW], ACT.Copy).then_inc(qkv_cp, 1)
            act.wait_ge(qkv_cp, 3 * t + 2)
            if t >= 1:
                act.wait_ge(qk_ss, t)
            nc.scalar.activation(qk2, qk[:, t % 2, :], ACT.Square).then_inc(qk_sq, 1)

        def transposed(t):
            i = TILES[t]
            act.wait_ge(qkT_mm, 2 * (t + 1))
            nc.scalar.activation(qT[:, :, tok(i)], ps[:, t % 2, :].rearrange("p (j n) -> p j n", n=P), ACT.Copy).then_inc(qkT_cp, 1)
            at = NTOK if i == LT else i * P
            nc.scalar.activation(kT[:, at:at + P], ps[:, 2, 0:P], ACT.Copy).then_inc(qkT_cp, 1)

        for t in range(NT):
            copies(t)
            if t == 0:
                act.wait_ge(rope_ok, 1)
                act.dma_start(new_k[0, 0].rearrange("s h d -> s (h d)"), qk[:, 0, AW:NTOK]).then_inc(new_k_done, 16)
            if t >= 1:
                transposed(t - 1)
        act.wait_ge(qkv_cp, 3)
        act.dma_start(new_v[0, 0].rearrange("s h d -> s (h d)"), v[:, NT, :]).then_inc(kv_done, 16)
        transposed(NT - 1)

        def g_out(base):
            for n in range(4):
                act.wait_ge(g_mm, base + n + 1)
                nc.scalar.activation(gtile[:, n // 2, (n % 2) * 512:(n % 2 + 1) * 512], ps[:, (4 if base == 0 else 2) + n, :],
                                     ACT.Copy).then_inc(g_ok, 1)
        g_out(0)

        def exp(n):
            t, i, h = heads[n]
            w = P if i == LT else NTOK
            act.wait_ge(max_ok, n + 1)
            if n < 2:
                act.wait_ge(conv_pool, 1)
            else:
                act.wait_ge(t_mm, n - 1)
            s = s_buf[n]
            step(nc.scalar.activation(prob[:, n % 2, 0:w], ps[:, s:s + 2, :].rearrange("p b n -> p (b n)")[:, 0:w],
                                      ACT.Exp, bias=nmax[:, n:n + 1], accum_out=rsum[:, n:n + 1]))
            act.sem_inc(exp_ok, 1)

        def fifth(n):
            if heads[n][1] == LT:
                return
            act.wait_ge(t_mm, n + 1)
            if n >= 2:
                act.wait_ge(pv_mm, n - 1)
            nc.scalar.activation(probT[:, n % 2, 512:640], ps[:, 5, 0:P], ACT.Copy).then_inc(pt_act, 1)

        def heads_out(t):
            act.wait_ge(ot_mm, t + 1)
            nc.scalar.activation(attnT[:, :, tok(TILES[t])], ps[:, 7, :].rearrange("p (j n) -> p j n", n=P),
                                 ACT.Copy).then_inc(ot_ok, 1)

        for n in range(NU + 3):
            if n == LN_MEAN:
                act.wait_ge(ln_cen, 2)
                nc.scalar.activation(ln_sq[:, :, 0:NLAT], y[:, :, 0:NLAT], ACT.Square).then_inc(ln_sq_ok, 1)
                nc.scalar.activation(ln_sq[:, :, NLAT:NTOK], y[:, :, CTX_Y:CY], ACT.Square).then_inc(ln_sq_ok, 1)
            c = (n - LATE["silu"]) // 2
            if n >= LATE["silu"] and (n - LATE["silu"]) % 2 == 0 and c < CC:
                act.wait_ge(ln_yn, 2)
                act.wait_ge(ln_mm, 2)
                step(nc.scalar.activation(y[:, c, :], y[:, c, :], ACT.Identity, scale=lnc[:, 0, c:c + 1], bias=lnc[:, 1, c:c + 1]))
                nc.scalar.activation(ln_tanh[:, c, :], y[:, c, :], ACT.Tanh).then_inc(ln_th, 1)
            if n < NU:
                exp(n)
            if 1 <= n <= NU:
                fifth(n - 1)
            if n >= NH + 2 and (n - 2) % NH == 0:
                heads_out((n - 2) // NH - 1)

        def epilogue(t):
            i = TILES[t]
            act.wait_ge(out_mm, t + 1)
            if t >= 2:
                act.wait_ge(table_in[t % 2], 16 * (t // 2))
                act.wait_ge(x2T_mm, 2 * (t - 1))
            else:
                act.wait_ge(rope_ok, NT)
            n = NT + t
            s = 2 * (t % 2)
            step(nc.scalar.activation(rows[:, t % 2, :], ps[:, s:s + 2, :].rearrange("p b n -> p (b n)"),
                                      ACT.Square, accum_out=ss[:, n:n + 1]))
            act.sem_inc(oss_ok, 1)
            act.wait_ge(x1_ok, t + 1)
            n = 2 * NT + t
            step(nc.scalar.activation(rows[:, t % 2, :], x[:, i, :], ACT.Square, accum_out=ss[:, n:n + 1]))
            act.sem_inc(xss_ok, 1)
            act.wait_ge(xrs_ok, t + 1)
            nc.scalar.activation(rows[:, t % 2, :], x[:, i, :], ACT.Copy, scale=rs[:, n:n + 1]).then_inc(xn2_ok, 1)
            act.wait_ge(xn2_ok, t + 1)
            act.dma_start(table[tok(i), :], rows[:, t % 2, :]).then_inc(table_in[t % 2], 16)
            act.wait_ge(x2T_mm, 2 * t + 1)
            for c in range(4):
                g = 1 if i == LT else 0
                nc.scalar.activation(big[:, c, tok(i)], ps[:, 4, c * P:(c + 1) * P], ACT.Identity,
                                     scale=a2[:, c, g:g + 1], bias=mod[:, 24 + c, g:g + 1]).then_inc(h2_act, 1)
            act.wait_ge(rt_mx, t + 1)
            step(nc.scalar.activation(rt_exp[:, t % 2, :], ps[:, 6, 0:NE], ACT.Exp, bias=rt_max[:, t:t + 1],
                                      accum_out=rt_sum[:, t:t + 1]))
            act.sem_inc(rt_ex, 1)

        for t in range(NT):
            epilogue(t)
        g_out(4)

        def group(b):
            for q in range(GROUP):
                e = b * GROUP + q
                for j in range(2):
                    act.wait_ge(units_used, e * UNITS + (RING + 2 * j + 2))
                    act.wait_ge(hid_ok, e * 2 + (j + 1))
                    nc.scalar.activation(tanh_g[:, j, :], ps[:, 2 + 2 * j, 0:4 * CS], ACT.Tanh, scale=0.5).then_inc(th_ok, 1)
                act.wait_ge(units_used, e * UNITS + (RING + 5))
                act.wait_ge(scattered, e * 16 + (SCAT0 - 16))
                nc.scalar.activation(ys[:, q % 2, 0:512], ps[0:CS, 6, :], ACT.Copy, scale=gate_of[:, q, :]).then_inc(ye_act, 1)

        act.sem_inc(ye_act, 1)
        with act.Fori(0, NE // GROUP) as b:
            group(b)

        for i in range(NT):
            act.wait_ge(fin_in[i], 16)
            n = 3 * NT + i
            if i >= 1:
                act.wait_ge(act_fin, i)
            nc.scalar.activation(rows[:, 0, :], fin[:, i, :], ACT.Square, accum_out=ss[:, n:n + 1]).then_inc(act_fin, 1)
            act.wait_ge(act_fin, i + 1)
            act.sem_inc(fss_ok, 1)
        act.wait_ge(kv_done, 16)
        act.wait_ge(new_k_done, 16)

    @block.tensor
    def _(pe):
        def used(ins, unit):
            ins.then_inc(units_used if unit >= NPRE - PRE else pre_used, 1)

        def wait_unit(n):
            pe.wait_ge(landed[n % PRE], 16 * (n // PRE + 1))

        def T(out, in_, k=P):
            return nc.tensor.transpose(out, in_, ident[0:k, 0:k])

        pe.wait_ge(ident_in, 16)
        pe.wait_ge(params_in, 16 * 10)
        T(ps[:, 0, 0:PROWS], prow[0:PROWS, :], PROWS).then_inc(pT, 1)
        pe.wait_ge(cw_in, 16)
        T(ps[:, 1, 0:TAPS * CC], cw_rows[0:TAPS * CC, :], TAPS * CC).then_inc(pT, 1)
        pe.wait_ge(kc_in, 16)
        T(ps[:, 3, 0:P], kcache[:]).then_inc(pT, 1)

        def modulate(n, bank, at):
            unit = n if n < 4 else U_MOD + n - 4
            wait_unit(unit)
            w = slot(unit % PRE)
            for m in range(4):
                for k in range(KC):
                    ins = nc.tensor.matmul(ps[:, bank, at + 2 * m:at + 2 * m + 2], w[:, k, m * P:(m + 1) * P],
                                           cond[:, k, :], start=(k == 0), stop=(k == KC - 1))
            used(ins, unit)

        pe.wait_ge(cond_ok, 1)
        for n in range(4):
            modulate(n, 2, 8 * n)
        pe.wait_ge(pre_used, 4)
        pe.sem_inc(mod_mm, 1)

        pe.wait_ge(xn_ok, NT)
        for c in range(KC):
            if c >= 4:
                pe.wait_ge(hT_act if c % 2 == 0 else hT_dve, (c - 4) // 2 + 1)
            for i in range(LT):
                ins = T(ps[:, 4 + c % 4, tok(i)], xn[:, i, c * P:(c + 1) * P])
            ins.then_inc(xT_mm, 1)
        pe.wait_ge(pcols, 2)
        for c in range(KC):
            ins = T(ps[:, c // 4, (c % 4) * P:(c % 4 + 1) * P], xn[:, LT, c * P:(c + 1) * P])
        ins.then_inc(xT_mm, 1)

        pe.wait_ge(hT_act, 8)
        pe.wait_ge(hT_dve, 8)
        pe.wait_ge(pcols, 3)
        for m in range(2 * CC):
            unit = U_GT + m // CC
            wait_unit(unit)
            if m >= CC:
                pe.wait_ge(gt_ok, 2 * (m - CC + 1))
            w = slot(unit % PRE)
            for bank, cols_ in ((4 + m % 4, slice(0, NLAT)), (m % 4, slice(NLAT, NTOK))):
                for k in range(KC):
                    ins = nc.tensor.matmul(ps[:, bank, 0:cols_.stop - cols_.start], w[:, k, (m % 4) * P:(m % 4 + 1) * P],
                                           big[:, k, cols_], start=(k == 0), stop=(k == KC - 1))
            ins.then_inc(glu_mm, 1)
            if m % CC == CC - 1:
                pe.wait_ge(glu_mm, m + 1)
                pe.sem_inc(pre_used, 1)

        pe.wait_ge(glu_ok, 2 * CC)
        for n in range(4, 12):
            modulate(n, 3, 8 * (n - 4))
        pe.wait_ge(units_used, 2)
        pe.sem_inc(mod_mm, 1)

        def project(t):
            i = TILES[t]
            wait_unit(U_KV)
            wait_unit(U_Q)
            if t >= 2:
                pe.wait_ge(qkv_cp, 3 * (t - 1))
            for k in range(KC):
                ins = nc.tensor.matmul(ps[:, 6 + t % 2, 0:2 * KVW], big[:, k, tok(i)], slot(U_KV % PRE, 2 * KVW)[:, k, :],
                                       start=(k == 0), stop=(k == KC - 1))
            if t == NT - 1:
                used(ins, U_KV)
            for k in range(KC):
                ins = nc.tensor.matmul(ps[:, 4 + t % 2, :], big[:, k, tok(i)], slot(U_Q % PRE)[:, k, :],
                                       start=(k == 0), stop=(k == KC - 1))
            ins.then_inc(qkv_mm, 1)
            if t == NT - 1:
                pe.wait_ge(qkv_mm, NT)
                pe.sem_inc(units_used, 1)

        def transpose_qk(t):
            pe.wait_ge(rope_ok, t + 1)
            if t >= 1:
                pe.wait_ge(qkT_cp, 2 * t)
            for j in range(4):
                ins = T(ps[:, t % 2, j * P:(j + 1) * P],
                        qk[:, t % 2, j * P:(j + 1) * P])
            ins.then_inc(qkT_mm, 1)
            T(ps[:, 2, 0:P], qk[:, t % 2, AW:NTOK]).then_inc(qkT_mm, 1)

        for t in range(NT):
            project(t)
            if t >= 1:
                transpose_qk(t - 1)

        def g_tiles(layer, bank, done):
            for n in range(4):
                g, half = n // 2, n % 2
                for c in range(4):
                    col = gcol[:, layer, 4 * half + c, g:g + 1]
                    ins = T(ps[:, bank + n, c * P:(c + 1) * P], col.to_broadcast([P, P]))
                ins.then_inc(g_mm, 1)

        pe.wait_ge(mod_ok, 2)
        pe.wait_ge(qkv_cp, 3 * NT)
        g_tiles(0, 4, g_mm)
        transpose_qk(NT - 1)

        def scores(n):
            t, i, h = heads[n]
            k = stages.index(n)
            prev = stages[k - 2] if k >= 2 else None
            if prev is None:
                pe.wait_ge(qkT_cp, 2 * NT)
                pe.wait_ge(pcols, 4)
                pe.wait_ge(mod_raw, 1)
            elif prev == "mean":
                pe.wait_ge(ln_cen, 2)
            elif prev == "var":
                pe.wait_ge(ln_var, 1)
            else:
                pe.wait_ge(exp_ok, prev + 1)
            s = s_buf[n]
            p0 = HD * (h // 4)
            q = qT[p0:p0 + HD, h % 4, tok(i)]
            if i == LT:
                nc.tensor.matmul(ps[:, s, 0:P], q, kT[p0:p0 + HD, NTOK:NTOK + P], start=True, stop=True).then_inc(s_mm, 1)
            else:
                nc.tensor.matmul(ps[:, s, :], q, kT[p0:p0 + HD, 0:512], start=True, stop=True)
                nc.tensor.matmul(ps[:, s + 1, 0:P], q, kT[p0:p0 + HD, 512:640], start=True, stop=True).then_inc(s_mm, 1)

        def ln_sum(which):
            prev = stages[stages.index(which) - 2]
            pe.wait_ge(exp_ok, prev + 1)
            if which == "mean":
                pe.wait_ge(conv_dve, 1)
                pe.wait_ge(conv_pool, 1)
            else:
                pe.wait_ge(ln_sq_ok, 2)
            s = s_buf[which]
            for bank, n, lo, hi in ((s, NLAT, 0, NLAT), (s + 1, NCTX, CTX_Y if which == "mean" else NLAT, None)):
                src = y[:] if which == "mean" else ln_sq
                for c in range(CC):
                    ins = nc.tensor.matmul(ps[:, bank, 0:n], ones[:], src[:, c, lo:lo + n], start=(c == 0), stop=(c == CC - 1))
            ins.then_inc(ln_mm, 1)

        def transpose_p(n):
            pe.wait_ge(exp_ok, n + 1)
            if n == 0:
                pe.wait_ge(g_ok, 4)
            else:
                pe.wait_ge(pt_dve, n)
                if n_lat(n):
                    pe.wait_ge(pt_act, n_lat(n))
            if heads[n][1] == LT:
                T(ps[:, 4, 0:P], prob[:, n % 2, 0:P]).then_inc(t_mm, 1)
                return
            for kc in range(NT):
                ins = T(ps[:, 4 + kc // 4, (kc % 4) * P:(kc % 4 + 1) * P], prob[:, n % 2, kc * P:(kc + 1) * P])
            ins.then_inc(t_mm, 1)

        def values(n):
            t, i, h = heads[n]
            pe.wait_ge(pt_dve, n + 1)
            if n_lat(n + 1):
                pe.wait_ge(pt_act, n_lat(n + 1))
            if h == 0 and t >= 1:
                pe.wait_ge(o_norm, t)
            if n == 0:
                pe.wait_ge(vc_in, 16)
            chunks = [(0, NT)] if i == LT else [(kc, kc) for kc in range(NT)]
            for m, (kc, vt) in enumerate(chunks):
                ins = nc.tensor.matmul(ps[:, 6, h * HD:(h + 1) * HD], probT[:, n % 2, kc * P:(kc + 1) * P],
                                       v[:, vt, (h // 4) * HD:(h // 4 + 1) * HD], start=(m == 0), stop=(m == len(chunks) - 1))
            ins.then_inc(pv_mm, 1)

        def transpose_o(t):
            pe.wait_ge(o_norm, t + 1)
            if t >= 1:
                pe.wait_ge(ot_ok, t)
            for j in range(4):
                ins = T(ps[:, 7, j * P:(j + 1) * P], attn[:, t % 2, j * P:(j + 1) * P])
            ins.then_inc(ot_mm, 1)

        scores(0)
        for n in range(NU + 2):
            if n + 1 == LN_MEAN:
                ln_sum("mean")
            if n + 1 == LN_VAR:
                ln_sum("var")
            if n + 1 < NU:
                scores(n + 1)
            if n < NU:
                transpose_p(n)
            if 1 <= n <= NU:
                values(n - 1)
            if n >= NH + 1 and (n - 1) % NH == 0:
                transpose_o((n - 1) // NH - 1)

        def out_project(t):
            i = TILES[t]
            s = 2 * (t % 2)
            if t == 0:
                pe.wait_ge(conv_ok, 1)
                pe.wait_ge(exp_ok, NU)
            pe.wait_ge(ot_ok, t + 1)
            if t >= 2:
                pe.wait_ge(x1_ok, t - 1)
            for n in range(2):
                unit = U_WO + n
                wait_unit(unit)
                w = slot(unit % PRE)
                for k in range(KC):
                    lhs = attnT[:, k, tok(i)] if k < 4 else y[:, k - 4, ycols(i)]
                    ins = nc.tensor.matmul(ps[:, s + n, :], lhs, w[:, k, :], start=(k == 0), stop=(k == KC - 1))
                if t == NT - 1 and n == 0:
                    used(ins, unit)
            ins.then_inc(out_mm, 1)
            if t == NT - 1:
                pe.wait_ge(out_mm, NT)
                pe.sem_inc(units_used, 1 + RING - PRE)

        def route(t):
            i = TILES[t]
            pe.wait_ge(xn2_ok, t + 1)
            if t >= 1:
                pe.wait_ge(h2_act, 4 * t)
                pe.wait_ge(h2_dve, 4 * t)
            else:
                pe.wait_ge(pt_dve, NU)
            for c in range(KC):
                ins = T(ps[:, 4 + c // 4, (c % 4) * P:(c % 4 + 1) * P], rows[:, t % 2, c * P:(c + 1) * P])
                if c % 4 == 3:
                    ins.then_inc(x2T_mm, 1)
            pe.wait_ge(h2_act, 4 * (t + 1))
            pe.wait_ge(h2_dve, 4 * (t + 1))
            if t == 0:
                pe.wait_ge(wr_in, 16)
                pe.wait_ge(o_norm, NT)
            else:
                pe.wait_ge(rt_ex, t)
            for k in range(KC):
                ins = nc.tensor.matmul(ps[:, 6, 0:NE], big[:, k, tok(i)], wr[:, k, :], start=(k == 0), stop=(k == KC - 1))
            ins.then_inc(rt_mm, 1)

        def transpose_aff(t):
            pe.wait_ge(aff_ok, t + 1)
            if t >= 1:
                pe.wait_ge(affT_ok, t)
            T(ps[0:NE, 7, 0:P], aff[:, t % 2, :]).then_inc(affT_mm, 1)

        for t in range(NT):
            out_project(t)
            if t >= 1:
                route(t - 1)
                if t >= 2:
                    transpose_aff(t - 2)
        route(NT - 1)
        transpose_aff(NT - 2)
        transpose_aff(NT - 1)

        pe.wait_ge(h2_act, 4 * NT)
        pe.wait_ge(x1_ok, NT)
        g_tiles(1, 2, g_mm)

        pe.wait_ge(top_ok, 1)
        T(ps[0:CS, 6, 0:NE], topv[:], NE).then_inc(topT_mm, 1)
        T(ps[0:CS, 7, 0:NE], topf[:], NE).then_inc(topT_mm, 1)

        def transpose_x(q, value):
            pe.wait_ge(gathered[q % 2], value)
            for c in range(KC):
                ins = T(ps[:, c // 4, (c % 4) * CS:(c % 4 + 1) * CS], xg[0:CS, q % 2, c * P:(c + 1) * P], CS)
            ins.then_inc(xgT_mm, 1)

        pe.wait_ge(g_ok, 8)
        pe.wait_ge(slots_ok, 1)
        transpose_x(0, 16)

        def group(b, last):
            for q in range(GROUP):
                e = b * GROUP + q

                def unit(n):
                    j = UNITS * q + n
                    uses = NPRE // PRE if j % RING < PRE else 0
                    pe.wait_ge(landed[j % RING], b * (16 * GROUP * UNITS // RING) + 16 * (uses + j // RING + 1))
                    return slot(j % RING)

                pe.wait_ge(xTe_ok, e * 2 + 2)
                for half in range(2):
                    pe.wait_ge(hid_ok, e * 2 + (half + 1))
                    for m in range(2):
                        w = unit(2 * half + m)
                        for f in range(4):
                            for k in range(KC):
                                ins = nc.tensor.matmul(ps[:, 2 + 2 * half + m, f * CS:(f + 1) * CS], w[:, k, f * P:(f + 1) * P],
                                                       xT[q % 2][:, k, :], start=(k == 0), stop=(k == KC - 1))
                        ins.then_inc(units_used, 1)
                if not (last and q == GROUP - 1):
                    transpose_x((q + 1) % GROUP, b * (16 * GROUP // 2) + 16 * ((q + 1) // 2 + 1))
                for n in range(2):
                    w = unit(4 + n)
                    pe.wait_ge(ye_act if n == 0 else ye_dve, e + 1)
                    for f in range(KC):
                        if n == 0 and f % 4 == 0:
                            pe.wait_ge(hid_ok, e * 2 + (3 + f // 4))
                        ins = nc.tensor.matmul(ps[0:CS, 6 + n, :], hid[q % 2][:, f, :], w[:, f, :],
                                               start=(f == 0), stop=(f == KC - 1))
                    ins.then_inc(units_used, 1)

        with pe.Fori(0, NE // GROUP - 1) as b:
            group(b, False)
        group(NE // GROUP - 1, True)

    @block.vector
    def _(dve):
        V = nc.vector
        step = stepper(dve, dve_step)
        dve.wait_ge(pT, 1)
        V.tensor_copy(pcol[:, 0:PROWS], ps[:, 0, 0:PROWS]).then_inc(pcols, 1)
        dve.wait_ge(pT, 2)
        V.tensor_scalar(cw[:].rearrange("p t c -> p (t c)"), ps[:, 1, 0:TAPS * CC], 0.5, None, ALU.mult).then_inc(pcols, 1)
        dve.wait_ge(pT, 3)
        V.tensor_copy(kT[:, NLAT:NTOK], ps[:, 3, 0:P]).then_inc(pcols, 1)
        dve.wait_ge(pcols, 3)
        step(V.tensor_scalar(lnc[:, 0, :], pcol[:, PLG:PLG + CC], 0.5, None, ALU.mult))
        step(V.tensor_scalar(lnc[:, 1, :], pcol[:, PLB:PLB + CC], 0.5, None, ALU.mult))
        dve.sem_inc(pcols, 1)
        dve.wait_ge(cond_tanh, 1)
        step(V.scalar_tensor_tensor(cond_s[:], cond_t[:], 1.0, pcol[:, PCND:PROWS], ALU.add, ALU.mult))
        V.tensor_scalar(cond[:].rearrange("p k g -> p g k"), cond_s[:].rearrange("p (g k) -> p g k", g=2), 0.5, None,
                        ALU.mult).then_inc(cond_ok, 1)

        for i in range(NT):
            dve.wait_ge(rs_ok, i + 1)
            V.tensor_scalar(xn[:, i, :], x[:, i, :], rs[:, i:i + 1], None, ALU.mult).then_inc(xn_ok, 1)

        def both(ap):
            return ap.unsqueeze(2).to_broadcast([P, ap.shape[1], 2])
        dve.wait_ge(mod_mm, 1)
        step(V.tensor_tensor(mod[:, 0:16, :], ps[:, 2, 0:32].rearrange("p (c n) -> p c n", n=2), both(pcol[:, 0:16]), ALU.add))
        step(V.scalar_tensor_tensor(a1[:], mod[:, 8:16, :], 1.0, both(pcol[:, PG:PG + KC]), ALU.add, ALU.mult))
        dve.sem_inc(mod_ok, 1)

        dve.wait_ge(scattered, SCAT0)
        for c in range(1, KC, 2):
            dve.wait_ge(xT_mm, c + 1)
            V.tensor_scalar(big[:, c, 0:NLAT], ps[:, 4 + c % 4, :], a1[:, c, 0:1], mod[:, c, 0:1],
                            ALU.mult, ALU.add).then_inc(hT_dve, 1)
        dve.wait_ge(xT_mm, KC + 1)
        for c in range(4, KC):
            V.tensor_scalar(big[:, c, NLAT:NTOK], ps[:, 1, (c - 4) * P:(c - 3) * P], a1[:, c, 1:2], mod[:, c, 1:2],
                            ALU.mult, ALU.add).then_inc(hT_dve, 1)

        dve.wait_ge(tab_in, 16 * 12)
        step(V.tensor_scalar(gain[:, 0:AW], gain[:, 0:AW], HD ** -0.5, None, ALU.mult))

        for c in range(CC):
            dve.wait_ge(glu_mm, CC + c + 1)
            dve.wait_ge(gt_ok, 2 * (c + 1))
            for lo, hi, bank in ((PAD, PAD + NLAT, 4 + c), (2 * PAD + NLAT, CU - PAD, c)):
                V.scalar_tensor_tensor(u[:, c, lo:hi], u[:, c, lo:hi], 1.0, ps[:, bank, 0:hi - lo],
                                       ALU.add, ALU.mult).then_inc(glu_ok, 1)
        dve.wait_ge(glu_ok, 2 * CC)
        dve.wait_ge(pads, 1)

        taps = [0]
        steps0 = 0

        def conv(n):
            for k in range(taps[0], min(TAPS, taps[0] + n)):
                for c in range(CC - 1):
                    if k == 0:
                        V.tensor_scalar(y[:, c, :], u[:, c, 0:CY], cw[:, 0, c:c + 1], pcol[:, PCB + c:PCB + c + 1],
                                        ALU.mult, ALU.add).then_inc(conv_dve_step, 1)
                    else:
                        dve.wait_ge(conv_dve_step, (CC - 1) * (k - 1) + c + 1)
                        V.scalar_tensor_tensor(y[:, c, :], u[:, c, k:k + CY], cw[:, k, c:c + 1], y[:, c, :],
                                               ALU.mult, ALU.add).then_inc(conv_dve_step, 1)
            taps[0] = min(TAPS, taps[0] + n)

        conv(12)

        dve.wait_ge(mod_raw, 1)
        step(V.tensor_tensor(mod[:, 16:48, :], mod[:, 16:48, :], both(pcol[:, 16:48]), ALU.add))
        step(V.scalar_tensor_tensor(a2[:], mod[:, 32:40, :], 1.0, both(pcol[:, PG + 2 * KC:PG + 3 * KC]), ALU.add, ALU.mult))
        step(V.tensor_tensor(gcol[:, 0], mod[:, 16:24, :], both(pcol[:, PG + KC:PG + 2 * KC]), ALU.mult))
        step(V.tensor_tensor(gcol[:, 1], mod[:, 40:48, :], both(pcol[:, PG + 3 * KC:PG + 4 * KC]), ALU.mult))
        dve.sem_inc(mod_ok, 1)

        NHH = NH + NKV
        for t in range(NT):
            i = TILES[t]
            dve.wait_ge(qk_sq, t + 1)
            V.tensor_reduce(hss[:, t % 2, :], qk2.rearrange("p (h d) -> p h d", d=HD), AX.X, ALU.add).then_inc(qk_ss, 1)
            cur = qk[:, t % 2, :]
            step(V.tensor_tensor(cur, cur, gain, ALU.mult))
            dve.wait_ge(qk_rs, t + 1)
            step(V.tensor_tensor(cur.rearrange("p (h d) -> p h d", d=HD), cur.rearrange("p (h d) -> p h d", d=HD),
                                 hrs[:, t % 2, :].unsqueeze(2).to_broadcast([P, NHH, HD]), ALU.mult))
            pair = cur.rearrange("p (h a s d) -> p s h a d", h=NHH, a=2, s=2)
            part = rope_a.rearrange("p (h a s d) -> p s h a d", h=NHH, a=2, s=2)
            sn = sin[:, i, :].rearrange("p (a s d) -> p s a d", a=2, s=2)
            for s in range(2):
                tab = sn[:, s].unsqueeze(1).to_broadcast([P, NHH, 2, 16])
                V.tensor_tensor(part[:, s], pair[:, 1 - s], tab, ALU.mult).then_inc(rope_half, 1)
            dve.wait_ge(rope_half, 2 * (t + 1))
            step(V.tensor_tensor(cur.rearrange("p (h d) -> p h d", d=HD), cur.rearrange("p (h d) -> p h d", d=HD),
                                 cos[:, i, :].unsqueeze(1).to_broadcast([P, NHH, HD]), ALU.mult))
            V.tensor_tensor(cur, cur, rope_a, ALU.add).then_inc(rope_ok, 1)
            dve.wait_ge(rope_ok, t + 1)
            conv(3)
        conv(TAPS)
        dve.wait_ge(conv_dve_step, (CC - 1) * TAPS)
        dve.sem_inc(conv_dve, 1)

        def head_max(n):
            w = P if heads[n][1] == LT else NTOK
            dve.wait_ge(s_mm, n + 1)
            s = s_buf[n]
            V.tensor_reduce(nmax[:, n:n + 1], ps[:, s:s + 2, :].rearrange("p b n -> p (b n)")[:, 0:w], AX.X, ALU.max,
                            negate=True).then_inc(max_ok, 1)

        def first_four(n):
            w = P if heads[n][1] == LT else 512
            dve.wait_ge(t_mm, n + 1)
            if n >= 2:
                dve.wait_ge(pv_mm, n - 1)
            V.tensor_copy(probT[:, n % 2, 0:w], ps[:, 4, 0:w]).then_inc(pt_dve, 1)

        def normalise(t):
            dve.wait_ge(pv_mm, NH * (t + 1))
            dve.wait_ge(exp_ok, NH * (t + 1))
            step(V.reciprocal(rinv[:, t, :], rsum[:, t * NH:(t + 1) * NH]))
            if t >= 2:
                dve.wait_ge(ot_mm, t - 1)
            V.tensor_tensor(attn[:, t % 2, :].rearrange("p (h d) -> p h d", d=HD),
                            ps[:, 6, :].rearrange("p (h d) -> p h d", d=HD),
                            rinv[:, t, :].unsqueeze(2).to_broadcast([P, NH, HD]), ALU.mult).then_inc(o_norm, 1)

        head_max(0)
        dve.wait_ge(qkT_mm, 2 * NT)
        for n in range(NU + 2):
            if n + 1 == LN_MEAN:
                dve.wait_ge(ln_mm, 1)
                s = s_buf["mean"]
                V.tensor_tensor(y[:, :, 0:NLAT], y[:, :, 0:NLAT],
                                ps[:, s, :].unsqueeze(1).to_broadcast([P, CC, NLAT]), ALU.subtract).then_inc(ln_cen, 1)
                V.tensor_tensor(y[:, :, CTX_Y:CY], y[:, :, CTX_Y:CY],
                                ps[:, s + 1, 0:P].unsqueeze(1).to_broadcast([P, CC, NCTX]), ALU.subtract).then_inc(ln_cen, 1)
            if n + 1 == LN_VAR:
                dve.wait_ge(ln_mm, 2)
                s = s_buf["var"]
                V.tensor_scalar(ln_rstd, ps[:, s:s + 2, :].rearrange("p b n -> p (b n)")[:, 0:NTOK], EPS, None,
                                ALU.add).then_inc(ln_var, 1)
            if n + 1 == LATE["norm"]:
                dve.wait_ge(ln_rs, 1)
                V.tensor_tensor(y[:, :, 0:NLAT], y[:, :, 0:NLAT],
                                ln_rstd[:, 0:NLAT].unsqueeze(1).to_broadcast([P, CC, NLAT]), ALU.mult).then_inc(ln_yn, 1)
                V.tensor_tensor(y[:, :, CTX_Y:CY], y[:, :, CTX_Y:CY],
                                ln_rstd[:, NLAT:NTOK].unsqueeze(1).to_broadcast([P, CC, NCTX]), ALU.mult).then_inc(ln_yn, 1)
            if n + 1 == LATE["gate"]:
                dve.wait_ge(ln_th, CC)
                V.scalar_tensor_tensor(y[:], ln_tanh, 1.0, y[:], ALU.add, ALU.mult).then_inc(conv_ok, 1)
            if n + 1 < NU:
                head_max(n + 1)
            if n < NU:
                first_four(n)
            if n >= NH and n % NH == 0:
                normalise(n // NH - 1)

        def epilogue(t):
            i = TILES[t]
            g = 1 if i == LT else 0
            s = 2 * (t % 2)
            dve.wait_ge(ors_ok, t + 1)
            if t == 0:
                dve.wait_ge(g_ok, 4)
            buf = rows[:, t % 2, :]
            step(V.scalar_tensor_tensor(buf, ps[:, s:s + 2, :].rearrange("p b n -> p (b n)"), rs[:, NT + t:NT + t + 1],
                                        gtile[:, g, :], ALU.mult, ALU.mult))
            V.tensor_tensor(x[:, i, :], x[:, i, :], buf, ALU.add).then_inc(x1_ok, 1)

        def h2(t):
            i = TILES[t]
            g = 1 if i == LT else 0
            dve.wait_ge(x2T_mm, 2 * t + 2)
            for c in range(4, KC):
                V.tensor_scalar(big[:, c, tok(i)], ps[:, 5, (c - 4) * P:(c - 3) * P], a2[:, c, g:g + 1],
                                mod[:, 24 + c, g:g + 1], ALU.mult, ALU.add).then_inc(h2_dve, 1)
            dve.wait_ge(rt_mm, t + 1)
            V.tensor_reduce(rt_max[:, t:t + 1], ps[:, 6, 0:NE], AX.X, ALU.max, negate=True).then_inc(rt_mx, 1)
            dve.wait_ge(rt_ex, t + 1)
            step(V.reciprocal(rt_inv[:, t:t + 1], rt_sum[:, t:t + 1]))
            if t >= 2:
                dve.wait_ge(affT_mm, t - 1)
            V.tensor_scalar(aff[:, t % 2, :], rt_exp[:, t % 2, :], rt_inv[:, t:t + 1], None, ALU.mult).then_inc(aff_ok, 1)

        def aff_out(t):
            dve.wait_ge(affT_mm, t + 1)
            V.tensor_copy(affT[:, tok(TILES[t])], ps[0:NE, 7, 0:P]).then_inc(affT_ok, 1)

        def top(cols_, at, rounds, tiles):
            dve.wait_ge(affT_ok, tiles)
            w = affT[:, cols_]
            for r in range(rounds):
                o = slice(at + 8 * r, at + 8 * r + 8)
                step(V.max(topv[:, o], w))
                step(V.max_index(topi[:, o], topv[:, o], w))
                if r < rounds - 1:
                    step(V.match_replace(w, topv[:, o], w, -1.0))

        for t in range(NT):
            epilogue(t)
            h2(t)
            if t >= 1:
                aff_out(t - 1)
            if t == 2:
                top(slice(NLAT, NTOK), CL, CP // 8, 1)
        aff_out(NT - 1)

        dve.wait_ge(rt_mm, NT)
        for dst, src in ((a2x, a2[:]), (sh2x, mod[:, 24:32, :])):
            step(V.tensor_copy(dst[:, :, 0:CL], src[:, :, 0:1].to_broadcast([P, KC, CL])))
            step(V.tensor_copy(dst[:, :, CL:CS], src[:, :, 1:2].to_broadcast([P, KC, CP])))

        top(slice(0, NLAT), 0, CL // 8, NT)
        step(V.tensor_copy(topf[:, 0:CL], topi[:, 0:CL]))
        step(V.tensor_scalar(topf[:, CL:CS], topi[:, CL:CS], float(NLAT), None, ALU.add))
        dve.sem_inc(top_ok, 1)
        dve.wait_ge(topT_mm, 2)
        step(V.tensor_copy(gateT[:], ps[0:CS, 6, 0:NE]))
        step(V.tensor_copy(idxT[:], ps[0:CS, 7, 0:NE]))

        def pick(e, q):
            V.tensor_copy(gate_of[:, q, :], gateT[:, bass.ds(e, 1)])
            V.tensor_copy(idx_of[q][:], idxT[:, bass.ds(e, 1)]).then_inc(picked, 1)

        def columns(q, value):
            dve.wait_ge(xgT_mm, value)
            for j in range(2):
                src = ps[:, j, 0:4 * CS].rearrange("p (c n) -> p c n", n=CS)
                V.tensor_tensor(xT[q % 2][:, 4 * j:4 * j + 4, :], src, a2x[:, 4 * j:4 * j + 4, :], ALU.mult).then_inc(mul_ok, 1)
            for j in range(2):
                dve.wait_ge(mul_ok, value * 2 + (j - 1))
                V.tensor_tensor(xT[q % 2][:, 4 * j:4 * j + 4, :], xT[q % 2][:, 4 * j:4 * j + 4, :],
                                sh2x[:, 4 * j:4 * j + 4, :], ALU.add).then_inc(xTe_ok, 1)

        dve.sem_inc(slots_ok, 1)
        pick(0, 0)
        pick(1, 1)
        dve.sem_inc(hid_ok, 2)
        dve.sem_inc(ye_dve, 1)
        columns(0, 1)

        def group(b, last):
            for q in range(GROUP):
                e = b * GROUP + q
                if not (last and q >= 2):
                    dve.wait_ge(scattered, e * 16 + (SCAT0 - 16))
                    pick(e + 2, (q + 2) % GROUP)
                for j in range(2):
                    dve.wait_ge(th_ok, e * 2 + (j + 1))
                    V.scalar_tensor_tensor(act_g[:, j, :], tanh_g[:, j, :], 1.0, ps[:, 2 + 2 * j, 0:4 * CS],
                                           ALU.add, ALU.mult).then_inc(silu_ok, 1)
                    dve.wait_ge(silu_ok, e * 2 + (j + 1))
                    V.scalar_tensor_tensor(hid[q % 2][:, 4 * j:4 * j + 4, :].rearrange("p c n -> p (c n)"), act_g[:, j, :], 0.5,
                                           ps[:, 3 + 2 * j, 0:4 * CS], ALU.mult, ALU.mult).then_inc(hid_ok, 1)
                if not (last and q == GROUP - 1):
                    columns((q + 1) % GROUP, e + 2)
                dve.wait_ge(units_used, e * UNITS + (RING + 6))
                dve.wait_ge(scattered, e * 16 + (SCAT0 - 16))
                V.tensor_scalar(ys[:, q % 2, 512:1024], ps[0:CS, 7, :], gate_of[:, q, :], None, ALU.mult).then_inc(ye_dve, 1)

        with dve.Fori(0, NE // GROUP - 1) as b:
            group(b, False)
        group(NE // GROUP - 1, True)

        for i in range(NT):
            n = 3 * NT + i
            dve.wait_ge(frs_ok, i + 1)
            V.scalar_tensor_tensor(fin[:, i, :], fin[:, i, :], rs[:, n:n + 1], gtile[:, 1 if i == LT else 0, :],
                                   ALU.mult, ALU.mult).then_inc(fin_mul, 1)
            dve.wait_ge(fin_mul, i + 1)
            V.tensor_tensor(fin[:, i, :], fin[:, i, :], x[:, i, :], ALU.add).then_inc(fin_ok, 1)

    block.__exit__(None, None, None)


_INS = ['x_prompt', 'x_sample', 'c', 'c_ctx', 'cache_k', 'cache_v', 'w_mod', 'b_mod', 'g_pre_mix', 'g_post_mix',
        'g_pre_ffn', 'g_post_ffn', 'w_in', 'q_norm', 'k_norm', 'conv_w', 'conv_b', 'conv_ln_g', 'conv_ln_b',
        'w_out', 'w_router', 'w_gate', 'w_up', 'w_down']
_OUTS = [(1, NCTX, D), (1, NLAT, D), (1, 1, NCTX, NKV, HD), (1, 1, NCTX, NKV, HD)]


def _constants():
    grid, half = 64, HD // 4
    freqs = (np.float32(10000.0) ** (-np.arange(half, dtype=np.float32) / np.float32(half))).astype(np.float32)
    pos = np.arange(NLAT)
    cos, sin = np.ones((NTOK, HD), np.float32), np.zeros((NTOK, HD), np.float32)
    for axis, p in enumerate((pos // grid, pos % grid)):
        ang = p.astype(np.float32)[:, None] * freqs[None, :]
        at = axis * 2 * half
        cos[:NLAT, at:at + half] = cos[:NLAT, at + half:at + 2 * half] = np.cos(ang)
        sin[:NLAT, at:at + half] = -np.sin(ang)
        sin[:NLAT, at + half:at + 2 * half] = np.sin(ang)
    return {"ident": np.eye(P, dtype=np.float32), "cos": cos, "sin": sin}


def kernel(**inputs):
    import concourse.bacc as bacc
    from concourse.bass_utils import run_bass_kernel_spmd

    nc = bacc.Bacc("TRN2", target_bir_lowering=False, num_devices=1)
    arrays, aps = {}, {}
    for name, value in [(n, np.ascontiguousarray(inputs[n])) for n in _INS] + list(_constants().items()):
        arrays[f"in_{name}"] = value
        aps[name] = nc.dram_tensor(f"in_{name}", value.shape, mybir.dt.from_np(value.dtype), kind="ExternalInput").ap()
    outs = [nc.dram_tensor(f"out_{i}", shape, mybir.dt.float32, kind="ExternalOutput").ap() for i, shape in enumerate(_OUTS)]
    build(nc, aps, outs)
    r = run_bass_kernel_spmd(nc, [arrays], core_ids=[0])
    return tuple(r.results[0][f"out_{i}"] for i in range(len(_OUTS)))
```

```python
import numpy as np
import concourse.bass as bass
import concourse.mybir as mybir

P = 128
D = 1024
KC = D // P
NLAT, NCTX = 512, 128
NTOK = NLAT + NCTX
LT = NLAT // P
NT = NTOK // P
HD, NH, NKV = 64, 8, 2
AW, KVW, DC = NH * HD, NKV * HD, 512
CC = DC // P
TAPS, PAD = 31, 15
NE, F = 16, 1024
CL, CP = 2 * NLAT // NE, 2 * NCTX // NE
CS = CL + CP
EPS = 1e-6
PRODS = 3
HALF = 512
MOD_CHUNKS = 6 * KC

RING = 8
PRE = 6
GROUP = 4
UNITS = 6
QR = 32
GS = -(-CS // QR)
CSP = GS * QR
QN = D // (GS + 1)

CU = PAD + NLAT + PAD + NCTX + PAD
CY = NLAT + PAD + NCTX
CTX_Y = NLAT + PAD

TILES = [4, 0, 1, 2, 3]
SCAT0 = 16 * NT


def tok(i):
    return slice(i * P, (i + 1) * P)


def ycols(i):
    return slice(CTX_Y, CTX_Y + P) if i == LT else slice(i * P, (i + 1) * P)


def build(nc, a, outs):
    F32, U32 = mybir.dt.float32, mybir.dt.uint32
    ALU, ACT, AX = mybir.AluOpType, mybir.ActivationFunctionType, mybir.AxisListType

    def sb(name, shape, dt=F32):
        return nc.alloc_sbuf_tensor(name, shape, dt)

    def sem(name):
        return nc.alloc_semaphore(name)

    ring = sb("ring", [P, RING, KC * HALF])
    scratch = ring[:, PRE:RING, :].rearrange("p s n -> p (s n)")
    xn = scratch[:, 0:NT * D].rearrange("p (t d) -> p t d", d=D)
    xjunk = scratch[:, NT * D:(NT + 1) * D]
    at = 0
    u = scratch[:, at:at + CC * CU].rearrange("p (c n) -> p c n", n=CU); at += CC * CU
    taps_out = scratch[:, at:at + PRODS * CY].rearrange("p (b n) -> p b n", n=CY)
    prob = scratch[:, at:at + 2 * NTOK].rearrange("p (b n) -> p b n", n=NTOK); at += 2 * NTOK
    probT = scratch[:, at:at + 4 * NTOK].rearrange("p (b n) -> p b n", n=NTOK); at += 2 * NTOK
    qk = scratch[:, at:at + 2 * NTOK].rearrange("p (b n) -> p b n", n=NTOK); at += 2 * NTOK
    qk2 = scratch[:, at:at + NTOK]; rinv_rep = qk2[:, 0:AW]; at += NTOK
    rope_a = scratch[:, at:at + NTOK]; rinvT = rope_a[:, 0:AW]; at += NTOK
    assert at <= scratch.shape[1]
    ln_sq = scratch[:, 0:CC * NTOK].rearrange("p (c n) -> p c n", n=NTOK)
    ln_tanh = scratch[:, 0:CC * CY].rearrange("p (c n) -> p c n", n=CY)

    x = sb("x", [P, NT, D])
    big = sb("big", [P, KC, NTOK])
    y = sb("y", [P, CC, CY])
    rows = sb("rows", [P, 2, D])
    gtile = sb("gtile", [P, 2, D])
    kT = sb("kT", [P, NTOK + P])
    v = sb("v", [P, NT + 1, KVW])
    ident = sb("ident", [P, P])
    ones = sb("ones", [P, P])
    pcol = sb("pcol", [P, P])
    cw = sb("cw", [P, TAPS, CC])
    wr = sb("wr", [P, KC, NE])
    cond = sb("cond", [P, KC, 32])
    sel = sb("sel", [P, 2])
    sh_rows = sb("sh_rows", [2, NE])
    rbias = sb("rbias", [P, 2, NE])
    rlog = sb("rlog", [P, 2, NE])
    cond_t = sb("cond_t", [P, 2 * KC])
    cond_s = sb("cond_s", [P, 2 * KC])
    mod = sb("mod", [P, MOD_CHUNKS, 2])
    a1 = sb("a1", [P, KC, 2])
    a2 = sb("a2", [P, KC, 2])
    gcol = sb("gcol", [P, 2, KC, 2])
    lnc = sb("lnc", [P, 2, CC])
    nhalf = sb("nhalf", [P, 1])
    ss = sb("ss", [P, 4 * NT])
    ss2 = sb("ss2", [P, 4 * NT])
    ms = sb("ms", [P, 4 * NT])
    ln_m = sb("ln_m", [P, NT])
    ln_rs = sb("ln_rs", [P, NT])
    rs = sb("rs", [P, 4 * NT])
    hss = sb("hss", [P, 2, 10])
    hms = sb("hms", [P, 2, 10])
    hrs = sb("hrs", [P, 2, 10])
    nmax = sb("nmax", [P, NT * NH])
    rsum = sb("rsum", [P, NT * NH])
    rinv = sb("rinv", [P, NT, NH])
    rt_max = sb("rt_max", [P, NT])
    rt_sum = sb("rt_sum", [P, NT])
    rt_inv = sb("rt_inv", [P, NT])
    rt_exp = sb("rt_exp", [P, 2, NE])
    aff = sb("aff", [P, 2, NE])
    topv = sb("topv", [NE, CS])
    topi = sb("topi", [NE, CS], U32)
    topf = sb("topf", [NE, CS])
    gate3 = sb("gate3", [P, GS, NE])
    idxT = sb("idxT", [CS, NE], U32)
    gate_of = sb("gate_of", [P, GROUP, GS])
    idx_of = [sb(f"idx_of{i}", [CS, 1], U32) for i in range(GROUP)]

    affT = kT[0:NE, 0:NTOK]
    modrow_a = gtile[:, 0, :].rearrange("p (b n) -> p b n", n=HALF)
    modrow_b = rows[:, :, 0:HALF]
    cos = rows[:, 0, 0:NT * HD].rearrange("p (t d) -> p t d", d=HD)
    sin = rows[:, 0, NT * HD:2 * NT * HD].rearrange("p (t d) -> p t d", d=HD)
    gain = rows[:, 1, 0:NTOK]
    kcache = rows[:, 0, 640:640 + KVW]
    prow = rows[:, 0, 768:768 + P]
    cw_rows = rows[:, 0, 896:896 + P]
    pick2 = rows[0:2, 1, 640:640 + 2 * P].rearrange("p (g n) -> p g n", n=P)
    wra = cond[:].rearrange("p k n -> p (k n)").rearrange("p (g k e) -> p g k e", g=2, e=NE)
    qT = big[:, 0:4, :]
    attnT = big[:, 4:8, :]
    flat = big[:].rearrange("p c n -> p (c n)")
    BUF = KC * CSP
    xT = [flat[:, i * BUF:(i + 1) * BUF].rearrange("p (c n) -> p c n", n=CSP) for i in range(2)]
    hid = flat[:, 2 * BUF:3 * BUF].rearrange("p (c n) -> p c n", n=CSP)
    tanh_g = flat[:, 3 * BUF:3 * BUF + GS * QN]
    act_g = flat[:, 4 * BUF:4 * BUF + GS * QN]
    a2x = flat[:, 5 * BUF:5 * BUF + KC * CS].rearrange("p (c n) -> p c n", n=CS)
    gq = flat[0:NE, 5 * BUF + KC * CS:5 * BUF + KC * CS + GS * P].rearrange("p (r n) -> p r n", n=P)
    assert 5 * BUF + KC * CS + GS * P <= KC * NTOK
    sh2x = v[:].rearrange("p t n -> p (t n)")[:, 0:KC * CS].rearrange("p (c n) -> p c n", n=CS)
    xg = rows
    yflat = y[:].rearrange("p c n -> p (c n)")
    ys = yflat[0:CS, 0:2 * D].rearrange("p (b n) -> p b n", n=D)
    fin = ring[:, 0:2, :].rearrange("p s n -> p (s n)")[:, 0:NT * D].rearrange("p (t d) -> p t d", d=D)

    ps = nc.alloc_psum_tensor("ps", [P, 8, 512], F32)

    def two(bank):
        return ps[:, bank:bank + 2, :].rearrange("p b n -> p (b n)")[:, 0:GS * QN]

    PB_MOD, PG = 0, MOD_CHUNKS
    PCB = PG + 4 * KC
    PLG, PLB, PCND = PCB + CC, PCB + 2 * CC, PCB + 3 * CC
    PROWS = PCND + 2 * KC

    table = nc.dram_tensor("norm_rows", [NTOK, D], F32).ap()
    accum = nc.dram_tensor("expert_sum", [NTOK, D], F32).ap()
    y_prompt, y_sample, new_k, new_v = outs
    x_rows = [a["x_sample"][0, tok(i), :] for i in range(LT)] + [a["x_prompt"][0]]
    y_rows = [y_sample[0, tok(i), :] for i in range(LT)] + [y_prompt[0]]
    w_mod, w_in, w_out = a["w_mod"][0], a["w_in"][0], a["w_out"][0]

    def cols(w, c0, n):
        return w[:, c0:c0 + n].rearrange("(k p) n -> p k n", p=P)

    GT0 = AW + 2 * KVW + DC
    pre_units = ([cols(w_mod, n * HALF, HALF) for n in range(4)]
                 + [cols(w_in, GT0, DC), cols(w_in, AW + 2 * KVW, DC)]
                 + [cols(w_in, AW, 2 * KVW), cols(w_in, 0, AW)]
                 + [cols(w_mod, n * HALF, HALF) for n in range(4, 12)]
                 + [cols(w_out, n * HALF, HALF) for n in range(2)])
    U_GT, U_A, U_KV, U_Q, U_MOD, U_WO = 4, 5, 6, 7, 8, 16
    NPRE = len(pre_units)
    assert NPRE % PRE == 0

    def slot(s, n=HALF):
        return ring[:, s, 0:KC * (n if n < HALF else HALF)].rearrange("p (k n) -> p k n", n=n)

    landed = [sem(f"landed{s}") for s in range(RING)]
    pre_used = sem("pre_used")
    units_used = sem("units_used")
    x_in = [sem(f"x_in{i}") for i in range(NT)]
    params_in, cw_in, tab_in, wr_in, kc_in, vc_in = (
        sem(n) for n in ("params_in", "cw_in", "tab_in", "wr_in", "kc_in", "vc_in"))
    ident_in = sem("ident_in")
    consts = sem("consts")
    pT, pcols = sem("pT"), sem("pcols")
    cond_tanh, cond_ok = sem("cond_tanh"), sem("cond_ok")
    mod_mm, mod_ok, mod_raw = sem("mod_mm"), sem("mod_ok"), sem("mod_raw")
    ss_ok, rs_ok, xn_ok = sem("ss_ok"), sem("rs_ok"), sem("xn_ok")
    xT_mm, hT_act, hT_dve = sem("xT_mm"), sem("hT_act"), sem("hT_dve")
    glu_mm, gt_ok, glu_ok, pads = sem("glu_mm"), sem("gt_ok"), sem("glu_ok"), sem("pads")
    prod_ok, add_ok, modrow_ok, modrow_mm = sem("prod_ok"), sem("add_ok"), sem("modrow_ok"), sem("modrow_mm")
    rowsum_ok, rep_ok, rinvT_mm, rinvT_ok = sem("rowsum_ok"), sem("rep_ok"), sem("rinvT_mm"), sem("rinvT_ok")
    ln_ms, ln_rsT, wra_ok, shr_mm, shr_ok, rb_mm, rb_ok = (
        sem(n) for n in ("ln_ms", "ln_rsT", "wra_ok", "shr_mm", "shr_ok", "rb_mm", "rb_ok"))
    small_in = sem("small_in")
    conv_dve, conv_pool, pool_step = sem("conv_dve"), sem("conv_pool"), sem("pool_step")
    qkv_mm, qkv_cp, qk_sq, qk_ss, qk_rs, rope_ok = (
        sem(n) for n in ("qkv_mm", "qkv_cp", "qk_sq", "qk_ss", "qk_rs", "rope_ok"))
    gain_ok = sem("gain_ok")
    qkT_mm, qkT_cp = sem("qkT_mm"), sem("qkT_cp")
    g_mm, g_ok = sem("g_mm"), sem("g_ok")
    s_mm, max_ok, exp_ok, t_mm, pt_dve, pt_act, pv_mm = (
        sem(n) for n in ("s_mm", "max_ok", "exp_ok", "t_mm", "pt_dve", "pt_act", "pv_mm"))
    o_norm, ot_mm, ot_ok = sem("o_norm"), sem("ot_mm"), sem("ot_ok")
    ln_mm, ln_cen, ln_sq_ok, ln_rs_ok, ln_yn, ln_th, conv_ok = (
        sem(n) for n in ("ln_mm", "ln_cen", "ln_sq_ok", "ln_rs_ok", "ln_yn", "ln_th", "conv_ok"))
    out_mm, oss_ok, ors_ok, x1_ok, xss_ok, xrs_ok, xn2_ok = (
        sem(n) for n in ("out_mm", "oss_ok", "ors_ok", "x1_ok", "xss_ok", "xrs_ok", "xn2_ok"))
    table_in = [sem("table_in0"), sem("table_in1")]
    x2T_mm, h2_act, h2_dve, rt_mm, rt_mx, rt_ex, aff_ok, affT_mm, affT_ok = (
        sem(n) for n in ("x2T_mm", "h2_act", "h2_dve", "rt_mm", "rt_mx", "rt_ex", "aff_ok", "affT_mm", "affT_ok"))
    top_ok, topT_mm, slots_ok, picked = sem("top_ok"), sem("topT_mm"), sem("slots_ok"), sem("picked")
    gathered = [sem("gathered0"), sem("gathered1")]
    xgT_mm, xTe_ok, th_ok, hid_ok, ye_act, ye_dve = (
        sem(n) for n in ("xgT_mm", "xTe_ok", "th_ok", "hid_ok", "ye_act", "ye_dve"))
    hidT_mm, hidc_act, hidc_dve, gate_at = (sem(n) for n in ("hidT_mm", "hidc_act", "hidc_dve", "gate_at"))
    mul_ok, silu_ok, conv_dve_step, rope_half, fin_mul, pool_fin, act_fin, new_k_done, pool_turn = (
        sem(n) for n in ("mul_ok", "silu_ok", "conv_dve_step", "rope_half", "fin_mul", "pool_fin", "act_fin", "new_k_done", "pool_turn"))
    scattered = sem("scattered")
    fin_in = [sem(f"fin_in{i}") for i in range(NT)]
    fss_ok, frs_ok, fin_ok, y_done, kv_done = (
        sem(n) for n in ("fss_ok", "frs_ok", "fin_ok", "y_done", "kv_done"))
    act_step, dve_step, zero_ok = sem("act_step"), sem("dve_step"), sem("zero_ok")

    def stepper(eng, s):
        count = [0]

        def step(ins):
            count[0] += 1
            ins.then_inc(s, 1)
            eng.wait_ge(s, count[0])
        return step

    heads = [(t, i, h) for t, i in enumerate(TILES) for h in range(NH)]
    NU = len(heads)
    BETWEEN = {9: "mod8", 11: "mod9", 13: "mod10", 15: "mod11", 27: "mean", 29: "var", 31: "rstd"}
    CONV_AT = range(8, 26, 2)
    LN_SQ_AT = 28
    SILU_AT, GATE_AT = 33, 38
    stages = []
    for n in range(NU):
        if n in BETWEEN:
            stages.append(BETWEEN[n])
        stages.append(n)
    s_buf = {st: 2 * (k % 2) for k, st in enumerate(stages)}
    n_lat = lambda n: max(0, n - NH)

    block = nc.Block()
    block.__enter__()

    @block.sync
    def _(sp):
        sp.dma_start(prow[PCND:PCND + KC, :], a["c"][0].rearrange("(c p) -> c p", p=P)).then_inc(params_in, 16)
        sp.dma_start(prow[PCND + KC:PROWS, :], a["c_ctx"].rearrange("(c p) -> c p", p=P)).then_inc(params_in, 16)
        for r, name, n in ((PB_MOD, "b_mod", MOD_CHUNKS), (PG, "g_pre_mix", KC), (PG + KC, "g_post_mix", KC)):
            sp.dma_start(prow[r:r + n, :], a[name][0].rearrange("(c p) -> c p", p=P)).then_inc(params_in, 16)
        for n, src in enumerate(pre_units):
            if n == 2:
                for i in range(NT):
                    sp.dma_start(x[:, i, :], x_rows[i]).then_inc(x_in[i], 16)
            if n >= PRE:
                sp.wait_ge(pre_used, n - PRE + 1)
            sp.dma_start(slot(n % PRE, src.shape[2]), src).then_inc(landed[n % PRE], 16)

        def unit(j, w, e, half):
            src = a[w][0, e].rearrange("(h k p) n -> h p k n", p=P, h=2)[half]
            sp.dma_start(slot(j % RING, D), src).then_inc(landed[j % RING], 16)

        for half in range(2):
            sp.wait_ge(units_used, half + 1)
            unit(half, "w_gate", 0, half)

        def group(b, last):
            for q in range(GROUP):
                e = b * GROUP + q
                n = 2 + UNITS * q
                for w, after in (("w_up", 0), ("w_gate", 1), ("w_down", 0)):
                    if after and last and q == GROUP - 1:
                        continue
                    for half in range(2):
                        sp.wait_ge(units_used, b * (GROUP * UNITS) + (n + 1))
                        unit(n, w, e + after, half)
                        n += 1

        with sp.Fori(0, NE // GROUP - 1) as b:
            group(b, False)
        group(NE // GROUP - 1, True)

        sp.wait_ge(scattered, SCAT0 + 16 * NE)
        sp.wait_ge(units_used, RING + UNITS * NE)
        for i in range(NT):
            sp.dma_start(fin[:, i, :], accum[tok(i), :]).then_inc(fin_in[i], 16)
        for i in range(NT):
            sp.wait_ge(fin_ok, i + 1)
            sp.dma_start(y_rows[i], fin[:, i, :]).then_inc(y_done, 16)
        sp.wait_ge(y_done, 16 * NT)

    @block.gpsimd
    def _(pool):
        step = stepper(pool, pool_step)
        nc.gpsimd.memset(cond[:], 0.0).then_inc(consts, 1)
        nc.gpsimd.memset(nhalf[:], -0.5)
        nc.gpsimd.memset(ones[:], 1.0 / DC).then_inc(consts, 1)
        nc.gpsimd.memset(big[:, 0:2, 0:512], 0.0).then_inc(zero_ok, 1)
        pool.wait_ge(zero_ok, 1)
        zero = big[:, 0:2, 0:512]
        for i in range(NT):
            pool.dma_start(accum[tok(i), :].rearrange("p (a n) -> p a n", a=2), zero).then_inc(scattered, 16)

        def root(n, src, dst, scale, ready, value, done):
            pool.wait_ge(ready, value)
            tmp = ms[:, n[0]:n[1]]
            step(nc.gpsimd.tensor_scalar(tmp, src, scale, EPS, ALU.mult, ALU.add))
            nc.gpsimd.tensor_tensor(dst, tmp, nhalf[:].to_broadcast([P, n[1] - n[0]]), ALU.pow).then_inc(done, 1)

        pool.wait_ge(consts, 2)
        for i in range(NT):
            root((i, i + 1), ss[:, i:i + 1], rs[:, i:i + 1], 1.0 / D, ss_ok, i + 1, rs_ok)

        pool.wait_ge(xT_mm, KC + 1)
        nc.gpsimd.memset(u[:, :, 0:PAD], 0.0)
        nc.gpsimd.memset(u[:, :, PAD + NLAT:2 * PAD + NLAT], 0.0)
        nc.gpsimd.memset(u[:, :, CU - PAD:CU], 0.0).then_inc(pads, 1)

        taps = [1]

        def conv(n):
            for k in range(taps[0], min(TAPS, taps[0] + n)):
                pool.wait_ge(prod_ok, k + 1)
                if k > 1:
                    pool.wait_ge(add_ok, k - 1)
                nc.gpsimd.tensor_tensor(y[:, CC - 1, :], y[:, CC - 1, :], taps_out[:, k % PRODS, :], ALU.add).then_inc(add_ok, 1)
            taps[0] = min(TAPS, taps[0] + n)

        for t in range(NT):
            conv(4)
            pool.wait_ge(qk_ss, t + 1)
            step(nc.gpsimd.tensor_scalar(hms[:, t % 2, :], hss[:, t % 2, :], 1.0 / HD, EPS, ALU.mult, ALU.add))
            nc.gpsimd.tensor_tensor(hrs[:, t % 2, :], hms[:, t % 2, :], nhalf[:].to_broadcast([P, 10]),
                                    ALU.pow).then_inc(qk_rs, 1)
            conv(2)
        conv(TAPS)
        pool.wait_ge(add_ok, TAPS - 1)
        pool.sem_inc(conv_pool, 1)

        for t in range(NT):
            if t == 3:
                pool.wait_ge(ln_ms, 1)
                nc.gpsimd.tensor_tensor(ln_rs[:], ln_m[:], nhalf[:].to_broadcast([P, NT]), ALU.pow).then_inc(ln_rs_ok, 1)
            pool.wait_ge(rowsum_ok, t + 1)
            if t >= 1:
                pool.wait_ge(rinvT_mm, t)
            else:
                pool.wait_ge(rope_ok, NT)
            nc.gpsimd.tensor_copy(rinv_rep.rearrange("p (h d) -> p h d", d=HD),
                                  rinv[:, t, :].unsqueeze(2).to_broadcast([P, NH, HD])).then_inc(rep_ok, 1)

        for t in range(NT):
            for n, ready, done in ((NT + t, oss_ok, ors_ok), (2 * NT + t, xss_ok, xrs_ok)):
                pool.wait_ge(ready, 2 * (t + 1))
                step(nc.gpsimd.tensor_scalar(ms[:, n:n + 1], ss[:, n:n + 1], EPS, ss2[:, n:n + 1], ALU.add, ALU.add))
                nc.gpsimd.tensor_tensor(rs[:, n:n + 1], ms[:, n:n + 1], nhalf[:], ALU.pow).then_inc(done, 1)

        def gather(q, value, gvalue, first):
            pool.wait_ge(picked, value)
            if not first:
                pool.wait_ge(xgT_mm, gvalue)
            pool.sem_inc(pool_turn, 1)
            nc.gpsimd.indirect_dma_start(
                out=xg[0:CS, q % 2, :], out_offset=None, in_=table,
                in_offset=bass.IndirectOffsetOnAxis(ap=idx_of[q][:, :1], axis=0)).then_inc(gathered[q % 2], 16)

        pool.wait_ge(table_in[0], 16 * 3)
        pool.wait_ge(table_in[1], 16 * 2)
        gather(0, 1, 0, True)
        gather(1, 2, 0, True)

        def group(b, last):
            for q in range(GROUP):
                e = b * GROUP + q
                if not (last and q >= 2):
                    gather((q + 2) % GROUP, e + 3, e + 1, False)
                pool.wait_ge(ye_act, e + 2)
                pool.wait_ge(ye_dve, e * GS + 2 * GS)
                pool.wait_ge(scattered, e * 16 + SCAT0)
                pool.sem_inc(pool_turn, 1)
                nc.gpsimd.indirect_dma_start(
                    out=accum, out_offset=bass.IndirectOffsetOnAxis(ap=idx_of[q][:, :1], axis=0),
                    in_=ys[:, q % 2, :], in_offset=None, compute_op=ALU.add).then_inc(scattered, 16)

        with pool.Fori(0, NE // GROUP - 1) as b:
            group(b, False)
        group(NE // GROUP - 1, True)

        for i in range(NT):
            n = 3 * NT + i
            pool.wait_ge(fss_ok, i + 1)
            nc.gpsimd.tensor_scalar(ms[:, n:n + 1], ss[:, n:n + 1], 1.0 / D, EPS, ALU.mult, ALU.add).then_inc(pool_fin, 1)
            pool.wait_ge(pool_fin, i + 1)
            nc.gpsimd.tensor_tensor(rs[:, n:n + 1], ms[:, n:n + 1], nhalf[:], ALU.pow).then_inc(frs_ok, 1)

    @block.scalar
    def _(act):
        step = stepper(act, act_step)
        act.dma_start(ident[:], a["ident"]).then_inc(ident_in, 16)
        for r, name, n in ((PG + 2 * KC, "g_pre_ffn", KC), (PG + 3 * KC, "g_post_ffn", KC),
                           (PCB, "conv_b", CC), (PLG, "conv_ln_g", CC), (PLB, "conv_ln_b", CC)):
            act.dma_start(prow[r:r + n, :], a[name][0].rearrange("(c p) -> c p", p=P)).then_inc(params_in, 16)
        act.dma_start(sel[:], a["sel"]).then_inc(small_in, 16)
        act.dma_start(pick2[:], a["pick2"].rearrange("a g p -> a g p")).then_inc(small_in, 16)
        act.dma_start(cw_rows[0:TAPS * CC, :], a["conv_w"][0].rearrange("t (c p) -> (t c) p", p=P)).then_inc(cw_in, 16)
        act.dma_start(kcache[:], a["cache_k"][0, 0].rearrange("s h d -> s (h d)")).then_inc(kc_in, 16)
        act.dma_start(v[:, LT, :], a["cache_v"][0, 0].rearrange("s h d -> s (h d)")).then_inc(vc_in, 16)
        act.dma_start(cos, a["cos"].rearrange("(t p) d -> p t d", p=P)).then_inc(tab_in, 16)
        act.dma_start(sin, a["sin"].rearrange("(t p) d -> p t d", p=P)).then_inc(tab_in, 16)
        for h in range(NH + NKV):
            src = a["q_norm" if h < NH else "k_norm"]
            act.dma_start(gain[:, h * HD:(h + 1) * HD], src[0:1, :].to_broadcast([P, HD])).then_inc(tab_in, 16)
        act.dma_start(wr[:], a["w_router"][0].rearrange("(k p) e -> p k e", p=P)).then_inc(wr_in, 16)

        act.wait_ge(pcols, 1)
        nc.scalar.activation(cond_t[:], pcol[:, PCND:PROWS], ACT.Tanh, scale=0.5).then_inc(cond_tanh, 1)

        for i in range(NT):
            act.wait_ge(x_in[i], 16)
            step(nc.scalar.activation(xjunk, x[:, i, :], ACT.Square, accum_out=ss[:, i:i + 1]))
            act.sem_inc(ss_ok, 1)

        def mod_rows(m, bank, dst):
            act.wait_ge(mod_mm, m + 1)
            if m % 4 >= 2:
                act.wait_ge(modrow_mm, m - 1)
            nc.scalar.activation(dst[:, m % 2, :], ps[:, bank, :], ACT.Copy).then_inc(modrow_ok, 1)

        for m in range(4):
            mod_rows(m, 2 + m % 2, modrow_a)

        act.wait_ge(mod_ok, 1)
        act.wait_ge(scattered, SCAT0)
        for c in range(0, KC, 2):
            act.wait_ge(xT_mm, c + 1)
            nc.scalar.activation(big[:, c, 0:NLAT], ps[:, 4 + c % 4, :], ACT.Identity,
                                 scale=a1[:, c, 0:1], bias=mod[:, c, 0:1]).then_inc(hT_act, 1)
        act.wait_ge(xT_mm, KC + 1)
        for c in range(4):
            nc.scalar.activation(big[:, c, NLAT:NTOK], ps[:, 0, c * P:(c + 1) * P], ACT.Identity,
                                 scale=a1[:, c, 1:2], bias=mod[:, c, 1:2]).then_inc(hT_act, 1)

        for c in range(CC):
            act.wait_ge(glu_mm, c + 1)
            nc.scalar.activation(u[:, c, PAD:PAD + NLAT], ps[:, 4 + c, :], ACT.Tanh, scale=0.5).then_inc(gt_ok, 1)
            nc.scalar.activation(u[:, c, 2 * PAD + NLAT:CU - PAD], ps[:, c, 0:P], ACT.Tanh, scale=0.5).then_inc(gt_ok, 1)

        act.wait_ge(glu_ok, 2 * CC)
        act.wait_ge(pads, 1)
        taps = [0]
        c3 = CC - 1

        def products(n):
            for k in range(taps[0], min(TAPS, taps[0] + n)):
                if k == 0:
                    nc.scalar.activation(y[:, c3, :], u[:, c3, 0:CY], ACT.Identity, scale=cw[:, 0, c3:c3 + 1],
                                         bias=pcol[:, PCB + c3:PCB + c3 + 1]).then_inc(prod_ok, 1)
                else:
                    if k > PRODS:
                        act.wait_ge(add_ok, k - PRODS)
                    nc.scalar.activation(taps_out[:, k % PRODS, :], u[:, c3, k:k + CY], ACT.Copy,
                                         scale=cw[:, k, c3:c3 + 1]).then_inc(prod_ok, 1)
            taps[0] = min(TAPS, taps[0] + n)

        def copies(t):
            i = TILES[t]
            act.wait_ge(qkv_mm, t + 1)
            if t >= 2:
                act.wait_ge(rope_ok, t - 1)
                act.wait_ge(qkT_mm, 2 * (t - 1))
            if t == 2:
                act.wait_ge(new_k_done, 16)
            nc.scalar.activation(qk[:, t % 2, 0:AW].rearrange("p (j g d) -> p g j d", g=2, d=HD),
                                 ps[:, 4 + t % 2, :].rearrange("p (g j d) -> p g j d", g=2, d=HD), ACT.Copy).then_inc(qkv_cp, 1)
            nc.scalar.activation(qk[:, t % 2, AW:NTOK], ps[:, 6 + t % 2, 0:KVW], ACT.Copy).then_inc(qkv_cp, 1)
            nc.scalar.activation(v[:, i if i < LT else NT, :], ps[:, 6 + t % 2, KVW:2 * KVW], ACT.Copy).then_inc(qkv_cp, 1)
            act.wait_ge(qkv_cp, 3 * t + 2)
            if t >= 1:
                act.wait_ge(qk_ss, t)
            nc.scalar.activation(qk2, qk[:, t % 2, :], ACT.Square).then_inc(qk_sq, 1)

        def transposed(t):
            i = TILES[t]
            act.wait_ge(qkT_mm, 2 * (t + 1))
            nc.scalar.activation(qT[:, :, tok(i)], ps[:, t % 2, :].rearrange("p (j n) -> p j n", n=P), ACT.Copy).then_inc(qkT_cp, 1)
            at = NTOK if i == LT else i * P
            nc.scalar.activation(kT[:, at:at + P], ps[:, 2, 0:P], ACT.Copy).then_inc(qkT_cp, 1)

        for t in range(NT):
            products(4)
            copies(t)
            if t == 1:
                act.wait_ge(rope_ok, 1)
                act.dma_start(new_k[0, 0].rearrange("s h d -> s (h d)"), qk[:, 0, AW:NTOK]).then_inc(new_k_done, 16)
            products(2)
            if t >= 1:
                transposed(t - 1)
        act.wait_ge(qkv_cp, 3)
        act.dma_start(new_v[0, 0].rearrange("s h d -> s (h d)"), v[:, NT, :]).then_inc(kv_done, 16)
        products(TAPS)
        for m in range(4, 8):
            mod_rows(m, 6 + m % 2, modrow_a)
            if m == 4:
                transposed(NT - 1)

        def g_out(base):
            for n in range(4):
                act.wait_ge(g_mm, base + n + 1)
                nc.scalar.activation(gtile[:, n // 2, (n % 2) * 512:(n % 2 + 1) * 512], ps[:, (4 if base == 0 else 2) + n, :],
                                     ACT.Copy).then_inc(g_ok, 1)
        act.wait_ge(modrow_mm, 8)
        g_out(0)

        def exp(n):
            t, i, h = heads[n]
            w = P if i == LT else NTOK
            act.wait_ge(max_ok, n + 1)
            if n < 2:
                act.wait_ge(conv_pool, 1)
            else:
                act.wait_ge(t_mm, n - 1)
            s = s_buf[n]
            step(nc.scalar.activation(prob[:, n % 2, 0:w], ps[:, s:s + 2, :].rearrange("p b n -> p (b n)")[:, 0:w],
                                      ACT.Exp, bias=nmax[:, n:n + 1], accum_out=rsum[:, n:n + 1]))
            act.sem_inc(exp_ok, 1)

        def first_four(n):
            w = P if heads[n][1] == LT else 512
            act.wait_ge(t_mm, n + 1)
            if n >= 4:
                act.wait_ge(pv_mm, (n - 4) // 2 + 1)
            elif n == 0:
                act.wait_ge(qkT_mm, 2 * NT)
            nc.scalar.activation(probT[:, n % 4, 0:w], ps[:, 4, 0:w], ACT.Copy).then_inc(pt_act, 1)

        def sums_out(t):
            act.wait_ge(rinvT_mm, t + 1)
            if t >= 1:
                act.wait_ge(o_norm, t)
            nc.scalar.activation(rinvT, ps[:, 7, :], ACT.Copy).then_inc(rinvT_ok, 1)

        for n in range(NU + 4):
            if n < NU and n in BETWEEN:
                what = BETWEEN[n]
                if what.startswith("mod"):
                    if what == "mod8":
                        act.wait_ge(rope_ok, NT)
                    mod_rows(int(what[3:]), s_buf[what], modrow_b)
            if n == LN_SQ_AT:
                act.wait_ge(ln_cen, 2)
                nc.scalar.activation(ln_sq[:, :, 0:NLAT], y[:, :, 0:NLAT], ACT.Square).then_inc(ln_sq_ok, 1)
                nc.scalar.activation(ln_sq[:, :, NLAT:NTOK], y[:, :, CTX_Y:CY], ACT.Square).then_inc(ln_sq_ok, 1)
            c = n - SILU_AT
            if 0 <= c < CC:
                act.wait_ge(ln_yn, 2)
                step(nc.scalar.activation(y[:, c, :], y[:, c, :], ACT.Identity, scale=lnc[:, 0, c:c + 1], bias=lnc[:, 1, c:c + 1]))
                nc.scalar.activation(ln_tanh[:, c, :], y[:, c, :], ACT.Tanh).then_inc(ln_th, 1)
            if n < NU:
                exp(n)
            if 1 <= n <= NU:
                first_four(n - 1)
            if n >= NH + 1 and (n - 1) % NH == 0:
                sums_out((n - 1) // NH - 1)

        def squares(t):
            for half in range(2):
                act.wait_ge(out_mm, 2 * t + half + 1)
                if half == 0 and t >= 2:
                    act.wait_ge(table_in[t % 2], 16 * (t // 2))
                elif half == 0:
                    act.wait_ge(modrow_mm, 12)
                n = NT + t
                dst = (ss, ss2)[half][:, n:n + 1]
                step(nc.scalar.activation(rows[:, t % 2, half * HALF:(half + 1) * HALF], ps[:, 2 * (t % 2) + half, :],
                                          ACT.Square, scale=D ** -0.5, accum_out=dst))
                act.sem_inc(oss_ok, 1)

        def epilogue(t):
            i = TILES[t]
            n = 2 * NT + t
            for half in range(2):
                act.wait_ge(x1_ok, 2 * t + half + 1)
                dst = (ss, ss2)[half][:, n:n + 1]
                step(nc.scalar.activation(rows[:, t % 2, half * HALF:(half + 1) * HALF], x[:, i, half * HALF:(half + 1) * HALF],
                                          ACT.Square, scale=D ** -0.5, accum_out=dst))
                act.sem_inc(xss_ok, 1)
            act.wait_ge(x2T_mm, 2 * t + 1)
            nc.scalar.activation(big[:, 0:4, tok(i)], ps[:, 4, :].rearrange("p (c n) -> p c n", n=P), ACT.Copy).then_inc(h2_act, 1)
            act.wait_ge(xrs_ok, t + 1)
            nc.scalar.activation(rows[:, t % 2, :], x[:, i, :], ACT.Copy, scale=rs[:, n:n + 1]).then_inc(xn2_ok, 1)
            act.wait_ge(xn2_ok, t + 1)
            act.dma_start(table[tok(i), :], rows[:, t % 2, :]).then_inc(table_in[t % 2], 16)
            act.wait_ge(rt_mx, t + 1)
            step(nc.scalar.activation(rt_exp[:, t % 2, :], rlog[:, t % 2, :], ACT.Exp, bias=rt_max[:, t:t + 1],
                                      accum_out=rt_sum[:, t:t + 1]))
            act.sem_inc(rt_ex, 1)

        for t in range(NT):
            squares(t)
            epilogue(t)
        g_out(4)

        nc_tanh = lambda: nc.scalar.activation(tanh_g, two(0), ACT.Tanh, scale=0.5).then_inc(th_ok, 1)
        act.sem_inc(ye_act, 1)
        act.wait_ge(units_used, RING + 2)
        nc_tanh()

        def group(b, last):
            for q in range(GROUP):
                e = b * GROUP + q
                end = last and q == GROUP - 1
                act.wait_ge(hidT_mm, e + 1)
                hp = ps[:, 6, :].rearrange("p (b n) -> p b n", n=P)
                nc.scalar.activation(hid[:, 0:4, :], hp[:, :, 0:CSP], ACT.Copy).then_inc(hidc_act, 1)
                nc.scalar.activation(hid[:, 6:8, 0:2 * QR].rearrange("p h (r t) -> p r h t", r=2),
                                     hp[:, :, CSP:P].rearrange("p (r h) t -> p r h t", r=2), ACT.Copy).then_inc(hidc_act, 1)
                if not end:
                    act.wait_ge(units_used, e * UNITS + (RING + 6))
                    act.wait_ge(silu_ok, e + 1)
                    nc_tanh()
                act.wait_ge(units_used, e * UNITS + (RING + (6 if end else 8)))
                act.wait_ge(scattered, e * 16 + (SCAT0 - 16))
                nc.scalar.activation(ys[:, q % 2, 0:GS * QN], two(4)[0:CS, :], ACT.Copy).then_inc(ye_act, 1)

        with act.Fori(0, NE // GROUP - 1) as b:
            group(b, False)
        group(NE // GROUP - 1, True)

        for i in range(NT):
            act.wait_ge(fin_in[i], 16)
            n = 3 * NT + i
            if i >= 1:
                act.wait_ge(act_fin, i)
            nc.scalar.activation(rows[:, 0, :], fin[:, i, :], ACT.Square, accum_out=ss[:, n:n + 1]).then_inc(act_fin, 1)
            act.wait_ge(act_fin, i + 1)
            act.sem_inc(fss_ok, 1)
        act.wait_ge(kv_done, 16)
        act.wait_ge(new_k_done, 16)

    @block.tensor
    def _(pe):
        def used(ins, unit):
            ins.then_inc(units_used if unit >= NPRE - PRE else pre_used, 1)

        def wait_unit(n):
            pe.wait_ge(landed[n % PRE], 16 * (n // PRE + 1))

        def T(out, in_, k=P):
            return nc.tensor.transpose(out, in_, ident[0:k, 0:k])

        pe.wait_ge(ident_in, 16)
        pe.wait_ge(params_in, 16 * 10)
        T(ps[:, 0, 0:PROWS], prow[0:PROWS, :], PROWS).then_inc(pT, 1)
        pe.wait_ge(cw_in, 16)
        T(ps[:, 1, 0:TAPS * CC], cw_rows[0:TAPS * CC, :], TAPS * CC).then_inc(pT, 1)
        pe.wait_ge(kc_in, 16)
        T(ps[:, 3, 0:P], kcache[:]).then_inc(pT, 1)

        def modulate(n, bank):
            unit = n if n < 4 else U_MOD + n - 4
            wait_unit(unit)
            w = slot(unit % PRE)
            for k in range(KC):
                q = 32 * (k % 4)
                ins = nc.tensor.matmul(ps[q:q + 32, bank, :], cond[:, k, :], w[:, k, :], start=(k < 4), stop=(k >= 4))
            ins.then_inc(mod_mm, 1)
            pe.wait_ge(mod_mm, n + 1)
            pe.sem_inc(units_used if unit >= NPRE - PRE else pre_used, 1)

        def mod_columns(n, bank, at, src):
            pe.wait_ge(modrow_ok, n + 1)
            for m in range(4):
                ins = nc.tensor.matmul(ps[:, bank, at + 2 * m:at + 2 * m + 2], src[:, n % 2, m * P:(m + 1) * P], sel[:],
                                       start=True, stop=True)
            ins.then_inc(modrow_mm, 1)

        def latent_xT(c):
            for i in range(LT):
                ins = T(ps[:, 4 + c % 4, tok(i)], xn[:, i, c * P:(c + 1) * P])
            ins.then_inc(xT_mm, 1)

        pe.wait_ge(cond_ok, 1)
        modulate(0, 2)
        pe.wait_ge(pcols, 3)
        modulate(1, 3)
        pe.wait_ge(small_in, 32)
        mod_columns(0, 1, 0, modrow_a)
        pe.wait_ge(xn_ok, LT)
        for c in range(4):
            latent_xT(c)
        modulate(2, 2)
        mod_columns(1, 1, 8, modrow_a)
        modulate(3, 3)
        mod_columns(2, 1, 16, modrow_a)
        mod_columns(3, 1, 24, modrow_a)
        for c in range(4, KC):
            pe.wait_ge(hT_act if c % 2 == 0 else hT_dve, (c - 4) // 2 + 1)
            latent_xT(c)
        pe.wait_ge(xn_ok, NT)
        for c in range(KC):
            ins = T(ps[:, 2 * (c // 4), (c % 4) * P:(c % 4 + 1) * P], xn[:, LT, c * P:(c + 1) * P])
        ins.then_inc(xT_mm, 1)

        pe.wait_ge(hT_act, 8)
        pe.wait_ge(hT_dve, 8)
        for m in range(2 * CC):
            unit = U_GT + m // CC
            wait_unit(unit)
            if m >= CC:
                pe.wait_ge(gt_ok, 2 * (m - CC + 1))
            w = slot(unit % PRE)
            for bank, cols_ in ((4 + m % 4, slice(0, NLAT)), (m % 4, slice(NLAT, NTOK))):
                for k in range(KC):
                    ins = nc.tensor.matmul(ps[:, bank, 0:cols_.stop - cols_.start], w[:, k, (m % 4) * P:(m % 4 + 1) * P],
                                           big[:, k, cols_], start=(k == 0), stop=(k == KC - 1))
            ins.then_inc(glu_mm, 1)
            if m % CC == CC - 1:
                pe.wait_ge(glu_mm, m + 1)
                pe.sem_inc(pre_used, 1)

        def project(t):
            i = TILES[t]
            wait_unit(U_KV)
            wait_unit(U_Q)
            if t >= 2:
                pe.wait_ge(qkv_cp, 3 * (t - 1))
            else:
                pe.wait_ge(glu_ok, 2 * CC)
            for k in range(KC):
                ins = nc.tensor.matmul(ps[:, 6 + t % 2, 0:2 * KVW], big[:, k, tok(i)], slot(U_KV % PRE, 2 * KVW)[:, k, :],
                                       start=(k == 0), stop=(k == KC - 1))
            if t == NT - 1:
                used(ins, U_KV)
            for k in range(KC):
                ins = nc.tensor.matmul(ps[:, 4 + t % 2, :], big[:, k, tok(i)], slot(U_Q % PRE)[:, k, :],
                                       start=(k == 0), stop=(k == KC - 1))
            ins.then_inc(qkv_mm, 1)
            if t == NT - 1:
                pe.wait_ge(qkv_mm, NT)
                pe.sem_inc(pre_used, 1)

        def transpose_qk(t):
            pe.wait_ge(rope_ok, t + 1)
            if t >= 1:
                pe.wait_ge(qkT_cp, 2 * t)
            for j in range(4):
                ins = T(ps[:, t % 2, j * P:(j + 1) * P],
                        qk[:, t % 2, j * P:(j + 1) * P])
            ins.then_inc(qkT_mm, 1)
            T(ps[:, 2, 0:P], qk[:, t % 2, AW:NTOK]).then_inc(qkT_mm, 1)

        for t in range(NT):
            project(t)
            if t >= 1:
                transpose_qk(t - 1)

        pe.wait_ge(qkv_cp, 3 * NT)
        for m in range(4, 8):
            modulate(m, 6 + m % 2)
            if m > 4:
                mod_columns(m - 1, 3, 8 * (m - 5), modrow_a)
            if m == 4:
                transpose_qk(NT - 1)
        mod_columns(7, 3, 24, modrow_a)

        def g_tiles(layer, bank, done):
            for n in range(4):
                g, half = n // 2, n % 2
                for c in range(4):
                    col = gcol[:, layer, 4 * half + c, g:g + 1]
                    ins = T(ps[:, bank + n, c * P:(c + 1) * P], col.to_broadcast([P, P]))
                ins.then_inc(g_mm, 1)

        pe.wait_ge(mod_ok, 2)
        g_tiles(0, 4, g_mm)
        pe.wait_ge(wr_in, 16)
        for k in range(KC):
            ins = nc.tensor.matmul(ps[0:2, 3, 64:64 + NE], mod[:, 24 + k, :], wr[:, k, :], start=(k == 0), stop=(k == KC - 1))
        ins.then_inc(shr_mm, 1)
        pe.wait_ge(shr_ok, 1)
        for g in range(2):
            ins = nc.tensor.matmul(ps[:, 3, 128 + g * NE:128 + (g + 1) * NE], pick2[:, g, :], sh_rows[:], start=True, stop=True)
        ins.then_inc(rb_mm, 1)

        def free(st):
            k = stages.index(st)
            prev = stages[k - 2] if k >= 2 else None
            if prev is None:
                pe.wait_ge(qkT_cp, 2 * NT)
                pe.wait_ge(rb_ok, 1)
            elif prev == "mean":
                pe.wait_ge(ln_cen, 2)
            elif prev == "var":
                pe.wait_ge(ln_ms, 1)
            elif prev == "rstd":
                pe.wait_ge(ln_yn, 2)
            elif isinstance(prev, str):
                pe.wait_ge(mod_raw, int(prev[3:]) - 7)
            else:
                pe.wait_ge(exp_ok, prev + 1)

        def scores(n):
            t, i, h = heads[n]
            free(n)
            s = s_buf[n]
            p0 = HD * (h // 4)
            q = qT[p0:p0 + HD, h % 4, tok(i)]
            if i == LT:
                nc.tensor.matmul(ps[:, s, 0:P], q, kT[p0:p0 + HD, NTOK:NTOK + P], start=True, stop=True).then_inc(s_mm, 1)
            else:
                nc.tensor.matmul(ps[:, s, :], q, kT[p0:p0 + HD, 0:512], start=True, stop=True)
                nc.tensor.matmul(ps[:, s + 1, 0:P], q, kT[p0:p0 + HD, 512:640], start=True, stop=True).then_inc(s_mm, 1)

        def between(what):
            free(what)
            s = s_buf[what]
            if what.startswith("mod"):
                modulate(int(what[3:]), s)
            elif what == "mean":
                pe.wait_ge(conv_dve, 1)
                pe.wait_ge(conv_pool, 1)
                for bank, n, lo in ((s, NLAT, 0), (s + 1, NCTX, CTX_Y)):
                    for c in range(CC):
                        ins = nc.tensor.matmul(ps[:, bank, 0:n], ones[:], y[:, c, lo:lo + n], start=(c == 0), stop=(c == CC - 1))
                ins.then_inc(ln_mm, 1)
            elif what == "var":
                pe.wait_ge(ln_sq_ok, 2)
                for i in range(NT):
                    for c in range(CC):
                        ins = nc.tensor.matmul(ps[:, s, i:i + 1], ln_sq[:, c, tok(i)], ones[:, 0:1], start=(c == 0), stop=(c == CC - 1))
                ins.then_inc(ln_mm, 1)
            else:
                pe.wait_ge(ln_rs_ok, 1)
                for i in range(NT):
                    ins = T(ps[:, s + i // 4, (i % 4) * P:(i % 4 + 1) * P], ln_rs[:, i:i + 1].to_broadcast([P, P]))
                ins.then_inc(ln_mm, 1)

        def after(what):
            if what.startswith("mod"):
                mod_columns(int(what[3:]), s_buf[what] + 1, 0, modrow_b)

        def transpose_p(n):
            pe.wait_ge(exp_ok, n + 1)
            if n == 0:
                pe.wait_ge(g_ok, 4)
            else:
                pe.wait_ge(pt_act, n)
                if n_lat(n):
                    pe.wait_ge(pt_dve, n_lat(n))
            if heads[n][1] == LT:
                T(ps[:, 4, 0:P], prob[:, n % 2, 0:P]).then_inc(t_mm, 1)
                return
            for kc in range(NT):
                ins = T(ps[:, 4 + kc // 4, (kc % 4) * P:(kc % 4 + 1) * P], prob[:, n % 2, kc * P:(kc + 1) * P])
            ins.then_inc(t_mm, 1)

        def values(pair):
            n = 2 * pair
            t, i, h = heads[n]
            pe.wait_ge(pt_act, n + 2)
            if n_lat(n + 2):
                pe.wait_ge(pt_dve, n_lat(n + 2))
            if h == 0 and t >= 1:
                pe.wait_ge(o_norm, t)
            if n == 0:
                pe.wait_ge(vc_in, 16)
            chunks = [(0, NT)] if i == LT else [(kc, kc) for kc in range(NT)]
            for m, (kc, vt) in enumerate(chunks):
                for j in range(2):
                    ins = nc.tensor.matmul(ps[j * HD:(j + 1) * HD, 6, (h // 2) * P:(h // 2 + 1) * P],
                                           v[:, vt, (h // 4) * HD:(h // 4 + 1) * HD],
                                           probT[:, (n + j) % 4, kc * P:(kc + 1) * P], start=(m == 0), stop=(m == len(chunks) - 1))
            ins.then_inc(pv_mm, 1)

        def transpose_sums(t):
            pe.wait_ge(rep_ok, t + 1)
            if t >= 1:
                pe.wait_ge(rinvT_ok, t)
            for j in range(4):
                ins = T(ps[:, 7, j * P:(j + 1) * P], rinv_rep[:, j * P:(j + 1) * P])
            ins.then_inc(rinvT_mm, 1)

        scores(0)
        for n in range(NU + 3):
            if n + 1 in BETWEEN:
                between(BETWEEN[n + 1])
            if n + 1 < NU:
                scores(n + 1)
            if n + 1 in BETWEEN:
                after(BETWEEN[n + 1])
            if n < NU:
                transpose_p(n)
            if n % 2 == 0 and 2 <= n <= NU:
                values(n // 2 - 1)
            if n >= NH and n % NH == 0:
                transpose_sums(n // NH - 1)

        def out_project(t):
            i = TILES[t]
            s = 2 * (t % 2)
            if t == 0:
                pe.wait_ge(exp_ok, NU)
                pe.wait_ge(o_norm, NT)
            for n in range(2):
                if t >= 2:
                    pe.wait_ge(x1_ok, 2 * (t - 2) + n + 1)
                unit = U_WO + n
                wait_unit(unit)
                w = slot(unit % PRE)
                for k in range(KC):
                    if t == 0 and n == 0 and k == 4:
                        pe.wait_ge(conv_ok, 1)
                    lhs = attnT[:, k, tok(i)] if k < 4 else y[:, k - 4, ycols(i)]
                    ins = nc.tensor.matmul(ps[:, s + n, :], lhs, w[:, k, :], start=(k == 0), stop=(k == KC - 1))
                ins.then_inc(out_mm, 1)
                if t == NT - 1:
                    pe.wait_ge(out_mm, 2 * t + n + 1)
                    pe.sem_inc(units_used, 1 + n * (RING - PRE))

        def route(t):
            i = TILES[t]
            g = 1 if i == LT else 0
            for half in range(2):
                pe.wait_ge(x1_ok, 2 * t + half + 1)
                if t >= 1:
                    pe.wait_ge(h2_act if half == 0 else h2_dve, t)
                elif half == 0:
                    pe.wait_ge(pt_act, NU)
                    pe.wait_ge(pt_dve, NU - NH)
                for c in range(4):
                    ins = T(ps[:, 4 + half, c * P:(c + 1) * P], x[:, i, half * HALF + c * P:half * HALF + (c + 1) * P])
                ins.then_inc(x2T_mm, 1)
            if t == 0:
                pe.wait_ge(wra_ok, 1)
            else:
                pe.wait_ge(rt_mx, t)
            for k in range(KC):
                if k == 0:
                    pe.wait_ge(h2_act, t + 1)
                if k == 4:
                    pe.wait_ge(h2_dve, t + 1)
                ins = nc.tensor.matmul(ps[:, 6, 0:NE], big[:, k, tok(i)], wra[:, g, k, :], start=(k == 0), stop=(k == KC - 1))
            ins.then_inc(rt_mm, 1)

        def transpose_aff(t):
            pe.wait_ge(aff_ok, t + 1)
            if t >= 1:
                pe.wait_ge(affT_ok, t)
            else:
                pe.wait_ge(rinvT_ok, NT)
            T(ps[0:NE, 7, 0:P], aff[:, t % 2, :]).then_inc(affT_mm, 1)

        for t in range(NT):
            out_project(t)
            if t >= 1:
                route(t - 1)
                if t >= 2:
                    transpose_aff(t - 2)
        route(NT - 1)
        transpose_aff(NT - 2)
        transpose_aff(NT - 1)

        pe.wait_ge(h2_act, NT)
        pe.wait_ge(h2_dve, NT)
        g_tiles(1, 2, g_mm)

        pe.wait_ge(top_ok, 1)
        T(ps[0:CS, 7, 0:NE], topf[:], NE).then_inc(topT_mm, 1)
        pe.wait_ge(top_ok, 2)
        for r in range(GS):
            ins = T(ps[:, 6, r * NE:(r + 1) * NE], gq[:, r, :], NE)
        ins.then_inc(topT_mm, 1)

        def product(x_, w, half, bank):
            out = two(bank)
            for k in range(4):
                c = 4 * half + k
                for qd, g, lo, n in ((3, 0, 0, QN), (0, 0, 0, 2 * QN), (1, 1, 0, 2 * QN), (3, 1, QN, QN), (2, 2, 0, 2 * QN),
                                     (0, 0, 2 * QN, QN), (3, 2, 2 * QN, QN), (1, 1, 2 * QN, QN), (2, 2, 2 * QN, QN)):
                    src = w[:, k, GS * QN:D] if qd == GS else w[:, k, lo:lo + n]
                    ins = nc.tensor.matmul(out[qd * QR:(qd + 1) * QR, lo:lo + n], x_[:, c, g * QR:(g + 1) * QR], src,
                                           start=(c == 0 and lo % HALF == 0), stop=(c == KC - 1 and not (qd == GS and lo == 0)))
            ins.then_inc(units_used, 1)

        def transpose_x(q, value):
            pe.wait_ge(gathered[q % 2], value)
            for c in range(KC):
                ins = T(ps[:, 6 + c // 4, (c % 4) * CS:(c % 4 + 1) * CS], xg[0:CS, q % 2, c * P:(c + 1) * P], CS)
            ins.then_inc(xgT_mm, 1)

        pe.wait_ge(g_ok, 8)
        pe.wait_ge(slots_ok, 1)
        transpose_x(0, 16)
        pe.wait_ge(xTe_ok, 2)
        for half in range(2):
            pe.wait_ge(landed[half], 16 * (NPRE // PRE + 1))
            product(xT[0], slot(half, D), half, 0)

        def group(b, last):
            for q in range(GROUP):
                e = b * GROUP + q

                def unit(n):
                    j = 2 + UNITS * q + n
                    uses = NPRE // PRE if j % RING < PRE else 0
                    pe.wait_ge(landed[j % RING], b * (16 * GROUP * UNITS // RING) + 16 * (uses + j // RING + 1))
                    return slot(j % RING, D)

                end = last and q == GROUP - 1
                product(xT[q % 2], unit(0), 0, 2)
                if not end:
                    transpose_x((q + 1) % GROUP, b * (16 * GROUP // 2) + 16 * ((q + 1) // 2 + 1))
                product(xT[q % 2], unit(1), 1, 2)
                if not end:
                    pe.wait_ge(xTe_ok, e * 2 + 4)
                    pe.wait_ge(silu_ok, e + 1)
                    product(xT[(q + 1) % 2], unit(2), 0, 0)
                pe.wait_ge(hid_ok, e * GS + GS)
                for m in range(2 * GS):
                    ins = T(ps[:, 6 + m // 4, (m % 4) * P:(m % 4 + 1) * P], act_g[:, m * P:(m + 1) * P])
                ins.then_inc(hidT_mm, 1)
                if not end:
                    product(xT[(q + 1) % 2], unit(3), 1, 0)
                pe.wait_ge(hidc_act, e * 2 + 2)
                pe.wait_ge(hidc_dve, e * 2 + 2)
                pe.wait_ge(ye_act, e + 1)
                pe.wait_ge(ye_dve, e * GS + GS)
                for half in range(2):
                    product(hid, unit((2 if end else 4) + half), half, 4)

        with pe.Fori(0, NE // GROUP - 1) as b:
            group(b, False)
        group(NE // GROUP - 1, True)

    @block.vector
    def _(dve):
        V = nc.vector
        step = stepper(dve, dve_step)
        dve.wait_ge(pT, 1)
        V.tensor_copy(pcol[:, 0:PROWS], ps[:, 0, 0:PROWS]).then_inc(pcols, 1)
        dve.wait_ge(pT, 2)
        V.tensor_scalar(cw[:].rearrange("p t c -> p (t c)"), ps[:, 1, 0:TAPS * CC], 0.5, None, ALU.mult).then_inc(pcols, 1)
        dve.wait_ge(pT, 3)
        V.tensor_copy(kT[:, NLAT:NTOK], ps[:, 3, 0:P]).then_inc(pcols, 1)
        dve.wait_ge(pcols, 3)
        step(V.tensor_scalar(lnc[:, 0, :], pcol[:, PLG:PLG + CC], 0.5, None, ALU.mult))
        step(V.tensor_scalar(lnc[:, 1, :], pcol[:, PLB:PLB + CC], 0.5, None, ALU.mult))
        dve.sem_inc(pcols, 1)
        dve.wait_ge(cond_tanh, 1)
        step(V.scalar_tensor_tensor(cond_s[:], cond_t[:], 1.0, pcol[:, PCND:PROWS], ALU.add, ALU.mult))
        dve.wait_ge(consts, 2)
        V.tensor_scalar(cond[:, :, 0:2].rearrange("p k g -> p g k"), cond_s[:].rearrange("p (g k) -> p g k", g=2), 0.5, None,
                        ALU.mult).then_inc(cond_ok, 1)

        for i in range(NT):
            dve.wait_ge(rs_ok, i + 1)
            V.tensor_scalar(xn[:, i, :], x[:, i, :], rs[:, i:i + 1], None, ALU.mult).then_inc(xn_ok, 1)

        def both(ap):
            return ap.unsqueeze(2).to_broadcast([P, ap.shape[1], 2])
        dve.wait_ge(modrow_mm, 4)
        step(V.tensor_tensor(mod[:, 0:16, :], ps[:, 1, 0:32].rearrange("p (c n) -> p c n", n=2), both(pcol[:, 0:16]), ALU.add))
        step(V.scalar_tensor_tensor(a1[:], mod[:, 8:16, :], 1.0, both(pcol[:, PG:PG + KC]), ALU.add, ALU.mult))
        dve.sem_inc(mod_ok, 1)

        dve.wait_ge(scattered, SCAT0)
        for c in range(1, KC, 2):
            dve.wait_ge(xT_mm, c + 1)
            V.tensor_scalar(big[:, c, 0:NLAT], ps[:, 4 + c % 4, :], a1[:, c, 0:1], mod[:, c, 0:1],
                            ALU.mult, ALU.add).then_inc(hT_dve, 1)
        dve.wait_ge(xT_mm, KC + 1)
        for c in range(4, KC):
            V.tensor_scalar(big[:, c, NLAT:NTOK], ps[:, 2, (c - 4) * P:(c - 3) * P], a1[:, c, 1:2], mod[:, c, 1:2],
                            ALU.mult, ALU.add).then_inc(hT_dve, 1)

        dve.wait_ge(tab_in, 16 * 12)
        step(V.tensor_scalar(gain[:, 0:AW], gain[:, 0:AW], HD ** -0.5, None, ALU.mult))

        for c in range(CC):
            dve.wait_ge(glu_mm, CC + c + 1)
            dve.wait_ge(gt_ok, 2 * (c + 1))
            for lo, hi, bank in ((PAD, PAD + NLAT, 4 + c), (2 * PAD + NLAT, CU - PAD, c)):
                V.scalar_tensor_tensor(u[:, c, lo:hi], u[:, c, lo:hi], 1.0, ps[:, bank, 0:hi - lo],
                                       ALU.add, ALU.mult).then_inc(glu_ok, 1)
        dve.wait_ge(glu_ok, 2 * CC)
        dve.wait_ge(pads, 1)

        taps = [0]
        steps0 = 0

        def conv(n):
            for k in range(taps[0], min(TAPS, taps[0] + n)):
                for c in range(CC - 1):
                    if k == 0:
                        V.tensor_scalar(y[:, c, :], u[:, c, 0:CY], cw[:, 0, c:c + 1], pcol[:, PCB + c:PCB + c + 1],
                                        ALU.mult, ALU.add).then_inc(conv_dve_step, 1)
                    else:
                        dve.wait_ge(conv_dve_step, (CC - 1) * (k - 1) + c + 1)
                        V.scalar_tensor_tensor(y[:, c, :], u[:, c, k:k + CY], cw[:, k, c:c + 1], y[:, c, :],
                                               ALU.mult, ALU.add).then_inc(conv_dve_step, 1)
            taps[0] = min(TAPS, taps[0] + n)

        conv(4)

        NHH = NH + NKV
        for t in range(NT):
            i = TILES[t]
            dve.wait_ge(qk_sq, t + 1)
            V.tensor_reduce(hss[:, t % 2, :], qk2.rearrange("p (h d) -> p h d", d=HD), AX.X, ALU.add).then_inc(qk_ss, 1)
            cur = qk[:, t % 2, :]
            step(V.tensor_tensor(cur, cur, gain, ALU.mult))
            conv(3)
            dve.wait_ge(qk_rs, t + 1)
            step(V.tensor_tensor(cur.rearrange("p (h d) -> p h d", d=HD), cur.rearrange("p (h d) -> p h d", d=HD),
                                 hrs[:, t % 2, :].unsqueeze(2).to_broadcast([P, NHH, HD]), ALU.mult))
            pair = cur.rearrange("p (h a s d) -> p s h a d", h=NHH, a=2, s=2)
            part = rope_a.rearrange("p (h a s d) -> p s h a d", h=NHH, a=2, s=2)
            sn = sin[:, i, :].rearrange("p (a s d) -> p s a d", a=2, s=2)
            for s in range(2):
                tab = sn[:, s].unsqueeze(1).to_broadcast([P, NHH, 2, 16])
                V.tensor_tensor(part[:, s], pair[:, 1 - s], tab, ALU.mult).then_inc(rope_half, 1)
            dve.wait_ge(rope_half, 2 * (t + 1))
            step(V.tensor_tensor(cur.rearrange("p (h d) -> p h d", d=HD), cur.rearrange("p (h d) -> p h d", d=HD),
                                 cos[:, i, :].unsqueeze(1).to_broadcast([P, NHH, HD]), ALU.mult))
            V.tensor_tensor(cur, cur, rope_a, ALU.add).then_inc(rope_ok, 1)

        dve.wait_ge(modrow_mm, 8)
        step(V.tensor_tensor(mod[:, 16:32, :], ps[:, 3, 0:32].rearrange("p (c n) -> p c n", n=2), both(pcol[:, 16:32]), ALU.add))
        step(V.tensor_tensor(gcol[:, 0], mod[:, 16:24, :], both(pcol[:, PG + KC:PG + 2 * KC]), ALU.mult))
        dve.sem_inc(mod_ok, 1)
        dve.wait_ge(shr_mm, 1)
        V.tensor_copy(sh_rows[:], ps[0:2, 3, 64:64 + NE]).then_inc(shr_ok, 1)
        dve.wait_ge(rb_mm, 1)
        V.tensor_copy(rbias[:].rearrange("p g e -> p (g e)"), ps[:, 3, 128:128 + 2 * NE]).then_inc(rb_ok, 1)

        def head_max(n):
            w = P if heads[n][1] == LT else NTOK
            dve.wait_ge(s_mm, n + 1)
            s = s_buf[n]
            V.tensor_reduce(nmax[:, n:n + 1], ps[:, s:s + 2, :].rearrange("p b n -> p (b n)")[:, 0:w], AX.X, ALU.max,
                            negate=True).then_inc(max_ok, 1)

        def fifth(n):
            if heads[n][1] == LT:
                return
            dve.wait_ge(t_mm, n + 1)
            dve.wait_ge(pv_mm, (n - 4) // 2 + 1)
            V.tensor_copy(probT[:, n % 4, 512:640], ps[:, 5, 0:P]).then_inc(pt_dve, 1)

        def row_sums(t):
            dve.wait_ge(exp_ok, NH * (t + 1))
            V.reciprocal(rinv[:, t, :], rsum[:, t * NH:(t + 1) * NH]).then_inc(rowsum_ok, 1)

        def normalise(t):
            i = TILES[t]
            dve.wait_ge(pv_mm, 4 * (t + 1))
            dve.wait_ge(rinvT_ok, t + 1)
            V.tensor_tensor(attnT[:, :, tok(i)], ps[:, 6, :].rearrange("p (j n) -> p j n", n=P),
                            rinvT.rearrange("p (j n) -> p j n", n=P), ALU.mult).then_inc(o_norm, 1)

        def between(what):
            s = s_buf[what]
            if what.startswith("mod"):
                m = int(what[3:])
                dve.wait_ge(modrow_mm, m + 1)
                V.tensor_tensor(mod[:, 4 * m:4 * m + 4, :], ps[:, s + 1, 0:8].rearrange("p (c n) -> p c n", n=2),
                                both(pcol[:, 4 * m:4 * m + 4]), ALU.add).then_inc(mod_raw, 1)
            elif what == "mean":
                dve.wait_ge(ln_mm, 1)
                V.tensor_tensor(y[:, :, 0:NLAT], y[:, :, 0:NLAT],
                                ps[:, s, :].unsqueeze(1).to_broadcast([P, CC, NLAT]), ALU.subtract).then_inc(ln_cen, 1)
                V.tensor_tensor(y[:, :, CTX_Y:CY], y[:, :, CTX_Y:CY],
                                ps[:, s + 1, 0:P].unsqueeze(1).to_broadcast([P, CC, NCTX]), ALU.subtract).then_inc(ln_cen, 1)
            elif what == "var":
                dve.wait_ge(ln_mm, 2)
                V.tensor_scalar(ln_m[:], ps[:, s, 0:NT], EPS, None, ALU.add).then_inc(ln_ms, 1)
            else:
                dve.wait_ge(ln_mm, 3)
                V.tensor_tensor(y[:, :, 0:NLAT], y[:, :, 0:NLAT],
                                ps[:, s, :].unsqueeze(1).to_broadcast([P, CC, NLAT]), ALU.mult).then_inc(ln_yn, 1)
                V.tensor_tensor(y[:, :, CTX_Y:CY], y[:, :, CTX_Y:CY],
                                ps[:, s + 1, 0:P].unsqueeze(1).to_broadcast([P, CC, NCTX]), ALU.mult).then_inc(ln_yn, 1)

        head_max(0)
        for n in range(NU + 3):
            if n + 1 in BETWEEN and not BETWEEN[n + 1].startswith("mod"):
                between(BETWEEN[n + 1])
            if n + 1 in CONV_AT:
                conv(1)
            if n + 1 == CONV_AT[-1] + 1:
                conv(TAPS)
                dve.wait_ge(conv_dve_step, (CC - 1) * TAPS)
                dve.sem_inc(conv_dve, 1)
            if n + 1 < NU:
                head_max(n + 1)
            if n + 1 in BETWEEN and BETWEEN[n + 1].startswith("mod"):
                between(BETWEEN[n + 1])
            if n + 1 == GATE_AT:
                dve.wait_ge(ln_th, CC)
                V.scalar_tensor_tensor(y[:], ln_tanh, 1.0, y[:], ALU.add, ALU.mult).then_inc(conv_ok, 1)
            if n < NU:
                fifth(n)
            if n % NH == NH - 1 and n < NU:
                row_sums(n // NH)
            if n > NH and (n - 1) % NH == 0:
                normalise((n - 1) // NH - 1)
            if n == 17:
                dve.wait_ge(mod_raw, 4)
                step(V.scalar_tensor_tensor(a2[:], mod[:, 32:40, :], 1.0, both(pcol[:, PG + 2 * KC:PG + 3 * KC]), ALU.add, ALU.mult))
                step(V.tensor_tensor(gcol[:, 1], mod[:, 40:48, :], both(pcol[:, PG + 3 * KC:PG + 4 * KC]), ALU.mult))
                for g in range(2):
                    step(V.tensor_tensor(wra[:, g], wr[:], a2[:, :, g:g + 1].to_broadcast([P, KC, NE]), ALU.mult))
                dve.sem_inc(wra_ok, 1)

        def epilogue(t):
            i = TILES[t]
            g = 1 if i == LT else 0
            dve.wait_ge(ors_ok, t + 1)
            if t == 0:
                dve.wait_ge(g_ok, 4)
            for half in range(2):
                cs = slice(half * HALF, (half + 1) * HALF)
                step(V.scalar_tensor_tensor(rows[:, t % 2, cs], ps[:, 2 * (t % 2) + half, :], rs[:, NT + t:NT + t + 1],
                                            gtile[:, g, cs], ALU.mult, ALU.mult))
                V.tensor_tensor(x[:, i, cs], x[:, i, cs], rows[:, t % 2, cs], ALU.add).then_inc(x1_ok, 1)

        def h2(t):
            i = TILES[t]
            g = 1 if i == LT else 0
            dve.wait_ge(x2T_mm, 2 * t + 2)
            V.tensor_copy(big[:, 4:8, tok(i)], ps[:, 5, :].rearrange("p (c n) -> p c n", n=P)).then_inc(h2_dve, 1)
            dve.wait_ge(rt_mm, t + 1)
            dve.wait_ge(xrs_ok, t + 1)
            if t >= 2:
                dve.wait_ge(rt_ex, t - 1)
            step(V.scalar_tensor_tensor(rlog[:, t % 2, :], ps[:, 6, 0:NE], rs[:, 2 * NT + t:2 * NT + t + 1], rbias[:, g, :],
                                        ALU.mult, ALU.add))
            V.tensor_reduce(rt_max[:, t:t + 1], rlog[:, t % 2, :], AX.X, ALU.max, negate=True).then_inc(rt_mx, 1)
            dve.wait_ge(rt_ex, t + 1)
            step(V.reciprocal(rt_inv[:, t:t + 1], rt_sum[:, t:t + 1]))
            if t >= 2:
                dve.wait_ge(affT_mm, t - 1)
            V.tensor_scalar(aff[:, t % 2, :], rt_exp[:, t % 2, :], rt_inv[:, t:t + 1], None, ALU.mult).then_inc(aff_ok, 1)

        def aff_out(t):
            dve.wait_ge(affT_mm, t + 1)
            V.tensor_copy(affT[:, tok(TILES[t])], ps[0:NE, 7, 0:P]).then_inc(affT_ok, 1)

        def top(cols_, at, rounds, tiles):
            dve.wait_ge(affT_ok, tiles)
            w = affT[:, cols_]
            for r in range(rounds):
                o = slice(at + 8 * r, at + 8 * r + 8)
                step(V.max(topv[:, o], w))
                step(V.max_index(topi[:, o], topv[:, o], w))
                if r < rounds - 1:
                    step(V.match_replace(w, topv[:, o], w, -1.0))

        for t in range(NT):
            epilogue(t)
            h2(t)
            if t >= 1:
                aff_out(t - 1)
            if t == 2:
                top(slice(NLAT, NTOK), CL, CP // 8, 1)
        aff_out(NT - 1)

        dve.wait_ge(rt_mm, NT)
        for buf in xT:
            V.memset(buf[:, :, CS:CSP], 0.0)
        V.memset(gq, 0.0)
        for dst, src in ((a2x, a2[:]), (sh2x, mod[:, 24:32, :])):
            step(V.tensor_copy(dst[:, :, 0:CL], src[:, :, 0:1].to_broadcast([P, KC, CL])))
            step(V.tensor_copy(dst[:, :, CL:CS], src[:, :, 1:2].to_broadcast([P, KC, CP])))

        top(slice(0, NLAT), 0, CL // 8, NT)
        step(V.tensor_copy(topf[:, 0:CL], topi[:, 0:CL]))
        step(V.tensor_scalar(topf[:, CL:CS], topi[:, CL:CS], float(NLAT), None, ALU.add))
        dve.sem_inc(top_ok, 1)
        step(V.tensor_copy(gq[:, :, 0:CS], topv[:].unsqueeze(1).to_broadcast([NE, GS, CS])))
        for r in range(GS):
            n = min(QR, CS - r * QR)
            step(V.tensor_copy(gq[:, r, GS * QR:GS * QR + n], topv[:, r * QR:r * QR + n]))
        dve.sem_inc(top_ok, 1)
        dve.wait_ge(topT_mm, 1)
        step(V.tensor_copy(idxT[:], ps[0:CS, 7, 0:NE]))

        def pick_tokens(e, q):
            V.tensor_copy(idx_of[q][:], idxT[:, bass.ds(e, 1)]).then_inc(picked, 1)

        def pick_gates(e, q):
            V.tensor_copy(gate_of[:, q, :].unsqueeze(2), gate3[:, :, bass.ds(e, 1)]).then_inc(gate_at, 1)

        def columns(q, value):
            dve.wait_ge(xgT_mm, value)
            for j in range(2):
                src = ps[:, 6 + j, 0:4 * CS].rearrange("p (c n) -> p c n", n=CS)
                V.tensor_tensor(xT[q % 2][:, 4 * j:4 * j + 4, 0:CS], src, a2x[:, 4 * j:4 * j + 4, :], ALU.mult).then_inc(mul_ok, 1)
            for j in range(2):
                dve.wait_ge(mul_ok, value * 2 + (j - 1))
                V.tensor_tensor(xT[q % 2][:, 4 * j:4 * j + 4, 0:CS], xT[q % 2][:, 4 * j:4 * j + 4, 0:CS],
                                sh2x[:, 4 * j:4 * j + 4, :], ALU.add).then_inc(xTe_ok, 1)

        pick_tokens(0, 0)
        pick_tokens(1, 1)
        dve.wait_ge(topT_mm, 2)
        step(V.tensor_scalar(gate3[:].rearrange("p r e -> p (r e)"), ps[:, 6, 0:GS * NE], 0.5, None, ALU.mult))
        dve.sem_inc(slots_ok, 1)
        pick_gates(0, 0)
        pick_gates(1, 1)
        dve.sem_inc(ye_dve, GS)
        columns(0, 1)

        def silu(value):
            dve.wait_ge(th_ok, value)
            V.scalar_tensor_tensor(act_g, tanh_g, 1.0, two(0), ALU.add, ALU.mult).then_inc(silu_ok, 1)

        silu(1)

        def group(b, last):
            for q in range(GROUP):
                e = b * GROUP + q
                end = last and q == GROUP - 1
                if not (last and q >= 2):
                    dve.wait_ge(scattered, e * 16 + (SCAT0 - 16))
                    pick_tokens(e + 2, (q + 2) % GROUP)
                    pick_gates(e + 2, (q + 2) % GROUP)
                if not end:
                    columns((q + 1) % GROUP, e + 2)
                dve.wait_ge(units_used, e * UNITS + (RING + 4))
                dve.wait_ge(silu_ok, e + 1)
                dve.wait_ge(gate_at, e + 1)
                for r in range(GS):
                    cs = slice(r * QN, (r + 1) * QN)
                    V.scalar_tensor_tensor(act_g[:, cs], act_g[:, cs], gate_of[:, q, r:r + 1], two(2)[:, cs],
                                           ALU.mult, ALU.mult).then_inc(hid_ok, 1)
                dve.wait_ge(hidT_mm, e + 1)
                hp = ps[:, 7, 0:2 * P].rearrange("p (b n) -> p b n", n=P)
                V.tensor_copy(hid[:, 4:6, :], hp[:, :, 0:CSP]).then_inc(hidc_dve, 1)
                V.tensor_copy(hid[:, 6:8, 2 * QR:CSP], hp[:, :, CSP:P]).then_inc(hidc_dve, 1)
                if not end:
                    silu(e + 2)
                dve.wait_ge(units_used, e * UNITS + (RING + (6 if end else 8)))
                dve.wait_ge(scattered, e * 16 + (SCAT0 - 16))
                for r in range(GS):
                    n = min(QR, CS - r * QR)
                    V.tensor_copy(ys[r * QR:r * QR + n, q % 2, GS * QN:D],
                                  two(4)[GS * QR:GS * QR + n, r * QN:(r + 1) * QN]).then_inc(ye_dve, 1)

        with dve.Fori(0, NE // GROUP - 1) as b:
            group(b, False)
        group(NE // GROUP - 1, True)

        for i in range(NT):
            n = 3 * NT + i
            dve.wait_ge(frs_ok, i + 1)
            V.scalar_tensor_tensor(fin[:, i, :], fin[:, i, :], rs[:, n:n + 1], gtile[:, 1 if i == LT else 0, :],
                                   ALU.mult, ALU.mult).then_inc(fin_mul, 1)
            dve.wait_ge(fin_mul, i + 1)
            V.tensor_tensor(fin[:, i, :], fin[:, i, :], x[:, i, :], ALU.add).then_inc(fin_ok, 1)

    block.__exit__(None, None, None)


_INS = ['x_prompt', 'x_sample', 'c', 'c_ctx', 'cache_k', 'cache_v', 'w_mod', 'b_mod', 'g_pre_mix', 'g_post_mix',
        'g_pre_ffn', 'g_post_ffn', 'w_in', 'q_norm', 'k_norm', 'conv_w', 'conv_b', 'conv_ln_g', 'conv_ln_b',
        'w_out', 'w_router', 'w_gate', 'w_up', 'w_down']
_OUTS = [(1, NCTX, D), (1, NLAT, D), (1, 1, NCTX, NKV, HD), (1, 1, NCTX, NKV, HD)]


def _constants():
    grid, half = 64, HD // 4
    freqs = (np.float32(10000.0) ** (-np.arange(half, dtype=np.float32) / np.float32(half))).astype(np.float32)
    pos = np.arange(NLAT)
    cos, sin = np.ones((NTOK, HD), np.float32), np.zeros((NTOK, HD), np.float32)
    for axis, p in enumerate((pos // grid, pos % grid)):
        ang = p.astype(np.float32)[:, None] * freqs[None, :]
        at = axis * 2 * half
        cos[:NLAT, at:at + half] = cos[:NLAT, at + half:at + 2 * half] = np.cos(ang)
        sin[:NLAT, at:at + half] = -np.sin(ang)
        sin[:NLAT, at + half:at + 2 * half] = np.sin(ang)
    sel = np.zeros((P, 2), np.float32)
    pick2 = np.zeros((2, 2, P), np.float32)
    for g in range(2):
        sel[g::32, g] = 1.0
        pick2[g, g] = 1.0
    return {"ident": np.eye(P, dtype=np.float32), "cos": cos, "sin": sin, "sel": sel, "pick2": pick2}


def kernel(**inputs):
    import concourse.bacc as bacc
    from concourse.bass_utils import run_bass_kernel_spmd

    nc = bacc.Bacc("TRN2", target_bir_lowering=False, num_devices=1)
    arrays, aps = {}, {}
    for name, value in [(n, np.ascontiguousarray(inputs[n])) for n in _INS] + list(_constants().items()):
        arrays[f"in_{name}"] = value
        aps[name] = nc.dram_tensor(f"in_{name}", value.shape, mybir.dt.from_np(value.dtype), kind="ExternalInput").ap()
    outs = [nc.dram_tensor(f"out_{i}", shape, mybir.dt.float32, kind="ExternalOutput").ap() for i, shape in enumerate(_OUTS)]
    build(nc, aps, outs)
    r = run_bass_kernel_spmd(nc, [arrays], core_ids=[0])
    return tuple(r.results[0][f"out_{i}"] for i in range(len(_OUTS)))
```

```python
import numpy as np
import concourse.bass as bass
import concourse.mybir as mybir

P = 128
D = 1024
KC = D // P
NLAT, NCTX = 512, 128
NTOK = NLAT + NCTX
LT = NLAT // P
NT = NTOK // P
HD, NH, NKV = 64, 8, 2
AW, KVW, DC = NH * HD, NKV * HD, 512
CC = DC // P
CD = CC - 2
TAPS, PAD = 31, 15
NE, F = 16, 1024
CL, CP = 2 * NLAT // NE, 2 * NCTX // NE
CS = CL + CP
EPS = 1e-6
PRODS = 3
EARLY = 5
HALF = 512
MOD_CHUNKS = 6 * KC

RING = 8
PRE = 6
GROUP = 4
UNITS = 6
QR = 32
GS = -(-CS // QR)
CSP = GS * QR
QN = D // (GS + 1)

CU = PAD + NLAT + PAD + NCTX + PAD
CY = NLAT + PAD + NCTX
CTX_Y = NLAT + PAD

TILES = [4, 0, 1, 2, 3]
OUT_TILES = [0, 1, 2, 3, 4]
POOL_FIN = [1]
SCAT0 = 16 * NT


def tok(i):
    return slice(i * P, (i + 1) * P)


def ycols(i):
    return slice(CTX_Y, CTX_Y + P) if i == LT else slice(i * P, (i + 1) * P)


def build(nc, a, outs):
    F32, U32 = mybir.dt.float32, mybir.dt.uint32
    ALU, ACT, AX = mybir.AluOpType, mybir.ActivationFunctionType, mybir.AxisListType

    def sb(name, shape, dt=F32):
        return nc.alloc_sbuf_tensor(name, shape, dt)

    def sem(name):
        return nc.alloc_semaphore(name)

    ring = sb("ring", [P, RING, KC * HALF])
    scratch = ring[:, PRE:RING, :].rearrange("p s n -> p (s n)")
    xn = scratch[:, 0:NT * D].rearrange("p (t d) -> p t d", d=D)
    xjunk = scratch[:, NT * D:(NT + 1) * D]
    at = 0
    u = scratch[:, at:at + CC * CU].rearrange("p (c n) -> p c n", n=CU); at += CC * CU
    taps_out = scratch[:, at:at + PRODS * CY].rearrange("p (b n) -> p b n", n=CY)
    prob = scratch[:, at:at + 2 * NTOK].rearrange("p (b n) -> p b n", n=NTOK); at += 2 * NTOK
    probT = scratch[:, at:at + 4 * NTOK].rearrange("p (b n) -> p b n", n=NTOK); at += 2 * NTOK
    qk = scratch[:, at:at + 2 * NTOK].rearrange("p (b n) -> p b n", n=NTOK); at += 2 * NTOK
    qk2 = scratch[:, at:at + NTOK]; rinv_rep = qk2[:, 0:AW]; at += NTOK
    rope_a = scratch[:, at:at + NTOK]; rinvT = rope_a[:, 0:AW]; at += NTOK
    assert at <= scratch.shape[1]
    ln_sq = scratch[:, 0:CC * NTOK].rearrange("p (c n) -> p c n", n=NTOK)
    ln_tanh = scratch[:, 0:CC * CY].rearrange("p (c n) -> p c n", n=CY)

    x = sb("x", [P, NT, D])
    big = sb("big", [P, KC, NTOK])
    y = sb("y", [P, CC, CY])
    rows = sb("rows", [P, 2, D])
    gtile = sb("gtile", [P, 2, D])
    kT = sb("kT", [P, NTOK + P])
    v = sb("v", [P, NT + 1, KVW])
    ident = sb("ident", [P, P])
    ones = sb("ones", [P, P])
    pcol = sb("pcol", [P, P])
    cw = sb("cw", [P, TAPS, CC])
    wr = sb("wr", [P, KC, NE])
    cond = sb("cond", [P, KC, 32])
    sel = sb("sel", [P, 2])
    sh_rows = sb("sh_rows", [2, NE])
    rbias = sb("rbias", [P, 2, NE])
    rlog = sb("rlog", [P, 2, NE])
    cond_t = sb("cond_t", [P, 2 * KC])
    cond_s = sb("cond_s", [P, 2 * KC])
    mod = sb("mod", [P, MOD_CHUNKS, 2])
    a1 = sb("a1", [P, KC, 2])
    a2 = sb("a2", [P, KC, 2])
    gcol = sb("gcol", [P, 2, KC, 2])
    lnc = sb("lnc", [P, 2, CC])
    nhalf = sb("nhalf", [P, 1])
    ss = sb("ss", [P, 4 * NT])
    ss2 = sb("ss2", [P, 4 * NT])
    ms = sb("ms", [P, 4 * NT])
    ln_m = sb("ln_m", [P, NT])
    ln_rs = sb("ln_rs", [P, NT])
    rs = sb("rs", [P, 4 * NT])
    hss = sb("hss", [P, 2, 10])
    hms = sb("hms", [P, 2, 10])
    hrs = sb("hrs", [P, 2, 10])
    nmax = sb("nmax", [P, NT * NH])
    rsum = sb("rsum", [P, NT * NH])
    rinv = sb("rinv", [P, NT, NH])
    rt_max = sb("rt_max", [P, NT])
    rt_sum = sb("rt_sum", [P, NT])
    rt_inv = sb("rt_inv", [P, NT])
    rt_exp = sb("rt_exp", [P, 2, NE])
    aff = sb("aff", [P, 2, NE])
    topv = sb("topv", [NE, CS])
    topi = sb("topi", [NE, CS], U32)
    topf = sb("topf", [NE, CS])
    gate3 = sb("gate3", [P, GS, NE])
    idxT = sb("idxT", [CS, NE], U32)
    gate_of = sb("gate_of", [P, GROUP, GS])
    idx_of = [sb(f"idx_of{i}", [CS, 1], U32) for i in range(GROUP)]

    affT = kT[0:NE, 0:NTOK]
    taps_out2 = gtile[:].rearrange("p g n -> p (g n)")[:, 0:PRODS * CY].rearrange("p (b n) -> p b n", n=CY)
    gflat = gtile[:].rearrange("p g n -> p (g n)")
    ch_sum = gflat[:, 0:CY]
    sq_sum = gflat[:, CY:CY + NTOK]
    modrow_a = gtile[:, 0, :].rearrange("p (b n) -> p b n", n=HALF)
    modrow_b = rows[:, :, 0:HALF]
    cos = rows[:, 0, 0:NT * HD].rearrange("p (t d) -> p t d", d=HD)
    sin = rows[:, 0, NT * HD:2 * NT * HD].rearrange("p (t d) -> p t d", d=HD)
    gain = rows[:, 1, 0:NTOK]
    kcache = rows[:, 0, 640:640 + KVW]
    prow = rows[:, 0, 768:768 + P]
    cw_rows = rows[:, 0, 896:896 + P]
    pick2 = rows[0:2, 1, 640:640 + 2 * P].rearrange("p (g n) -> p g n", n=P)
    wra = cond[:].rearrange("p k n -> p (k n)").rearrange("p (g k e) -> p g k e", g=2, e=NE)
    qT = big[:, 0:4, :]
    attnT = big[:, 4:8, :]
    flat = big[:].rearrange("p c n -> p (c n)")
    BUF = KC * CSP
    xT = [flat[:, i * BUF:(i + 1) * BUF].rearrange("p (c n) -> p c n", n=CSP) for i in range(2)]
    hid = flat[:, 2 * BUF:3 * BUF].rearrange("p (c n) -> p c n", n=CSP)
    tanh_g = flat[:, 3 * BUF:3 * BUF + GS * QN]
    act_g = flat[:, 4 * BUF:4 * BUF + GS * QN]
    a2x = flat[:, 5 * BUF:5 * BUF + KC * CS].rearrange("p (c n) -> p c n", n=CS)
    gq = flat[0:NE, 5 * BUF + KC * CS:5 * BUF + KC * CS + GS * P].rearrange("p (r n) -> p r n", n=P)
    assert 5 * BUF + KC * CS + GS * P <= KC * NTOK
    sh2x = v[:].rearrange("p t n -> p (t n)")[:, 0:KC * CS].rearrange("p (c n) -> p c n", n=CS)
    xg = rows
    yflat = y[:].rearrange("p c n -> p (c n)")
    ys = yflat[0:CS, 0:2 * D].rearrange("p (b n) -> p b n", n=D)
    fin_g = ring[:, 2:4, :].rearrange("p s n -> p (s n)")[:, 0:NT * D].rearrange("p (t d) -> p t d", d=D)
    fin = ring[:, 0:2, :].rearrange("p s n -> p (s n)")[:, 0:NT * D].rearrange("p (t d) -> p t d", d=D)

    ps = nc.alloc_psum_tensor("ps", [P, 8, 512], F32)

    def two(bank):
        return ps[:, bank:bank + 2, :].rearrange("p b n -> p (b n)")[:, 0:GS * QN]

    PCND = 0
    PB_MOD = 2 * KC
    PG = PB_MOD + MOD_CHUNKS
    PCB = PG + 4 * KC
    PLG, PLB, PROWS = PCB + CC, PCB + 2 * CC, PCB + 3 * CC

    table = nc.dram_tensor("norm_rows", [NTOK, D], F32).ap()
    accum = nc.dram_tensor("expert_sum", [NTOK, D], F32).ap()
    y_prompt, y_sample, new_k, new_v = outs
    x_rows = [a["x_sample"][0, tok(i), :] for i in range(LT)] + [a["x_prompt"][0]]
    y_rows = [y_sample[0, tok(i), :] for i in range(LT)] + [y_prompt[0]]
    w_mod, w_in, w_out = a["w_mod"][0], a["w_in"][0], a["w_out"][0]

    def cols(w, c0, n):
        return w[:, c0:c0 + n].rearrange("(k p) n -> p k n", p=P)

    GT0 = AW + 2 * KVW + DC
    pre_units = ([cols(w_mod, n * HALF, HALF) for n in range(4)]
                 + [cols(w_in, GT0, DC), cols(w_in, AW + 2 * KVW, DC)]
                 + [cols(w_in, AW, 2 * KVW), cols(w_in, 0, AW)]
                 + [cols(w_mod, n * HALF, HALF) for n in range(4, 12)]
                 + [cols(w_out, n * HALF, HALF) for n in range(2)])
    U_GT, U_A, U_KV, U_Q, U_MOD, U_WO = 4, 5, 6, 7, 8, 16
    NPRE = len(pre_units)
    assert NPRE % PRE == 0

    def slot(s, n=HALF):
        return ring[:, s, 0:KC * (n if n < HALF else HALF)].rearrange("p (k n) -> p k n", n=n)

    landed = [sem(f"landed{s}") for s in range(RING)]
    pre_used = sem("pre_used")
    units_used = sem("units_used")
    x_in = [sem(f"x_in{i}") for i in range(NT)]
    params_in, cond_in, cw_in, tab_in, wr_in, kc_in, vc_in = (
        sem(n) for n in ("params_in", "cond_in", "cw_in", "tab_in", "wr_in", "kc_in", "vc_in"))
    ident_in = sem("ident_in")
    consts = sem("consts")
    pT, pcols = sem("pT"), sem("pcols")
    cond_tanh, cond_ok = sem("cond_tanh"), sem("cond_ok")
    mod_mm, mod_ok, mod_raw = sem("mod_mm"), sem("mod_ok"), sem("mod_raw")
    ss_ok, rs_ok, xn_ok = sem("ss_ok"), sem("rs_ok"), sem("xn_ok")
    xT_mm, hT_act, hT_dve = sem("xT_mm"), sem("hT_act"), sem("hT_dve")
    glu_mm, gt_ok, glu_ok, pads = sem("glu_mm"), sem("gt_ok"), sem("glu_ok"), sem("pads")
    prod2_ok, add2_ok = sem("prod2_ok"), sem("add2_ok")
    prod_ok, add_ok, modrow_ok, modrow_mm = sem("prod_ok"), sem("add_ok"), sem("modrow_ok"), sem("modrow_mm")
    rowsum_ok, rep_ok, rinvT_mm, rinvT_ok = sem("rowsum_ok"), sem("rep_ok"), sem("rinvT_mm"), sem("rinvT_ok")
    ln_ms, wra_ok, shr_mm, shr_ok, rb_mm, rb_ok = (
        sem(n) for n in ("ln_ms", "wra_ok", "shr_mm", "shr_ok", "rb_mm", "rb_ok"))
    exp_zero, ctx_mm = sem("exp_zero"), sem("ctx_mm")
    small_in, pick2_in = sem("small_in"), sem("pick2_in")
    conv_dve, conv_pool, pool_step = sem("conv_dve"), sem("conv_pool"), sem("pool_step")
    qkv_mm, qkv_cp, qk_sq, qk_ss, qk_rs, rope_ok = (
        sem(n) for n in ("qkv_mm", "qkv_cp", "qk_sq", "qk_ss", "qk_rs", "rope_ok"))
    qkT_mm, qkT_cp = sem("qkT_mm"), sem("qkT_cp")
    g_mm, g_ok = sem("g_mm"), sem("g_ok")
    s_mm, max_ok, exp_ok, t_mm, pt_dve, pt_act, pv_mm = (
        sem(n) for n in ("s_mm", "max_ok", "exp_ok", "t_mm", "pt_dve", "pt_act", "pv_mm"))
    o_norm = sem("o_norm")
    ln_mm, ln_cen, ln_sq_ok, ln_rs_ok, ln_yn, ln_th, conv_ok = (
        sem(n) for n in ("ln_mm", "ln_cen", "ln_sq_ok", "ln_rs_ok", "ln_yn", "ln_th", "conv_ok"))
    out_mm, oss_ok, ors_ok, x1_ok, xss_ok, xrs_ok, xn2_ok = (
        sem(n) for n in ("out_mm", "oss_ok", "ors_ok", "x1_ok", "xss_ok", "xrs_ok", "xn2_ok"))
    table_in = [sem("table_in0"), sem("table_in1")]
    x2T_mm, h2_act, h2_dve, rt_mm, rt_mx, rt_ex, aff_ok, affT_mm, affT_ok = (
        sem(n) for n in ("x2T_mm", "h2_act", "h2_dve", "rt_mm", "rt_mx", "rt_ex", "aff_ok", "affT_mm", "affT_ok"))
    top_ok, topT_mm, slots_ok, picked = sem("top_ok"), sem("topT_mm"), sem("slots_ok"), sem("picked")
    gathered = [sem("gathered0"), sem("gathered1")]
    xgT_mm, xTe_ok, th_ok, hid_ok, ye_act, ye_dve = (
        sem(n) for n in ("xgT_mm", "xTe_ok", "th_ok", "hid_ok", "ye_act", "ye_dve"))
    hidT_mm, hidc_act, hidc_dve, gate_at = (sem(n) for n in ("hidT_mm", "hidc_act", "hidc_dve", "gate_at"))
    mul_ok, silu_ok, conv_dve_step, rope_half, fin_mul, pool_mul, pool_fin, act_fin, new_k_done, pool_turn = (
        sem(n) for n in ("mul_ok", "silu_ok", "conv_dve_step", "rope_half", "fin_mul", "pool_mul", "pool_fin", "act_fin", "new_k_done", "pool_turn"))
    scattered = sem("scattered")
    fin_in = [sem(f"fin_in{i}") for i in range(NT)]
    fss_ok, frs_ok, fin_ok, y_done, kv_done = (
        sem(n) for n in ("fss_ok", "frs_ok", "fin_ok", "y_done", "kv_done"))
    act_step, dve_step, zero_ok = sem("act_step"), sem("dve_step"), sem("zero_ok")

    def stepper(eng, s):
        count = [0]

        def step(ins):
            count[0] += 1
            ins.then_inc(s, 1)
            eng.wait_ge(s, count[0])
        return step

    heads = [(t, i, h) for t, i in enumerate(TILES) for h in range(NH)]
    NU = len(heads)
    BETWEEN = {9: "mod8", 11: "mod9", 13: "mod10", 15: "mod11", 25: "mean", 28: "var", 30: "rstd",
               32: "gain0", 34: "gain1"}
    CONV_AT = [*range(1, 9), *range(10, 24, 2)]
    LN_SQ_AT = 26
    SILU_AT, GATE_AT = 31, 33
    stages = []
    for n in range(NU):
        if n in BETWEEN:
            stages.append(BETWEEN[n])
        stages.append(n)
    s_buf = {st: 2 * (k % 2) for k, st in enumerate(stages)}
    HT_LAT = [1, 1, 2, 2, 7, 3, 8, 4]
    n_lat = lambda n: max(0, n - NH)

    block = nc.Block()
    block.__enter__()

    @block.sync
    def _(sp):
        sp.dma_start(prow[0:KC, :], a["c"][0].rearrange("(c p) -> c p", p=P)).then_inc(cond_in, 16)
        sp.dma_start(prow[KC:2 * KC, :], a["c_ctx"].rearrange("(c p) -> c p", p=P)).then_inc(cond_in, 16)
        for n, src in enumerate(pre_units):
            if n == 2:
                for i in range(NT):
                    sp.dma_start(x[:, i, :], x_rows[i]).then_inc(x_in[i], 16)
                for r, name, m in ((PB_MOD, "b_mod", MOD_CHUNKS), (PG, "g_pre_mix", KC), (PG + KC, "g_post_mix", KC),
                                   (PG + 2 * KC, "g_pre_ffn", KC), (PG + 3 * KC, "g_post_ffn", KC),
                                   (PCB, "conv_b", CC), (PLG, "conv_ln_g", CC), (PLB, "conv_ln_b", CC)):
                    sp.dma_start(prow[r:r + m, :], a[name][0].rearrange("(c p) -> c p", p=P)).then_inc(params_in, 16)
            if n == 4:
                sp.dma_start(cw_rows[0:TAPS * CC, :], a["conv_w"][0].rearrange("t (c p) -> (t c) p", p=P)).then_inc(cw_in, 16)
                sp.dma_start(kcache, a["cache_k"][0, 0].rearrange("s h d -> s (h d)")).then_inc(kc_in, 16)
            if n == PRE:
                sp.dma_start(v[:, LT, :], a["cache_v"][0, 0].rearrange("s h d -> s (h d)")).then_inc(vc_in, 16)
                sp.dma_start(cos, a["cos"].rearrange("(t p) d -> p t d", p=P)).then_inc(tab_in, 16)
                sp.dma_start(sin, a["sin"].rearrange("(t p) d -> p t d", p=P)).then_inc(tab_in, 16)
                for h in range(NH + NKV):
                    src_ = a["q_norm" if h < NH else "k_norm"]
                    sp.dma_start(gain[:, h * HD:(h + 1) * HD], src_[0:1, :].to_broadcast([P, HD])).then_inc(tab_in, 16)
                sp.dma_start(wr[:], a["w_router"][0].rearrange("(k p) e -> p k e", p=P)).then_inc(wr_in, 16)
                sp.dma_start(pick2, a["pick2"]).then_inc(pick2_in, 16)
            if n >= PRE:
                sp.wait_ge(pre_used, n - PRE + 1)
            sp.dma_start(slot(n % PRE, src.shape[2]), src).then_inc(landed[n % PRE], 16)

        def unit(j, w, e, half):
            src = a[w][0, e].rearrange("(h k p) n -> h p k n", p=P, h=2)[half]
            sp.dma_start(slot(j % RING, D), src).then_inc(landed[j % RING], 16)

        for half in range(2):
            sp.wait_ge(units_used, half + 1)
            unit(half, "w_gate", 0, half)

        def group(b, last):
            for q in range(GROUP):
                e = b * GROUP + q
                n = 2 + UNITS * q
                for w, after in (("w_up", 0), ("w_gate", 1), ("w_down", 0)):
                    if after and last and q == GROUP - 1:
                        continue
                    for half in range(2):
                        sp.wait_ge(units_used, b * (GROUP * UNITS) + (n + 1))
                        unit(n, w, e + after, half)
                        n += 1

        with sp.Fori(0, NE // GROUP - 1) as b:
            group(b, False)
        group(NE // GROUP - 1, True)

        sp.wait_ge(scattered, SCAT0 + 16 * NE)
        sp.wait_ge(units_used, RING + UNITS * NE)
        for i in range(NT):
            sp.dma_start(fin[:, i, :], accum[tok(i), :]).then_inc(fin_in[i], 16)
        for i in range(NT):
            sp.wait_ge(fin_ok, i + 1)
            sp.dma_start(y_rows[i], fin_g[:, i, :]).then_inc(y_done, 16)
        sp.wait_ge(y_done, 16 * NT)

    @block.gpsimd
    def _(pool):
        step = stepper(pool, pool_step)
        nc.gpsimd.memset(cond[:], 0.0).then_inc(consts, 1)
        nc.gpsimd.memset(nhalf[:], -0.5)
        nc.gpsimd.memset(ones[:], 1.0 / DC).then_inc(consts, 1)
        nc.gpsimd.memset(yflat[:, 0:D], 0.0).then_inc(zero_ok, 1)

        def root(n, src, dst, scale, ready, value, done):
            pool.wait_ge(ready, value)
            tmp = ms[:, n[0]:n[1]]
            step(nc.gpsimd.tensor_scalar(tmp, src, scale, EPS, ALU.mult, ALU.add))
            nc.gpsimd.tensor_tensor(dst, tmp, nhalf[:].to_broadcast([P, n[1] - n[0]]), ALU.pow).then_inc(done, 1)

        pool.wait_ge(consts, 2)
        for i in range(NT):
            root((i, i + 1), ss[:, i:i + 1], rs[:, i:i + 1], 1.0 / D, ss_ok, i + 1, rs_ok)

        pool.wait_ge(xT_mm, KC)
        pool.wait_ge(ctx_mm, 2)
        nc.gpsimd.memset(u[:, :, 0:PAD], 0.0)
        nc.gpsimd.memset(u[:, :, PAD + NLAT:2 * PAD + NLAT], 0.0)
        nc.gpsimd.memset(u[:, :, CU - PAD:CU], 0.0).then_inc(pads, 1)

        pool.wait_ge(zero_ok, 1)
        for i in range(NT):
            pool.dma_start(accum[tok(i), :], yflat[:, 0:D]).then_inc(scattered, 16)

        taps = [1]

        def conv(n):
            for k in range(taps[0], min(TAPS, taps[0] + n)):
                pool.wait_ge(prod_ok, k + 1)
                if k > 1:
                    pool.wait_ge(add_ok, k - 1)
                nc.gpsimd.tensor_tensor(y[:, CC - 1, :], y[:, CC - 1, :], taps_out[:, k % PRODS, :], ALU.add).then_inc(add_ok, 1)
            taps[0] = min(TAPS, taps[0] + n)

        taps2 = [1]

        def conv2(n):
            for k in range(taps2[0], min(TAPS, taps2[0] + n)):
                pool.wait_ge(prod2_ok, k + 1)
                if k > 1:
                    pool.wait_ge(add2_ok, k - 1)
                nc.gpsimd.tensor_tensor(y[:, CC - 2, :], y[:, CC - 2, :], (taps_out if k < EARLY else taps_out2)[:, k % PRODS, :], ALU.add).then_inc(add2_ok, 1)
            taps2[0] = min(TAPS, taps2[0] + n)

        for t in range(NT):
            conv(4)
            pool.wait_ge(qk_ss, t + 1)
            step(nc.gpsimd.tensor_scalar(hms[:, t % 2, :], hss[:, t % 2, :], 1.0 / HD, EPS, ALU.mult, ALU.add))
            nc.gpsimd.tensor_tensor(hrs[:, t % 2, :], hms[:, t % 2, :], nhalf[:].to_broadcast([P, 10]),
                                    ALU.pow).then_inc(qk_rs, 1)
            conv(2)
        conv(TAPS)
        conv2(EARLY - 1)
        pool.wait_ge(add2_ok, EARLY - 1)
        pool.sem_inc(conv_pool, 1)

        def chunk_sum(out, parts, ready, value):
            pool.wait_ge(ready, value)
            step(nc.gpsimd.tensor_tensor(out, parts[0], parts[1], ALU.add))
            step(nc.gpsimd.tensor_tensor(out, out, parts[2], ALU.add))
            nc.gpsimd.tensor_tensor(out, out, parts[3], ALU.add).then_inc(conv_pool, 1)

        for t in range(NT):
            conv2((7, 12, 0, 0, 0)[t])
            if t == 2:
                conv2(TAPS)
                pool.wait_ge(add2_ok, TAPS - 1)
                chunk_sum(ch_sum, [y[:, c, :] for c in range(CC)], conv_dve, 1)
            if t == 3:
                chunk_sum(sq_sum, [ln_sq[:, c, :] for c in range(CC)], ln_sq_ok, 2)
                pool.wait_ge(ln_ms, 1)
                nc.gpsimd.tensor_tensor(ln_rs[:], ln_m[:], nhalf[:].to_broadcast([P, NT]), ALU.pow).then_inc(ln_rs_ok, 1)
            pool.wait_ge(rowsum_ok, t + 1)
            if t >= 1:
                pool.wait_ge(rinvT_mm, t)
            else:
                pool.wait_ge(rope_ok, NT)
            nc.gpsimd.tensor_copy(rinv_rep.rearrange("p (h d) -> p h d", d=HD),
                                  rinv[:, t, :].unsqueeze(2).to_broadcast([P, NH, HD])).then_inc(rep_ok, 1)

        for t in range(NT):
            for n, ready, done in ((NT + t, oss_ok, ors_ok), (2 * NT + t, xss_ok, xrs_ok)):
                pool.wait_ge(ready, 2 * (t + 1))
                step(nc.gpsimd.tensor_scalar(ms[:, n:n + 1], ss[:, n:n + 1], EPS, ss2[:, n:n + 1], ALU.add, ALU.add))
                nc.gpsimd.tensor_tensor(rs[:, n:n + 1], ms[:, n:n + 1], nhalf[:], ALU.pow).then_inc(done, 1)

        pool.wait_ge(rt_mm, NT)
        nc.gpsimd.memset(gq, 0.0).then_inc(exp_zero, 1)
        for buf in xT:
            nc.gpsimd.memset(buf[:, :, CS:CSP], 0.0).then_inc(exp_zero, 1)

        def gather(q, value, gvalue, first):
            pool.wait_ge(picked, value)
            if not first:
                pool.wait_ge(xgT_mm, gvalue)
            pool.sem_inc(pool_turn, 1)
            nc.gpsimd.indirect_dma_start(
                out=xg[0:CS, q % 2, :], out_offset=None, in_=table,
                in_offset=bass.IndirectOffsetOnAxis(ap=idx_of[q][:, :1], axis=0)).then_inc(gathered[q % 2], 16)

        pool.wait_ge(table_in[0], 16 * 3)
        pool.wait_ge(table_in[1], 16 * 2)
        gather(0, 1, 0, True)
        gather(1, 2, 0, True)

        def group(b, last):
            for q in range(GROUP):
                e = b * GROUP + q
                if not (last and q >= 2):
                    gather((q + 2) % GROUP, e + 3, e + 1, False)
                pool.wait_ge(ye_act, e + 2)
                pool.wait_ge(ye_dve, e * GS + 2 * GS)
                pool.wait_ge(scattered, e * 16 + SCAT0)
                pool.sem_inc(pool_turn, 1)
                nc.gpsimd.indirect_dma_start(
                    out=accum, out_offset=bass.IndirectOffsetOnAxis(ap=idx_of[q][:, :1], axis=0),
                    in_=ys[:, q % 2, :], in_offset=None, compute_op=ALU.add).then_inc(scattered, 16)

        with pool.Fori(0, NE // GROUP - 1) as b:
            group(b, False)
        group(NE // GROUP - 1, True)

        for i in range(NT):
            n = 3 * NT + i
            if i in POOL_FIN:
                pool.wait_ge(fin_in[i], 16)
                nc.gpsimd.tensor_tensor(fin_g[:, i, :], fin[:, i, :], gtile[:, 1 if i == LT else 0, :], ALU.mult).then_inc(pool_mul, 1)
            pool.wait_ge(fss_ok, i + 1)
            nc.gpsimd.tensor_scalar(ms[:, n:n + 1], ss[:, n:n + 1], 1.0 / D, EPS, ALU.mult, ALU.add).then_inc(pool_fin, 1)
            pool.wait_ge(pool_fin, i + 1)
            nc.gpsimd.tensor_tensor(rs[:, n:n + 1], ms[:, n:n + 1], nhalf[:], ALU.pow).then_inc(frs_ok, 1)

    @block.scalar
    def _(act):
        step = stepper(act, act_step)
        act.dma_start(ident[:], a["ident"]).then_inc(ident_in, 16)
        act.dma_start(sel[:], a["sel"]).then_inc(small_in, 16)

        act.wait_ge(pcols, 1)
        nc.scalar.activation(cond_t[:], pcol[:, 0:2 * KC], ACT.Tanh, scale=0.5).then_inc(cond_tanh, 1)

        def mod_rows(m, bank, dst):
            act.wait_ge(mod_mm, m + 1)
            if m % 4 >= 2:
                act.wait_ge(modrow_mm, m - 1)
            nc.scalar.activation(dst[:, m % 2, :], ps[:, bank, :], ACT.Copy).then_inc(modrow_ok, 1)

        mod_rows(0, 2, modrow_a)
        mod_rows(1, 3, modrow_a)
        for i in range(NT):
            act.wait_ge(x_in[i], 16)
            step(nc.scalar.activation(xjunk, x[:, i, :], ACT.Square, accum_out=ss[:, i:i + 1]))
            act.sem_inc(ss_ok, 1)
        mod_rows(2, 2, modrow_a)

        def hT_lat(c):
            act.wait_ge(xT_mm, c + 1)
            nc.scalar.activation(big[:, c, 0:NLAT], ps[:, 4 + c % 4, :], ACT.Identity,
                                 scale=a1[:, c, 0:1], bias=mod[:, c, 0:1]).then_inc(hT_act, 1)

        act.wait_ge(mod_ok, 1)
        hT_lat(0)
        hT_lat(2)
        act.wait_ge(ctx_mm, 1)
        for c in range(4):
            nc.scalar.activation(big[:, c, NLAT:NTOK], ps[:, 0, c * P:(c + 1) * P], ACT.Identity,
                                 scale=a1[:, c, 1:2], bias=mod[:, c, 1:2]).then_inc(hT_act, 1)
        mod_rows(3, 3, modrow_a)
        act.wait_ge(mod_ok, 2)
        hT_lat(4)
        hT_lat(6)

        for c in range(CC):
            act.wait_ge(glu_mm, c + 1)
            nc.scalar.activation(u[:, c, PAD:PAD + NLAT], ps[:, 4 + c, :], ACT.Tanh, scale=0.5).then_inc(gt_ok, 1)
            nc.scalar.activation(u[:, c, 2 * PAD + NLAT:CU - PAD], ps[:, c, 0:P], ACT.Tanh, scale=0.5).then_inc(gt_ok, 1)

        act.wait_ge(glu_ok, 2 * CC)
        act.wait_ge(pads, 1)
        taps = [0]
        c3 = CC - 1

        def products(n):
            for k in range(taps[0], min(TAPS, taps[0] + n)):
                if k == 0:
                    nc.scalar.activation(y[:, c3, :], u[:, c3, 0:CY], ACT.Identity, scale=cw[:, 0, c3:c3 + 1],
                                         bias=pcol[:, PCB + c3:PCB + c3 + 1]).then_inc(prod_ok, 1)
                else:
                    if k > PRODS:
                        act.wait_ge(add_ok, k - PRODS)
                    nc.scalar.activation(taps_out[:, k % PRODS, :], u[:, c3, k:k + CY], ACT.Copy,
                                         scale=cw[:, k, c3:c3 + 1]).then_inc(prod_ok, 1)
            taps[0] = min(TAPS, taps[0] + n)

        taps2 = [0]

        def products2(n):
            c = CC - 2
            for k in range(taps2[0], min(TAPS, taps2[0] + n)):
                if k == 1:
                    act.wait_ge(add_ok, TAPS - 1)
                if k == EARLY:
                    act.wait_ge(modrow_mm, 8)
                if k == 0:
                    nc.scalar.activation(y[:, c, :], u[:, c, 0:CY], ACT.Identity, scale=cw[:, 0, c:c + 1],
                                         bias=pcol[:, PCB + c:PCB + c + 1]).then_inc(prod2_ok, 1)
                else:
                    if k > PRODS:
                        act.wait_ge(add2_ok, k - PRODS)
                    nc.scalar.activation((taps_out if k < EARLY else taps_out2)[:, k % PRODS, :], u[:, c, k:k + CY], ACT.Copy,
                                         scale=cw[:, k, c:c + 1]).then_inc(prod2_ok, 1)
            taps2[0] = min(TAPS, taps2[0] + n)

        def copies(t):
            i = TILES[t]
            act.wait_ge(qkv_mm, t + 1)
            if t >= 2:
                act.wait_ge(rope_ok, t - 1)
                act.wait_ge(qkT_mm, 2 * (t - 1))
            if t == 2:
                act.wait_ge(new_k_done, 16)
            nc.scalar.activation(qk[:, t % 2, 0:AW].rearrange("p (j g d) -> p g j d", g=2, d=HD),
                                 ps[:, 4 + t % 2, :].rearrange("p (g j d) -> p g j d", g=2, d=HD), ACT.Copy).then_inc(qkv_cp, 1)
            nc.scalar.activation(qk[:, t % 2, AW:NTOK], ps[:, 6 + t % 2, 0:KVW], ACT.Copy).then_inc(qkv_cp, 1)
            nc.scalar.activation(v[:, i if i < LT else NT, :], ps[:, 6 + t % 2, KVW:2 * KVW], ACT.Copy).then_inc(qkv_cp, 1)
            act.wait_ge(qkv_cp, 3 * t + 2)
            if t >= 1:
                act.wait_ge(qk_ss, t)
            nc.scalar.activation(qk2, qk[:, t % 2, :], ACT.Square).then_inc(qk_sq, 1)

        def transposed(t):
            i = TILES[t]
            act.wait_ge(qkT_mm, 2 * (t + 1))
            nc.scalar.activation(qT[:, :, tok(i)], ps[:, t % 2, :].rearrange("p (j n) -> p j n", n=P), ACT.Copy).then_inc(qkT_cp, 1)
            at = NTOK if i == LT else i * P
            nc.scalar.activation(kT[:, at:at + P], ps[:, 2, 0:P], ACT.Copy).then_inc(qkT_cp, 1)

        for t in range(NT):
            products(4)
            copies(t)
            if t == 1:
                act.wait_ge(rope_ok, 1)
                act.dma_start(new_k[0, 0].rearrange("s h d -> s (h d)"), qk[:, 0, AW:NTOK]).then_inc(new_k_done, 16)
            products(2)
            if t >= 1:
                transposed(t - 1)
        act.wait_ge(qkv_cp, 3)
        act.dma_start(new_v[0, 0].rearrange("s h d -> s (h d)"), v[:, NT, :]).then_inc(kv_done, 16)
        products(TAPS)
        for m in range(4, 8):
            mod_rows(m, 6 + m % 2, modrow_a)
            products2((0, 2, 2, 0)[m - 4])
        transposed(NT - 1)
        products2(EARLY - 4)

        def g_out(base, n, bank):
            act.wait_ge(g_mm, base + n + 1)
            nc.scalar.activation(gtile[:, n // 2, (n % 2) * 512:(n % 2 + 1) * 512], ps[:, bank, :], ACT.Copy).then_inc(g_ok, 1)

        def exp(n):
            t, i, h = heads[n]
            w = P if i == LT else NTOK
            act.wait_ge(max_ok, n + 1)
            if n < 2:
                act.wait_ge(conv_pool, 1)
            else:
                act.wait_ge(t_mm, n - 1)
            s = s_buf[n]
            step(nc.scalar.activation(prob[:, n % 2, 0:w], ps[:, s:s + 2, :].rearrange("p b n -> p (b n)")[:, 0:w],
                                      ACT.Exp, bias=nmax[:, n:n + 1], accum_out=rsum[:, n:n + 1]))
            act.sem_inc(exp_ok, 1)

        def first_four(n):
            w = P if heads[n][1] == LT else 512
            act.wait_ge(t_mm, n + 1)
            if n >= 4:
                act.wait_ge(pv_mm, (n - 4) // 2 + 1)
            elif n == 0:
                act.wait_ge(qkT_mm, 2 * NT)
            nc.scalar.activation(probT[:, n % 4, 0:w], ps[:, 4, 0:w], ACT.Copy).then_inc(pt_act, 1)

        def sums_out(t):
            act.wait_ge(rinvT_mm, t + 1)
            if t >= 1:
                act.wait_ge(o_norm, t)
            nc.scalar.activation(rinvT, ps[:, 7, :], ACT.Copy).then_inc(rinvT_ok, 1)

        for n in range(NU + 4):
            if n < NU and n in BETWEEN:
                what = BETWEEN[n]
                if what.startswith("mod"):
                    if what == "mod8":
                        act.wait_ge(rope_ok, NT)
                    mod_rows(int(what[3:]), s_buf[what], modrow_b)
                elif what.startswith("gain"):
                    act.wait_ge(ln_ms, 1)
                    m = 2 * int(what[4:])
                    g_out(0, m, s_buf[what])
                    g_out(0, m + 1, s_buf[what] + 1)
            if n == LN_SQ_AT:
                act.wait_ge(ln_cen, 2)
                nc.scalar.activation(ln_sq[:, :, 0:NLAT], y[:, :, 0:NLAT], ACT.Square).then_inc(ln_sq_ok, 1)
                nc.scalar.activation(ln_sq[:, :, NLAT:NTOK], y[:, :, CTX_Y:CY], ACT.Square).then_inc(ln_sq_ok, 1)
            c = n - SILU_AT
            if 0 <= c < CC:
                act.wait_ge(ln_yn, 2)
                step(nc.scalar.activation(y[:, c, :], y[:, c, :], ACT.Identity, scale=lnc[:, 0, c:c + 1], bias=lnc[:, 1, c:c + 1]))
                nc.scalar.activation(ln_tanh[:, c, :], y[:, c, :], ACT.Tanh).then_inc(ln_th, 1)
            if n < NU:
                exp(n)
            if 1 <= n <= NU:
                first_four(n - 1)
            if n < NU:
                products2(2 if n >= NH and n % 2 else 1)
            if n >= NH + 1 and (n - 1) % NH == 0:
                sums_out((n - 1) // NH - 1)

        def squares(t):
            for half in range(2):
                act.wait_ge(out_mm, 2 * t + half + 1)
                if half == 0 and t >= 2:
                    act.wait_ge(table_in[t % 2], 16 * (t // 2))
                elif half == 0:
                    act.wait_ge(modrow_mm, 12)
                n = NT + t
                dst = (ss, ss2)[half][:, n:n + 1]
                step(nc.scalar.activation(rows[:, t % 2, half * HALF:(half + 1) * HALF], ps[:, 2 * ((t + 1) % 2) + half, :],
                                          ACT.Square, scale=D ** -0.5, accum_out=dst))
                act.sem_inc(oss_ok, 1)

        def epilogue(t):
            i = OUT_TILES[t]
            n = 2 * NT + t
            for half in range(2):
                act.wait_ge(x1_ok, 2 * t + half + 1)
                dst = (ss, ss2)[half][:, n:n + 1]
                step(nc.scalar.activation(rows[:, t % 2, half * HALF:(half + 1) * HALF], x[:, i, half * HALF:(half + 1) * HALF],
                                          ACT.Square, scale=D ** -0.5, accum_out=dst))
                act.sem_inc(xss_ok, 1)
            act.wait_ge(x2T_mm, 2 * t + 1)
            nc.scalar.activation(big[:, 0:4, tok(i)], ps[:, 4, :].rearrange("p (c n) -> p c n", n=P), ACT.Copy).then_inc(h2_act, 1)
            act.wait_ge(xrs_ok, t + 1)
            nc.scalar.activation(rows[:, t % 2, :], x[:, i, :], ACT.Copy, scale=rs[:, n:n + 1]).then_inc(xn2_ok, 1)
            act.wait_ge(xn2_ok, t + 1)
            act.dma_start(table[tok(i), :], rows[:, t % 2, :]).then_inc(table_in[t % 2], 16)
            act.wait_ge(rt_mx, t + 1)
            step(nc.scalar.activation(rt_exp[:, t % 2, :], rlog[:, t % 2, :], ACT.Exp, bias=rt_max[:, t:t + 1],
                                      accum_out=rt_sum[:, t:t + 1]))
            act.sem_inc(rt_ex, 1)

        for t in range(NT):
            squares(t)
            epilogue(t)
        for n in range(4):
            g_out(4, n, 2 + n)

        def half_tanh():
            nc.scalar.activation(tanh_g, two(0), ACT.Tanh, scale=0.5).then_inc(th_ok, 1)

        act.sem_inc(ye_act, 1)
        act.wait_ge(units_used, RING + 2)
        half_tanh()

        def group(b, last):
            for q in range(GROUP):
                e = b * GROUP + q
                end = last and q == GROUP - 1
                act.wait_ge(hidT_mm, e + 1)
                hp = ps[:, 6, :].rearrange("p (b n) -> p b n", n=P)
                nc.scalar.activation(hid[:, 0:4, :], hp[:, :, 0:CSP], ACT.Copy).then_inc(hidc_act, 1)
                nc.scalar.activation(hid[:, 6:8, 0:2 * QR].rearrange("p h (r t) -> p r h t", r=2),
                                     hp[:, :, CSP:P].rearrange("p (r h) t -> p r h t", r=2), ACT.Copy).then_inc(hidc_act, 1)
                if not end:
                    act.wait_ge(units_used, e * UNITS + (RING + 6))
                    act.wait_ge(silu_ok, e + 1)
                    half_tanh()
                act.wait_ge(units_used, e * UNITS + (RING + (6 if end else 8)))
                act.wait_ge(scattered, e * 16 + (SCAT0 - 16))
                nc.scalar.activation(ys[:, q % 2, 0:GS * QN], two(4)[0:CS, :], ACT.Copy).then_inc(ye_act, 1)

        with act.Fori(0, NE // GROUP - 1) as b:
            group(b, False)
        group(NE // GROUP - 1, True)

        for i in range(NT):
            act.wait_ge(fin_in[i], 16)
            n = 3 * NT + i
            if i >= 1:
                act.wait_ge(act_fin, i)
            nc.scalar.activation(rows[:, 0, :], fin[:, i, :], ACT.Square, accum_out=ss[:, n:n + 1]).then_inc(act_fin, 1)
            act.wait_ge(act_fin, i + 1)
            act.sem_inc(fss_ok, 1)
        act.wait_ge(kv_done, 16)
        act.wait_ge(new_k_done, 16)

    @block.tensor
    def _(pe):
        def used(ins, unit):
            ins.then_inc(units_used if unit >= NPRE - PRE else pre_used, 1)

        def wait_unit(n):
            pe.wait_ge(landed[n % PRE], 16 * (n // PRE + 1))

        def T(out, in_, k=P):
            return nc.tensor.transpose(out, in_, ident[0:k, 0:k])

        pe.wait_ge(ident_in, 16)
        pe.wait_ge(cond_in, 16 * 2)
        T(ps[:, 0, 0:2 * KC], prow[0:2 * KC, :], 2 * KC).then_inc(pT, 1)

        def modulate(n, bank):
            unit = n if n < 4 else U_MOD + n - 4
            wait_unit(unit)
            w = slot(unit % PRE)
            for k in range(KC):
                q = 32 * (k % 4)
                ins = nc.tensor.matmul(ps[q:q + 32, bank, :], cond[:, k, :], w[:, k, :], start=(k < 4), stop=(k >= 4))
            ins.then_inc(mod_mm, 1)
            pe.wait_ge(mod_mm, n + 1)
            pe.sem_inc(units_used if unit >= NPRE - PRE else pre_used, 1)

        def mod_columns(n, bank, at, src):
            pe.wait_ge(modrow_ok, n + 1)
            for m in range(4):
                ins = nc.tensor.matmul(ps[:, bank, at + 2 * m:at + 2 * m + 2], src[:, n % 2, m * P:(m + 1) * P], sel[:],
                                       start=True, stop=True)
            ins.then_inc(modrow_mm, 1)

        def latent_xT(c):
            for i in range(LT):
                ins = T(ps[:, 4 + c % 4, tok(i)], xn[:, i, c * P:(c + 1) * P])
            ins.then_inc(xT_mm, 1)

        pe.wait_ge(cond_ok, 1)
        modulate(0, 2)
        modulate(1, 3)
        pe.wait_ge(small_in, 16)
        mod_columns(0, 1, 0, modrow_a)
        mod_columns(1, 1, 8, modrow_a)
        pe.wait_ge(xn_ok, LT)
        for c in range(4):
            latent_xT(c)
        pe.wait_ge(params_in, 16 * 8)
        T(ps[:, 0, 0:PROWS], prow[0:PROWS, :], PROWS).then_inc(pT, 1)
        def context_xT(half):
            for c in range(4 * half, 4 * half + 4):
                ins = T(ps[:, 2 * half, (c % 4) * P:(c % 4 + 1) * P], xn[:, LT, c * P:(c + 1) * P])
            ins.then_inc(ctx_mm, 1)

        modulate(2, 2)
        mod_columns(2, 1, 16, modrow_a)
        pe.wait_ge(xn_ok, NT)
        pe.wait_ge(pcols, 2)
        context_xT(0)
        for c in range(4, KC):
            pe.wait_ge(hT_act if c % 2 == 0 else hT_dve, (c - 4) // 2 + 1)
            latent_xT(c)
        modulate(3, 3)
        mod_columns(3, 1, 24, modrow_a)
        context_xT(1)
        pe.wait_ge(cw_in, 16)
        T(ps[:, 3, 0:TAPS * CC], cw_rows[0:TAPS * CC, :], TAPS * CC)
        pe.wait_ge(kc_in, 16)
        T(ps[:, 3, P:2 * P], kcache).then_inc(pT, 1)

        pe.wait_ge(hT_act, HT_LAT[4])
        for m in range(2 * CC):
            unit = U_GT + m // CC
            wait_unit(unit)
            if m >= CC:
                pe.wait_ge(gt_ok, 2 * (m - CC + 1))
            if m == CC - 1:
                pe.wait_ge(pcols, 4)
            w = slot(unit % PRE)
            for bank, cols_ in ((4 + m % 4, slice(0, NLAT)), (m % 4, slice(NLAT, NTOK))):
                for k in range(KC):
                    if m == 0 and bank == 4:
                        pe.wait_ge(hT_dve if k % 2 else hT_act, HT_LAT[k])
                    elif m == 0 and k == 0:
                        pe.wait_ge(hT_act, 8)
                        pe.wait_ge(hT_dve, 8)
                    ins = nc.tensor.matmul(ps[:, bank, 0:cols_.stop - cols_.start], w[:, k, (m % 4) * P:(m % 4 + 1) * P],
                                           big[:, k, cols_], start=(k == 0), stop=(k == KC - 1))
            ins.then_inc(glu_mm, 1)
            if m % CC == CC - 1:
                pe.wait_ge(glu_mm, m + 1)
                pe.sem_inc(pre_used, 1)

        def project(t):
            i = TILES[t]
            wait_unit(U_KV)
            wait_unit(U_Q)
            if t >= 2:
                pe.wait_ge(qkv_cp, 3 * (t - 1))
            else:
                pe.wait_ge(glu_ok, 2 * CC)
            for k in range(KC):
                ins = nc.tensor.matmul(ps[:, 6 + t % 2, 0:2 * KVW], big[:, k, tok(i)], slot(U_KV % PRE, 2 * KVW)[:, k, :],
                                       start=(k == 0), stop=(k == KC - 1))
            if t == NT - 1:
                used(ins, U_KV)
            for k in range(KC):
                ins = nc.tensor.matmul(ps[:, 4 + t % 2, :], big[:, k, tok(i)], slot(U_Q % PRE)[:, k, :],
                                       start=(k == 0), stop=(k == KC - 1))
            ins.then_inc(qkv_mm, 1)
            if t == NT - 1:
                pe.wait_ge(qkv_mm, NT)
                pe.sem_inc(pre_used, 1)

        def transpose_qk(t):
            pe.wait_ge(rope_ok, t + 1)
            if t >= 1:
                pe.wait_ge(qkT_cp, 2 * t)
            for j in range(4):
                ins = T(ps[:, t % 2, j * P:(j + 1) * P],
                        qk[:, t % 2, j * P:(j + 1) * P])
            ins.then_inc(qkT_mm, 1)
            T(ps[:, 2, 0:P], qk[:, t % 2, AW:NTOK]).then_inc(qkT_mm, 1)

        for t in range(NT):
            project(t)
            if t >= 1:
                transpose_qk(t - 1)

        pe.wait_ge(qkv_cp, 3 * NT)
        for m in range(4, 8):
            modulate(m, 6 + m % 2)
            if m > 4:
                mod_columns(m - 1, 3, 8 * (m - 5), modrow_a)
        mod_columns(7, 3, 24, modrow_a)
        transpose_qk(NT - 1)

        def g_tile(layer, n, bank):
            g, half = n // 2, n % 2
            for c in range(4):
                col = gcol[:, layer, 4 * half + c, g:g + 1]
                ins = T(ps[:, bank, c * P:(c + 1) * P], col.to_broadcast([P, P]))
            ins.then_inc(g_mm, 1)

        pe.wait_ge(mod_ok, 3)
        pe.wait_ge(wr_in, 16)
        for k in range(KC):
            ins = nc.tensor.matmul(ps[0:2, 3, 64:64 + NE], mod[:, 24 + k, :], wr[:, k, :], start=(k == 0), stop=(k == KC - 1))
        ins.then_inc(shr_mm, 1)
        pe.wait_ge(shr_ok, 1)
        pe.wait_ge(pick2_in, 16)
        for g in range(2):
            ins = nc.tensor.matmul(ps[:, 3, 128 + g * NE:128 + (g + 1) * NE], pick2[:, g, :], sh_rows[:], start=True, stop=True)
        ins.then_inc(rb_mm, 1)

        def free(st):
            k = stages.index(st)
            prev = stages[k - 2] if k >= 2 else None
            if k == 0:
                pe.wait_ge(qkT_cp, 2 * NT)
            elif k == 1:
                pe.wait_ge(rb_ok, 1)
            elif prev == "mean":
                pe.wait_ge(ln_cen, 2)
            elif prev == "var":
                pe.wait_ge(ln_ms, 1)
            elif prev == "rstd":
                pe.wait_ge(ln_yn, 2)
            elif isinstance(prev, str) and prev.startswith("gain"):
                pe.wait_ge(g_ok, 2 * int(prev[4:]) + 2)
            elif isinstance(prev, str):
                pe.wait_ge(mod_raw, int(prev[3:]) - 7)
            else:
                pe.wait_ge(exp_ok, prev + 1)

        def scores(n):
            t, i, h = heads[n]
            free(n)
            s = s_buf[n]
            p0 = HD * (h // 4)
            q = qT[p0:p0 + HD, h % 4, tok(i)]
            if i == LT:
                nc.tensor.matmul(ps[:, s, 0:P], q, kT[p0:p0 + HD, NTOK:NTOK + P], start=True, stop=True).then_inc(s_mm, 1)
            else:
                nc.tensor.matmul(ps[:, s, :], q, kT[p0:p0 + HD, 0:512], start=True, stop=True)
                nc.tensor.matmul(ps[:, s + 1, 0:P], q, kT[p0:p0 + HD, 512:640], start=True, stop=True).then_inc(s_mm, 1)

        def between(what):
            free(what)
            s = s_buf[what]
            if what.startswith("mod"):
                modulate(int(what[3:]), s)
            elif what.startswith("gain"):
                m = 2 * int(what[4:])
                g_tile(0, m, s)
                g_tile(0, m + 1, s + 1)
            elif what == "mean":
                pe.wait_ge(conv_pool, 2)
                for bank, n, lo in ((s, NLAT, 0), (s + 1, NCTX, CTX_Y)):
                    ins = nc.tensor.matmul(ps[:, bank, 0:n], ones[:], ch_sum[:, lo:lo + n], start=True, stop=True)
                ins.then_inc(ln_mm, 1)
            elif what == "var":
                pe.wait_ge(conv_pool, 3)
                for i in range(NT):
                    ins = nc.tensor.matmul(ps[:, s, i:i + 1], sq_sum[:, tok(i)], ones[:, 0:1], start=True, stop=True)
                ins.then_inc(ln_mm, 1)
            else:
                pe.wait_ge(ln_rs_ok, 1)
                for i in range(NT):
                    ins = T(ps[:, s + i // 4, (i % 4) * P:(i % 4 + 1) * P], ln_rs[:, i:i + 1].to_broadcast([P, P]))
                ins.then_inc(ln_mm, 1)

        def after(what):
            if what.startswith("mod"):
                mod_columns(int(what[3:]), s_buf[what] + 1, 0, modrow_b)

        def transpose_p(n):
            pe.wait_ge(exp_ok, n + 1)
            if n > 0:
                pe.wait_ge(pt_act, n)
                if n_lat(n):
                    pe.wait_ge(pt_dve, n_lat(n))
            if heads[n][1] == LT:
                T(ps[:, 4, 0:P], prob[:, n % 2, 0:P]).then_inc(t_mm, 1)
                return
            for kc in range(NT):
                ins = T(ps[:, 4 + kc // 4, (kc % 4) * P:(kc % 4 + 1) * P], prob[:, n % 2, kc * P:(kc + 1) * P])
            ins.then_inc(t_mm, 1)

        def values(pair, part):
            n = 2 * pair
            t, i, h = heads[n]
            pe.wait_ge(pt_act, n + 2)
            if n_lat(n + 2):
                pe.wait_ge(pt_dve, n_lat(n + 2))
            if h == 0 and t >= 1 and part == 0:
                pe.wait_ge(o_norm, t)
            if n == 0:
                pe.wait_ge(vc_in, 16)
            chunks = [(0, NT)] if i == LT else [(kc, kc) for kc in range(NT)]
            split = 3 if len(chunks) > 1 else 0
            for m in range(split) if part == 0 else range(split, len(chunks)):
                kc, vt = chunks[m]
                for j in range(2):
                    ins = nc.tensor.matmul(ps[j * HD:(j + 1) * HD, 6, (h // 2) * P:(h // 2 + 1) * P],
                                           v[:, vt, (h // 4) * HD:(h // 4 + 1) * HD],
                                           probT[:, (n + j) % 4, kc * P:(kc + 1) * P], start=(m == 0), stop=(m == len(chunks) - 1))
            if part == 1:
                ins.then_inc(pv_mm, 1)

        def transpose_sums(t):
            pe.wait_ge(rep_ok, t + 1)
            if t >= 1:
                pe.wait_ge(rinvT_ok, t)
            for j in range(4):
                ins = T(ps[:, 7, j * P:(j + 1) * P], rinv_rep[:, j * P:(j + 1) * P])
            ins.then_inc(rinvT_mm, 1)

        def out_project(t):
            for n in range(2):
                for quarter in range(2):
                    out_quarter(t, n, quarter)

        def out_quarter(t, n, quarter):
            i = OUT_TILES[t]
            s = 2 * ((t + 1) % 2)
            unit = U_WO + n
            if quarter == 0:
                if t >= 2:
                    pe.wait_ge(x1_ok, 2 * (t - 2) + n + 1)
                elif n == 0:
                    pe.wait_ge(exp_ok, NU - 1 + t)
                if n == 0:
                    pe.wait_ge(o_norm, TILES.index(i) + 1)
                wait_unit(unit)
            elif t == 0:
                pe.wait_ge(conv_ok, CC)
            w = slot(unit % PRE)
            for k in range(4 * quarter, 4 * quarter + 4):
                lhs = attnT[:, k, tok(i)] if k < 4 else y[:, k - 4, ycols(i)]
                ins = nc.tensor.matmul(ps[:, s + n, :], lhs, w[:, k, :], start=(k == 0), stop=(k == KC - 1))
            if quarter == 1:
                ins.then_inc(out_mm, 1)
                if t == NT - 1:
                    pe.wait_ge(out_mm, 2 * t + n + 1)
                    pe.sem_inc(units_used, 1 + n * (RING - PRE))

        scores(0)
        for n in range(NU + 3):
            if n + 1 in BETWEEN:
                between(BETWEEN[n + 1])
            if n + 1 < NU:
                scores(n + 1)
            if 3 <= n:
                values((n - 3) // 2, (n - 3) % 2)
            if NU - 2 <= n < NU + 2:
                out_quarter(0, n % 2, (n - NU + 2) // 2)
            if n < NU:
                transpose_p(n)
            if n + 1 in BETWEEN:
                after(BETWEEN[n + 1])
            if n >= NH and n % NH == 0:
                transpose_sums(n // NH - 1)

        def route(t):
            i = OUT_TILES[t]
            g = 1 if i == LT else 0
            for half in range(2):
                pe.wait_ge(x1_ok, 2 * t + half + 1)
                if t >= 1:
                    pe.wait_ge(h2_act if half == 0 else h2_dve, t)
                elif half == 0:
                    pe.wait_ge(pt_act, NU)
                    pe.wait_ge(pt_dve, NU - NH)
                for c in range(4):
                    ins = T(ps[:, 4 + half, c * P:(c + 1) * P], x[:, i, half * HALF + c * P:half * HALF + (c + 1) * P])
                ins.then_inc(x2T_mm, 1)
            if t == 0:
                pe.wait_ge(wra_ok, 1)
            else:
                pe.wait_ge(rt_mx, t)
            for k in range(KC):
                if k == 0:
                    pe.wait_ge(h2_act, t + 1)
                if k == 4:
                    pe.wait_ge(h2_dve, t + 1)
                ins = nc.tensor.matmul(ps[:, 6, 0:NE], big[:, k, tok(i)], wra[:, g, k, :], start=(k == 0), stop=(k == KC - 1))
            ins.then_inc(rt_mm, 1)

        def transpose_aff(t):
            pe.wait_ge(aff_ok, t + 1)
            if t >= 1:
                pe.wait_ge(affT_ok, t)
            else:
                pe.wait_ge(rinvT_ok, NT)
            T(ps[0:NE, 7, 0:P], aff[:, t % 2, :]).then_inc(affT_mm, 1)

        for t in range(NT - 1):
            if t >= 1:
                out_project(t)
                route(t - 1)
                if t >= 2:
                    transpose_aff(t - 2)
        last = NT - 1
        out_quarter(last, 0, 0)
        out_quarter(last, 0, 1)
        route(last - 1)
        transpose_aff(last - 2)
        out_quarter(last, 1, 0)
        transpose_aff(last - 1)
        out_quarter(last, 1, 1)
        route(last)
        transpose_aff(last)

        pe.wait_ge(h2_act, NT)
        pe.wait_ge(h2_dve, NT)
        for n in range(4):
            g_tile(1, n, 2 + n)

        pe.wait_ge(top_ok, 1)
        T(ps[0:CS, 7, 0:NE], topf[:], NE).then_inc(topT_mm, 1)
        pe.wait_ge(top_ok, 2)
        for r in range(GS):
            ins = T(ps[:, 6, r * NE:(r + 1) * NE], gq[:, r, :], NE)
        ins.then_inc(topT_mm, 1)

        def product(x_, w, half, bank):
            out = two(bank)
            for k in range(4):
                c = 4 * half + k
                for qd, g, lo, n in ((3, 0, 0, QN), (0, 0, 0, 2 * QN), (1, 1, 0, 2 * QN), (3, 1, QN, QN), (2, 2, 0, 2 * QN),
                                     (0, 0, 2 * QN, QN), (3, 2, 2 * QN, QN), (1, 1, 2 * QN, QN), (2, 2, 2 * QN, QN)):
                    src = w[:, k, GS * QN:D] if qd == GS else w[:, k, lo:lo + n]
                    ins = nc.tensor.matmul(out[qd * QR:(qd + 1) * QR, lo:lo + n], x_[:, c, g * QR:(g + 1) * QR], src,
                                           start=(c == 0 and lo % HALF == 0), stop=(c == KC - 1 and not (qd == GS and lo == 0)))
            ins.then_inc(units_used, 1)

        def transpose_x(q, value):
            pe.wait_ge(gathered[q % 2], value)
            for c in range(KC):
                ins = T(ps[:, 6 + c // 4, (c % 4) * CS:(c % 4 + 1) * CS], xg[0:CS, q % 2, c * P:(c + 1) * P], CS)
            ins.then_inc(xgT_mm, 1)

        pe.wait_ge(g_ok, 8)
        pe.wait_ge(slots_ok, 1)
        transpose_x(0, 16)
        pe.wait_ge(xTe_ok, 2)
        pe.wait_ge(exp_zero, 3)
        for half in range(2):
            pe.wait_ge(landed[half], 16 * (NPRE // PRE + 1))
            product(xT[0], slot(half, D), half, 0)

        def group(b, last):
            for q in range(GROUP):
                e = b * GROUP + q

                def unit(n):
                    j = 2 + UNITS * q + n
                    uses = NPRE // PRE if j % RING < PRE else 0
                    pe.wait_ge(landed[j % RING], b * (16 * GROUP * UNITS // RING) + 16 * (uses + j // RING + 1))
                    return slot(j % RING, D)

                end = last and q == GROUP - 1
                product(xT[q % 2], unit(0), 0, 2)
                if not end:
                    transpose_x((q + 1) % GROUP, b * (16 * GROUP // 2) + 16 * ((q + 1) // 2 + 1))
                product(xT[q % 2], unit(1), 1, 2)
                if not end:
                    pe.wait_ge(xTe_ok, e * 2 + 4)
                    pe.wait_ge(silu_ok, e + 1)
                    product(xT[(q + 1) % 2], unit(2), 0, 0)
                pe.wait_ge(hid_ok, e * GS + GS)
                for m in range(2 * GS):
                    ins = T(ps[:, 6 + m // 4, (m % 4) * P:(m % 4 + 1) * P], act_g[:, m * P:(m + 1) * P])
                ins.then_inc(hidT_mm, 1)
                if not end:
                    product(xT[(q + 1) % 2], unit(3), 1, 0)
                pe.wait_ge(hidc_act, e * 2 + 2)
                pe.wait_ge(hidc_dve, e * 2 + 2)
                pe.wait_ge(ye_act, e + 1)
                pe.wait_ge(ye_dve, e * GS + GS)
                for half in range(2):
                    product(hid, unit((2 if end else 4) + half), half, 4)

        with pe.Fori(0, NE // GROUP - 1) as b:
            group(b, False)
        group(NE // GROUP - 1, True)

    @block.vector
    def _(dve):
        V = nc.vector
        step = stepper(dve, dve_step)
        dve.wait_ge(pT, 1)
        V.tensor_copy(pcol[:, 0:2 * KC], ps[:, 0, 0:2 * KC]).then_inc(pcols, 1)
        dve.wait_ge(cond_tanh, 1)
        step(V.scalar_tensor_tensor(cond_s[:], cond_t[:], 1.0, pcol[:, 0:2 * KC], ALU.add, ALU.mult))
        dve.wait_ge(consts, 2)
        V.tensor_scalar(cond[:, :, 0:2].rearrange("p k g -> p g k"), cond_s[:].rearrange("p (g k) -> p g k", g=2), 0.5, None,
                        ALU.mult).then_inc(cond_ok, 1)

        for i in range(NT):
            dve.wait_ge(rs_ok, i + 1)
            V.tensor_scalar(xn[:, i, :], x[:, i, :], rs[:, i:i + 1], None, ALU.mult).then_inc(xn_ok, 1)

        dve.wait_ge(pT, 2)
        step(V.tensor_copy(pcol[:, 2 * KC:PROWS], ps[:, 0, 2 * KC:PROWS]))
        step(V.tensor_scalar(lnc[:, 0, :], pcol[:, PLG:PLG + CC], 0.5, None, ALU.mult))
        step(V.tensor_scalar(lnc[:, 1, :], pcol[:, PLB:PLB + CC], 0.5, None, ALU.mult))
        dve.sem_inc(pcols, 1)

        def both(ap):
            return ap.unsqueeze(2).to_broadcast([P, ap.shape[1], 2])
        def mod_cols(lo, hi):
            step(V.tensor_tensor(mod[:, lo:hi, :], ps[:, 1, 2 * lo:2 * hi].rearrange("p (c n) -> p c n", n=2),
                                 both(pcol[:, PB_MOD + lo:PB_MOD + hi]), ALU.add))
            k = max(lo, 8)
            step(V.scalar_tensor_tensor(a1[:, k - 8:hi - 8, :], mod[:, k:hi, :], 1.0, both(pcol[:, PG + k - 8:PG + hi - 8]),
                                        ALU.add, ALU.mult))
            dve.sem_inc(mod_ok, 1)

        def hT_lat(c):
            dve.wait_ge(xT_mm, c + 1)
            V.tensor_scalar(big[:, c, 0:NLAT], ps[:, 4 + c % 4, :], a1[:, c, 0:1], mod[:, c, 0:1],
                            ALU.mult, ALU.add).then_inc(hT_dve, 1)

        dve.wait_ge(modrow_mm, 3)
        mod_cols(0, 12)
        hT_lat(1)
        hT_lat(3)
        dve.wait_ge(modrow_mm, 4)
        mod_cols(12, 16)
        hT_lat(5)
        hT_lat(7)
        dve.wait_ge(ctx_mm, 2)
        for c in range(4, KC):
            V.tensor_scalar(big[:, c, NLAT:NTOK], ps[:, 2, (c - 4) * P:(c - 3) * P], a1[:, c, 1:2], mod[:, c, 1:2],
                            ALU.mult, ALU.add).then_inc(hT_dve, 1)

        dve.wait_ge(pT, 3)
        V.tensor_scalar(cw[:].rearrange("p t c -> p (t c)"), ps[:, 3, 0:TAPS * CC], 0.5, None, ALU.mult).then_inc(pcols, 1)
        V.tensor_copy(kT[:, NLAT:NTOK], ps[:, 3, P:2 * P]).then_inc(pcols, 1)
        for c in range(CC):
            dve.wait_ge(glu_mm, CC + c + 1)
            dve.wait_ge(gt_ok, 2 * (c + 1))
            for lo, hi, bank in ((PAD, PAD + NLAT, 4 + c), (2 * PAD + NLAT, CU - PAD, c)):
                V.scalar_tensor_tensor(u[:, c, lo:hi], u[:, c, lo:hi], 1.0, ps[:, bank, 0:hi - lo],
                                       ALU.add, ALU.mult).then_inc(glu_ok, 1)
        dve.wait_ge(glu_ok, 2 * CC)
        dve.wait_ge(pads, 1)

        taps = [0]

        def conv(n):
            for k in range(taps[0], min(TAPS, taps[0] + n)):
                for c in range(CD):
                    if k == 0:
                        V.tensor_scalar(y[:, c, :], u[:, c, 0:CY], cw[:, 0, c:c + 1], pcol[:, PCB + c:PCB + c + 1],
                                        ALU.mult, ALU.add).then_inc(conv_dve_step, 1)
                    else:
                        dve.wait_ge(conv_dve_step, CD * (k - 1) + c + 1)
                        V.scalar_tensor_tensor(y[:, c, :], u[:, c, k:k + CY], cw[:, k, c:c + 1], y[:, c, :],
                                               ALU.mult, ALU.add).then_inc(conv_dve_step, 1)
            taps[0] = min(TAPS, taps[0] + n)

        dve.wait_ge(scattered, SCAT0)
        conv(4)

        dve.wait_ge(tab_in, 16 * 12)
        step(V.tensor_scalar(gain[:, 0:AW], gain[:, 0:AW], HD ** -0.5, None, ALU.mult))

        NHH = NH + NKV
        for t in range(NT):
            i = TILES[t]
            dve.wait_ge(qk_sq, t + 1)
            V.tensor_reduce(hss[:, t % 2, :], qk2.rearrange("p (h d) -> p h d", d=HD), AX.X, ALU.add).then_inc(qk_ss, 1)
            cur = qk[:, t % 2, :]
            step(V.tensor_tensor(cur, cur, gain, ALU.mult))
            if t < NT - 1:
                conv(3)
            dve.wait_ge(qk_rs, t + 1)
            step(V.tensor_tensor(cur.rearrange("p (h d) -> p h d", d=HD), cur.rearrange("p (h d) -> p h d", d=HD),
                                 hrs[:, t % 2, :].unsqueeze(2).to_broadcast([P, NHH, HD]), ALU.mult))
            pair = cur.rearrange("p (h a s d) -> p s h a d", h=NHH, a=2, s=2)
            part = rope_a.rearrange("p (h a s d) -> p s h a d", h=NHH, a=2, s=2)
            sn = sin[:, i, :].rearrange("p (a s d) -> p s a d", a=2, s=2)
            for s in range(2):
                tab = sn[:, s].unsqueeze(1).to_broadcast([P, NHH, 2, 16])
                V.tensor_tensor(part[:, s], pair[:, 1 - s], tab, ALU.mult).then_inc(rope_half, 1)
            dve.wait_ge(rope_half, 2 * (t + 1))
            step(V.tensor_tensor(cur.rearrange("p (h d) -> p h d", d=HD), cur.rearrange("p (h d) -> p h d", d=HD),
                                 cos[:, i, :].unsqueeze(1).to_broadcast([P, NHH, HD]), ALU.mult))
            V.tensor_tensor(cur, cur, rope_a, ALU.add).then_inc(rope_ok, 1)

        dve.wait_ge(modrow_mm, 8)
        step(V.tensor_tensor(mod[:, 16:32, :], ps[:, 3, 0:32].rearrange("p (c n) -> p c n", n=2), both(pcol[:, PB_MOD + 16:PB_MOD + 32]), ALU.add))
        step(V.tensor_tensor(gcol[:, 0], mod[:, 16:24, :], both(pcol[:, PG + KC:PG + 2 * KC]), ALU.mult))
        dve.sem_inc(mod_ok, 1)
        dve.wait_ge(shr_mm, 1)
        V.tensor_copy(sh_rows[:], ps[0:2, 3, 64:64 + NE]).then_inc(shr_ok, 1)
        dve.wait_ge(rb_mm, 1)
        V.tensor_copy(rbias[:].rearrange("p g e -> p (g e)"), ps[:, 3, 128:128 + 2 * NE]).then_inc(rb_ok, 1)

        def head_max(n):
            w = P if heads[n][1] == LT else NTOK
            dve.wait_ge(s_mm, n + 1)
            s = s_buf[n]
            V.tensor_reduce(nmax[:, n:n + 1], ps[:, s:s + 2, :].rearrange("p b n -> p (b n)")[:, 0:w], AX.X, ALU.max,
                            negate=True).then_inc(max_ok, 1)

        def fifth(n):
            if heads[n][1] == LT:
                return
            dve.wait_ge(t_mm, n + 1)
            dve.wait_ge(pv_mm, (n - 4) // 2 + 1)
            V.tensor_copy(probT[:, n % 4, 512:640], ps[:, 5, 0:P]).then_inc(pt_dve, 1)

        def row_sums(t):
            dve.wait_ge(exp_ok, NH * (t + 1))
            V.reciprocal(rinv[:, t, :], rsum[:, t * NH:(t + 1) * NH]).then_inc(rowsum_ok, 1)

        def normalise(t):
            i = TILES[t]
            dve.wait_ge(pv_mm, 4 * (t + 1))
            dve.wait_ge(rinvT_ok, t + 1)
            V.tensor_tensor(attnT[:, :, tok(i)], ps[:, 6, :].rearrange("p (j n) -> p j n", n=P),
                            rinvT.rearrange("p (j n) -> p j n", n=P), ALU.mult).then_inc(o_norm, 1)

        def between(what):
            s = s_buf[what]
            if what.startswith("mod"):
                m = int(what[3:])
                dve.wait_ge(modrow_mm, m + 1)
                V.tensor_tensor(mod[:, 4 * m:4 * m + 4, :], ps[:, s + 1, 0:8].rearrange("p (c n) -> p c n", n=2),
                                both(pcol[:, PB_MOD + 4 * m:PB_MOD + 4 * m + 4]), ALU.add).then_inc(mod_raw, 1)
            elif what == "mean":
                dve.wait_ge(ln_mm, 1)
                V.tensor_tensor(y[:, :, 0:NLAT], y[:, :, 0:NLAT],
                                ps[:, s, :].unsqueeze(1).to_broadcast([P, CC, NLAT]), ALU.subtract).then_inc(ln_cen, 1)
                V.tensor_tensor(y[:, :, CTX_Y:CY], y[:, :, CTX_Y:CY],
                                ps[:, s + 1, 0:P].unsqueeze(1).to_broadcast([P, CC, NCTX]), ALU.subtract).then_inc(ln_cen, 1)
            elif what == "var":
                dve.wait_ge(ln_mm, 2)
                V.tensor_scalar(ln_m[:], ps[:, s, 0:NT], EPS, None, ALU.add).then_inc(ln_ms, 1)
            elif what == "rstd":
                dve.wait_ge(ln_mm, 3)
                V.tensor_tensor(y[:, :, 0:NLAT], y[:, :, 0:NLAT],
                                ps[:, s, :].unsqueeze(1).to_broadcast([P, CC, NLAT]), ALU.mult).then_inc(ln_yn, 1)
                V.tensor_tensor(y[:, :, CTX_Y:CY], y[:, :, CTX_Y:CY],
                                ps[:, s + 1, 0:P].unsqueeze(1).to_broadcast([P, CC, NCTX]), ALU.mult).then_inc(ln_yn, 1)

        head_max(0)
        for n in range(NU + 3):
            if n + 1 in CONV_AT:
                conv(1)
            if n + 1 == CONV_AT[-1] + 1:
                conv(TAPS)
                dve.wait_ge(conv_dve_step, CD * TAPS)
                dve.sem_inc(conv_dve, 1)
            if n + 1 < NU:
                head_max(n + 1)
            c = n + 1 - GATE_AT
            if 0 <= c < CC:
                dve.wait_ge(ln_th, c + 1)
                V.scalar_tensor_tensor(y[:, c, :], ln_tanh[:, c, :], 1.0, y[:, c, :], ALU.add, ALU.mult).then_inc(conv_ok, 1)
            if n < NU:
                fifth(n)
            if n + 1 in BETWEEN:
                between(BETWEEN[n + 1])
            if n % NH == NH - 1 and n < NU:
                row_sums(n // NH)
            if n > NH and n % NH == 2:
                normalise(n // NH - 1)
            if n == 17:
                dve.wait_ge(mod_raw, 4)
                step(V.scalar_tensor_tensor(a2[:], mod[:, 32:40, :], 1.0, both(pcol[:, PG + 2 * KC:PG + 3 * KC]), ALU.add, ALU.mult))
                step(V.tensor_tensor(gcol[:, 1], mod[:, 40:48, :], both(pcol[:, PG + 3 * KC:PG + 4 * KC]), ALU.mult))
                for g in range(2):
                    step(V.tensor_tensor(wra[:, g], wr[:], a2[:, :, g:g + 1].to_broadcast([P, KC, NE]), ALU.mult))
                dve.sem_inc(wra_ok, 1)

        def epilogue(t):
            i = OUT_TILES[t]
            g = 1 if i == LT else 0
            dve.wait_ge(ors_ok, t + 1)
            if t == 0:
                dve.wait_ge(g_ok, 4)
            for half in range(2):
                cs = slice(half * HALF, (half + 1) * HALF)
                step(V.scalar_tensor_tensor(rows[:, t % 2, cs], ps[:, 2 * ((t + 1) % 2) + half, :], rs[:, NT + t:NT + t + 1],
                                            gtile[:, g, cs], ALU.mult, ALU.mult))
                V.tensor_tensor(x[:, i, cs], x[:, i, cs], rows[:, t % 2, cs], ALU.add).then_inc(x1_ok, 1)

        def h2(t):
            h2_copy(t)
            logits(t)
            affinities(t)

        def h2_copy(t):
            i = OUT_TILES[t]
            dve.wait_ge(x2T_mm, 2 * t + 2)
            V.tensor_copy(big[:, 4:8, tok(i)], ps[:, 5, :].rearrange("p (c n) -> p c n", n=P)).then_inc(h2_dve, 1)

        def logits(t):
            g = 1 if OUT_TILES[t] == LT else 0
            dve.wait_ge(rt_mm, t + 1)
            dve.wait_ge(xrs_ok, t + 1)
            if t >= 2:
                dve.wait_ge(rt_ex, t - 1)
            step(V.scalar_tensor_tensor(rlog[:, t % 2, :], ps[:, 6, 0:NE], rs[:, 2 * NT + t:2 * NT + t + 1], rbias[:, g, :],
                                        ALU.mult, ALU.add))
            V.tensor_reduce(rt_max[:, t:t + 1], rlog[:, t % 2, :], AX.X, ALU.max, negate=True).then_inc(rt_mx, 1)

        def affinities(t):
            dve.wait_ge(rt_ex, t + 1)
            step(V.reciprocal(rt_inv[:, t:t + 1], rt_sum[:, t:t + 1]))
            if t >= 2:
                dve.wait_ge(affT_mm, t - 1)
            V.tensor_scalar(aff[:, t % 2, :], rt_exp[:, t % 2, :], rt_inv[:, t:t + 1], None, ALU.mult).then_inc(aff_ok, 1)

        def aff_out(t):
            dve.wait_ge(affT_mm, t + 1)
            V.tensor_copy(affT[:, tok(OUT_TILES[t])], ps[0:NE, 7, 0:P]).then_inc(affT_ok, 1)

        def top(cols_, at, r, rounds):
            w = affT[:, cols_]
            o = slice(at + 8 * r, at + 8 * r + 8)
            step(V.max(topv[:, o], w))
            step(V.max_index(topi[:, o], topv[:, o], w))
            if r < rounds - 1:
                step(V.match_replace(w, topv[:, o], w, -1.0))

        for t in range(NT - 1):
            epilogue(t)
            h2(t)
            if t >= 1:
                aff_out(t - 1)
        aff_out(NT - 2)
        dve.wait_ge(affT_ok, NT - 1)
        for r in range(CL // 8):
            if r == 2:
                epilogue(NT - 1)
            if r == 3:
                h2_copy(NT - 1)
            if r == 5:
                logits(NT - 1)
            if r == 6:
                affinities(NT - 1)
            top(slice(0, NLAT), 0, r, CL // 8)
        aff_out(NT - 1)
        dve.wait_ge(affT_ok, NT)
        for r in range(CP // 8):
            top(slice(NLAT, NTOK), CL, r, CP // 8)
        dve.wait_ge(exp_zero, 1)
        step(V.tensor_copy(topf[:, 0:CL], topi[:, 0:CL]))
        step(V.tensor_scalar(topf[:, CL:CS], topi[:, CL:CS], float(NLAT), None, ALU.add))
        dve.sem_inc(top_ok, 1)
        step(V.tensor_copy(gq[:, :, 0:CS], topv[:].unsqueeze(1).to_broadcast([NE, GS, CS])))
        for r in range(GS):
            n = min(QR, CS - r * QR)
            step(V.tensor_copy(gq[:, r, GS * QR:GS * QR + n], topv[:, r * QR:r * QR + n]))
        dve.sem_inc(top_ok, 1)
        dve.wait_ge(topT_mm, 1)
        step(V.tensor_copy(idxT[:], ps[0:CS, 7, 0:NE]))

        def pick_tokens(e, q):
            V.tensor_copy(idx_of[q][:], idxT[:, bass.ds(e, 1)]).then_inc(picked, 1)

        def pick_gates(e, q):
            V.tensor_copy(gate_of[:, q, :].unsqueeze(2), gate3[:, :, bass.ds(e, 1)]).then_inc(gate_at, 1)

        def columns(q, value):
            dve.wait_ge(xgT_mm, value)
            for j in range(2):
                src = ps[:, 6 + j, 0:4 * CS].rearrange("p (c n) -> p c n", n=CS)
                V.tensor_tensor(xT[q % 2][:, 4 * j:4 * j + 4, 0:CS], src, a2x[:, 4 * j:4 * j + 4, :], ALU.mult).then_inc(mul_ok, 1)
            for j in range(2):
                dve.wait_ge(mul_ok, value * 2 + (j - 1))
                V.tensor_tensor(xT[q % 2][:, 4 * j:4 * j + 4, 0:CS], xT[q % 2][:, 4 * j:4 * j + 4, 0:CS],
                                sh2x[:, 4 * j:4 * j + 4, :], ALU.add).then_inc(xTe_ok, 1)

        pick_tokens(0, 0)
        pick_tokens(1, 1)
        dve.wait_ge(topT_mm, 2)
        step(V.tensor_scalar(gate3[:].rearrange("p r e -> p (r e)"), ps[:, 6, 0:GS * NE], 0.5, None, ALU.mult))
        dve.sem_inc(slots_ok, 1)
        pick_gates(0, 0)
        pick_gates(1, 1)

        dve.wait_ge(rt_mm, NT)
        for dst, src in ((a2x, a2[:]), (sh2x, mod[:, 24:32, :])):
            step(V.tensor_copy(dst[:, :, 0:CL], src[:, :, 0:1].to_broadcast([P, KC, CL])))
            step(V.tensor_copy(dst[:, :, CL:CS], src[:, :, 1:2].to_broadcast([P, KC, CP])))
        dve.sem_inc(ye_dve, GS)
        columns(0, 1)

        def silu(value):
            dve.wait_ge(th_ok, value)
            V.scalar_tensor_tensor(act_g, tanh_g, 1.0, two(0), ALU.add, ALU.mult).then_inc(silu_ok, 1)

        silu(1)

        def group(b, last):
            for q in range(GROUP):
                e = b * GROUP + q
                end = last and q == GROUP - 1
                if not (last and q >= 2):
                    dve.wait_ge(scattered, e * 16 + (SCAT0 - 16))
                    pick_tokens(e + 2, (q + 2) % GROUP)
                    pick_gates(e + 2, (q + 2) % GROUP)
                if not end:
                    columns((q + 1) % GROUP, e + 2)
                dve.wait_ge(units_used, e * UNITS + (RING + 4))
                dve.wait_ge(silu_ok, e + 1)
                dve.wait_ge(gate_at, e + 1)
                for r in range(GS):
                    cs = slice(r * QN, (r + 1) * QN)
                    V.scalar_tensor_tensor(act_g[:, cs], act_g[:, cs], gate_of[:, q, r:r + 1], two(2)[:, cs],
                                           ALU.mult, ALU.mult).then_inc(hid_ok, 1)
                dve.wait_ge(hidT_mm, e + 1)
                hp = ps[:, 7, 0:2 * P].rearrange("p (b n) -> p b n", n=P)
                V.tensor_copy(hid[:, 4:6, :], hp[:, :, 0:CSP]).then_inc(hidc_dve, 1)
                V.tensor_copy(hid[:, 6:8, 2 * QR:CSP], hp[:, :, CSP:P]).then_inc(hidc_dve, 1)
                if not end:
                    silu(e + 2)
                dve.wait_ge(units_used, e * UNITS + (RING + (6 if end else 8)))
                dve.wait_ge(scattered, e * 16 + (SCAT0 - 16))
                for r in range(GS):
                    n = min(QR, CS - r * QR)
                    V.tensor_copy(ys[r * QR:r * QR + n, q % 2, GS * QN:D],
                                  two(4)[GS * QR:GS * QR + n, r * QN:(r + 1) * QN]).then_inc(ye_dve, 1)

        with dve.Fori(0, NE // GROUP - 1) as b:
            group(b, False)
        group(NE // GROUP - 1, True)

        def final(i):
            n = 3 * NT + i
            dve.wait_ge(frs_ok, i + 1)
            if i in POOL_FIN:
                dve.wait_ge(pool_mul, POOL_FIN.index(i) + 1)
            else:
                dve.wait_ge(fin_mul, i + 1 - sum(p < i for p in POOL_FIN))
            V.scalar_tensor_tensor(fin_g[:, i, :], fin_g[:, i, :], rs[:, n:n + 1], x[:, i, :], ALU.mult, ALU.add).then_inc(fin_ok, 1)

        for i in range(NT):
            if i not in POOL_FIN:
                dve.wait_ge(fin_in[i], 16)
                V.tensor_tensor(fin_g[:, i, :], fin[:, i, :], gtile[:, 1 if i == LT else 0, :], ALU.mult).then_inc(fin_mul, 1)
            if i >= 1:
                final(i - 1)
        final(NT - 1)

    block.__exit__(None, None, None)


_INS = ['x_prompt', 'x_sample', 'c', 'c_ctx', 'cache_k', 'cache_v', 'w_mod', 'b_mod', 'g_pre_mix', 'g_post_mix',
        'g_pre_ffn', 'g_post_ffn', 'w_in', 'q_norm', 'k_norm', 'conv_w', 'conv_b', 'conv_ln_g', 'conv_ln_b',
        'w_out', 'w_router', 'w_gate', 'w_up', 'w_down']
_OUTS = [(1, NCTX, D), (1, NLAT, D), (1, 1, NCTX, NKV, HD), (1, 1, NCTX, NKV, HD)]


def _constants():
    grid, half = 64, HD // 4
    freqs = (np.float32(10000.0) ** (-np.arange(half, dtype=np.float32) / np.float32(half))).astype(np.float32)
    pos = np.arange(NLAT)
    cos, sin = np.ones((NTOK, HD), np.float32), np.zeros((NTOK, HD), np.float32)
    for axis, p in enumerate((pos // grid, pos % grid)):
        ang = p.astype(np.float32)[:, None] * freqs[None, :]
        at = axis * 2 * half
        cos[:NLAT, at:at + half] = cos[:NLAT, at + half:at + 2 * half] = np.cos(ang)
        sin[:NLAT, at:at + half] = -np.sin(ang)
        sin[:NLAT, at + half:at + 2 * half] = np.sin(ang)
    sel = np.zeros((P, 2), np.float32)
    pick2 = np.zeros((2, 2, P), np.float32)
    for g in range(2):
        sel[g::32, g] = 1.0
        pick2[g, g] = 1.0
    return {"ident": np.eye(P, dtype=np.float32), "cos": cos, "sin": sin, "sel": sel, "pick2": pick2}


def kernel(**inputs):
    import concourse.bacc as bacc
    from concourse.bass_utils import run_bass_kernel_spmd

    nc = bacc.Bacc("TRN2", target_bir_lowering=False, num_devices=1)
    arrays, aps = {}, {}
    for name, value in [(n, np.ascontiguousarray(inputs[n])) for n in _INS] + list(_constants().items()):
        arrays[f"in_{name}"] = value
        aps[name] = nc.dram_tensor(f"in_{name}", value.shape, mybir.dt.from_np(value.dtype), kind="ExternalInput").ap()
    outs = [nc.dram_tensor(f"out_{i}", shape, mybir.dt.float32, kind="ExternalOutput").ap() for i, shape in enumerate(_OUTS)]
    build(nc, aps, outs)
    r = run_bass_kernel_spmd(nc, [arrays], core_ids=[0])
    return tuple(r.results[0][f"out_{i}"] for i in range(len(_OUTS)))
```
